# Optimizing a Trainium2 kernel written in Bass

```python
import functools
import jax, jax.numpy as jnp
from jax import lax
import numpy as np

D_MODEL = 2048
BATCH = 1
SEQ = 128
DEPTH = 1
DEC_BATCH = 1
DEC_SEQ = 256
PAST_LEN = 128

GRID_W = 64
HEAD_DIM = 64
MIX_W = D_MODEL
A_W = 3 * MIX_W // 8
B_W = MIX_W // 4
C_W = MIX_W - A_W - B_W
HA = A_W // HEAD_DIM
HC = C_W // HEAD_DIM
WIN_R = 8
WIN_C = 16
QBLK_C = WIN_C
KBLK_C = 2 * WIN_C
CONV_K = 31
W_RANK = 64
A_RANK = 64
G_RANK = 128
D_FF = 11 * D_MODEL // 4
N_MOD = 6
Q_BLOCK = 128
SPLIT_SIZES = (A_W, A_W, A_W, B_W, B_W, C_W, C_W, C_W, W_RANK, W_RANK, A_RANK, A_RANK, G_RANK)
IN_COLS = 3 * A_W + 2 * B_W + 3 * C_W + 2 * W_RANK + 2 * A_RANK + G_RANK
ATTN_SCALE = HEAD_DIM ** -0.5
DECAY_SCALE = 0.606531
RMS_EPS = 1e-6
LN_EPS = 1e-5
GN_EPS = 64e-5
L2_EPS = 1e-12
MASK_VALUE = -1e30

kernel_name = 'hybrid_diffusion_natten_conformer_rwkv7_step'

def rmsnorm(x, g):
    x32 = x.astype(jnp.float32)
    y = x32 * lax.rsqrt(jnp.mean(x32 * x32, axis=-1, keepdims=True) + RMS_EPS)
    return (y * g.astype(jnp.float32)).astype(x.dtype)

def ada_modulation(cvec, w_mod, b_mod):
    m = jax.nn.silu(cvec) @ w_mod + b_mod
    return jnp.split(m[:, None, :], N_MOD, axis=-1)

def split_columns(proj):
    cuts, acc = [], 0
    for s in SPLIT_SIZES[:-1]:
        acc += s
        cuts.append(acc)
    return jnp.split(proj, cuts, axis=-1)

def depthwise_conv(x, w, b):
    k = w.shape[0]
    y = lax.conv_general_dilated(x, w[:, None, :].astype(x.dtype), window_strides=(1,),
                                 padding=[((k - 1) // 2, k // 2)],
                                 dimension_numbers=('NWC', 'WIO', 'NWC'),
                                 feature_group_count=x.shape[-1])
    return y + b.astype(x.dtype)

def context_attention(q, k, v):
    bsz, s_len, n_h, d_h = q.shape
    nb = s_len // Q_BLOCK
    qb = jnp.moveaxis(q.reshape(bsz, nb, Q_BLOCK, n_h, d_h), 1, 0)

    def block(qi):
        s = jnp.einsum('bqhd,bkhd->bhqk', qi, k).astype(jnp.float32) * ATTN_SCALE
        p = jax.nn.softmax(s, axis=-1).astype(v.dtype)
        return jnp.einsum('bhqk,bkhd->bqhd', p, v)

    out = lax.map(block, qb)
    return jnp.moveaxis(out, 0, 1).reshape(bsz, s_len, n_h * d_h)

def neighbourhood_attention(q, k, v, ctx_k, ctx_v, rpb):
    bsz, t_len, n_h, d_h = q.shape
    rows = t_len // GRID_W
    kr = min(WIN_R, rows)
    n_cb = GRID_W // QBLK_C
    qg = q.reshape(bsz, rows, GRID_W, n_h, d_h)
    kg = k.reshape(bsz, rows, GRID_W, n_h, d_h)
    vg = v.reshape(bsz, rows, GRID_W, n_h, d_h)
    qcol = np.arange(GRID_W).reshape(n_cb, QBLK_C)
    key_start = np.clip(np.arange(n_cb) * QBLK_C - WIN_C // 2, 0, GRID_W - KBLK_C)
    col_idx = key_start[:, None] + np.arange(KBLK_C)[None, :]
    win_start = np.clip(qcol - WIN_C // 2, 0, GRID_W - WIN_C)
    kcol = col_idx[:, None, :]
    col_valid = (kcol >= win_start[:, :, None]) & (kcol < win_start[:, :, None] + WIN_C)
    col_bias_idx = np.clip(kcol - qcol[:, :, None] + WIN_C - 1, 0, 2 * WIN_C - 2)
    rpb32 = rpb.astype(jnp.float32)

    def row_block(i):
        rs = jnp.clip(i - kr // 2, 0, rows - kr)
        k_blk = lax.dynamic_slice_in_dim(kg, rs, kr, axis=1)[:, :, col_idx]
        v_blk = lax.dynamic_slice_in_dim(vg, rs, kr, axis=1)[:, :, col_idx]
        q_row = lax.dynamic_index_in_dim(qg, i, axis=1, keepdims=False).reshape(bsz, n_cb, QBLK_C, n_h, d_h)
        row_bias_idx = rs + jnp.arange(kr) - i + WIN_R - 1
        bias = rpb32[:, row_bias_idx][:, :, col_bias_idx].transpose(0, 2, 3, 1, 4)
        s_loc = jnp.einsum('bnqhd,brnkhd->bhnqrk', q_row, k_blk).astype(jnp.float32) * ATTN_SCALE + bias[None]
        s_loc = jnp.where(col_valid[:, :, None, :], s_loc, MASK_VALUE)
        s_loc = s_loc.reshape(bsz, n_h, n_cb, QBLK_C, kr * KBLK_C)
        s_ctx = jnp.einsum('bnqhd,bphd->bhnqp', q_row, ctx_k).astype(jnp.float32) * ATTN_SCALE
        p = jax.nn.softmax(jnp.concatenate([s_loc, s_ctx], axis=-1), axis=-1).astype(v.dtype)
        p_loc = p[..., :kr * KBLK_C].reshape(bsz, n_h, n_cb, QBLK_C, kr, KBLK_C)
        p_ctx = p[..., kr * KBLK_C:]
        o = (jnp.einsum('bhnqrk,brnkhd->bnqhd', p_loc, v_blk)
             + jnp.einsum('bhnqp,bphd->bnqhd', p_ctx, ctx_v.astype(v.dtype)))
        return o.reshape(bsz, GRID_W, n_h, d_h)

    out = lax.map(row_block, jnp.arange(rows))
    return jnp.moveaxis(out, 0, 1).reshape(bsz, t_len, n_h * d_h)

def conv_module(glu_a, glu_b, conv_w, conv_b, ln_g, ln_b):
    u = glu_a * jax.nn.sigmoid(glu_b)
    u = depthwise_conv(u, conv_w, conv_b).astype(jnp.float32)
    mu = jnp.mean(u, axis=-1, keepdims=True)
    var = jnp.mean(jnp.square(u - mu), axis=-1, keepdims=True)
    u = (u - mu) * lax.rsqrt(var + LN_EPS) * ln_g.astype(jnp.float32) + ln_b.astype(jnp.float32)
    return jax.nn.silu(u).astype(glu_a.dtype)

def wkv_scan(r, w, k, v, z, b, s0, reverse):
    xs = tuple(jnp.moveaxis(t, 1, 0) for t in (r, w, k, v, z, b))

    def step(s, inp):
        r_t, w_t, k_t, v_t, z_t, b_t = inp
        sz = jnp.einsum('bhvk,bhk->bhv', s, z_t)
        s = s * w_t[:, :, None, :] + sz[..., None] * b_t[:, :, None, :] + v_t[..., None] * k_t[:, :, None, :]
        return s, jnp.einsum('bhvk,bhk->bhv', s, r_t)

    s_final, o = lax.scan(step, s0, xs, reverse=reverse)
    return jnp.moveaxis(o, 0, 1), s_final

def rwkv7_bidirectional(r, k, v, xw_f, xw_b, xa_f, xa_b, xg, lp, s0_f, s0_b):
    f32 = jnp.float32
    bsz, t_len, _ = r.shape
    hd = lambda t: t.astype(f32).reshape(bsz, t_len, HC, HEAD_DIM)
    r_h, k_h, v_h = hd(r), hd(k), hd(v)
    kk = k_h * lp['k_k'].astype(f32).reshape(HC, HEAD_DIM)
    kk = kk * lax.rsqrt(jnp.sum(kk * kk, axis=-1, keepdims=True) + L2_EPS)
    k_a = lp['k_a'].astype(f32).reshape(HC, HEAD_DIM)
    r_k = lp['r_k'].astype(f32)

    def one_direction(xw, xa, d, s0, reverse):
        w = jnp.exp(-DECAY_SCALE * jax.nn.sigmoid(
            lp['w0'][d].astype(f32) + jnp.tanh(xw.astype(f32)) @ lp['w_lora'][d].astype(f32)))
        a = jax.nn.sigmoid(lp['a0'][d].astype(f32) + xa.astype(f32) @ lp['a_lora'][d].astype(f32))
        w, a = hd(w), hd(a)
        k_d = k_h * (1.0 + (a - 1.0) * k_a)
        o, s_fin = wkv_scan(r_h, w, k_d, v_h, -kk, kk * a, s0.astype(f32), reverse)
        bonus = jnp.sum(r_h * k_d * r_k, axis=-1, keepdims=True) * v_h
        return o, bonus, s_fin

    o_f, bonus_f, s_f = one_direction(xw_f, xa_f, 0, s0_f, False)
    o_b, bonus_b, s_b = one_direction(xw_b, xa_b, 1, s0_b, True)
    o = o_f + o_b
    mu = jnp.mean(o, axis=-1, keepdims=True)
    var = jnp.mean(jnp.square(o - mu), axis=-1, keepdims=True)
    o = ((o - mu) * lax.rsqrt(var + GN_EPS)).reshape(bsz, t_len, C_W)
    o = o * lp['ln_g'].astype(f32) + lp['ln_b'].astype(f32) + (bonus_f + bonus_b).reshape(bsz, t_len, C_W)
    g = jax.nn.sigmoid(xg.astype(f32)) @ lp['g_lora'].astype(f32)
    return o * g, s_f, s_b

def conv_ffn(h, w_up, dw_w, dw_b, w_down):
    u, gv = jnp.split(h @ w_up, 2, axis=-1)
    u = depthwise_conv(u, dw_w, dw_b)
    return (jax.nn.silu(u) * gv) @ w_down

def trunk_layer(x, cvec, attend, s0_f, s0_b, lp):
    bsz, t_len, _ = x.shape
    sh1, sc1, g1, sh2, sc2, g2 = ada_modulation(cvec, lp['w_mod'], lp['b_mod'])
    h = rmsnorm(x, lp['n1']) * (1.0 + sc1) + sh1
    (q, k, v, glu_a, glu_b, r, kc, vc, xw_f, xw_b, xa_f, xa_b, xg) = split_columns(h @ lp['w_in'])
    to_heads = lambda t: t.reshape(bsz, t_len, HA, HEAD_DIM)
    k_h, v_h = to_heads(k), to_heads(v)
    y_a = attend(to_heads(q), k_h, v_h)
    y_b = conv_module(glu_a, glu_b, lp['conv_w'], lp['conv_b'], lp['conv_ln_g'], lp['conv_ln_b'])
    y_c, s_f, s_b = rwkv7_bidirectional(r, kc, vc, xw_f, xw_b, xa_f, xa_b, xg, lp, s0_f, s0_b)
    y = jnp.concatenate([y_a.astype(x.dtype), y_b, y_c.astype(x.dtype)], axis=-1) @ lp['w_out']
    x = x + g1 * y
    h2 = rmsnorm(x, lp['n2']) * (1.0 + sc2) + sh2
    x = x + g2 * conv_ffn(h2, lp['w_up'], lp['ffn_conv_w'], lp['ffn_conv_b'], lp['w_down'])
    return x, k_h, v_h, s_f.astype(x.dtype), s_b.astype(x.dtype)

def setup_inputs(seed: int = 0) -> dict:
    key = jax.random.key(seed)
    keys = jax.random.split(key, 40)

    def nrm(i, shape, scale):
        return jax.random.normal(keys[i], shape, jnp.float32) * scale

    L = DEPTH
    return {
        'x_prompt': nrm(0, (BATCH, SEQ, D_MODEL), 1.0),
        'x_sample': nrm(1, (DEC_BATCH, DEC_SEQ, D_MODEL), 1.0),
        'cache_k': nrm(2, (DEC_BATCH, L, PAST_LEN, HA, HEAD_DIM), 1.0),
        'cache_v': nrm(3, (DEC_BATCH, L, PAST_LEN, HA, HEAD_DIM), 1.0),
        'state_fwd': nrm(4, (DEC_BATCH, L, HC, HEAD_DIM, HEAD_DIM), 0.3),
        'state_bwd': nrm(5, (DEC_BATCH, L, HC, HEAD_DIM, HEAD_DIM), 0.3),
        'c': nrm(6, (DEC_BATCH, D_MODEL), 1.0),
        'c_ctx': nrm(7, (D_MODEL,), 1.0),
        'norm1_g': 1.0 + nrm(8, (L, D_MODEL), 0.1),
        'norm2_g': 1.0 + nrm(9, (L, D_MODEL), 0.1),
        'w_mod': nrm(10, (L, D_MODEL, N_MOD * D_MODEL), 0.5 * D_MODEL ** -0.5),
        'b_mod': nrm(11, (L, N_MOD * D_MODEL), 0.01),
        'w_in': nrm(12, (L, D_MODEL, IN_COLS), D_MODEL ** -0.5),
        'w_out': nrm(13, (L, MIX_W, D_MODEL), MIX_W ** -0.5),
        'rpb': nrm(14, (L, HA, 2 * WIN_R - 1, 2 * WIN_C - 1), 0.2),
        'conv_w': nrm(15, (L, CONV_K, B_W), CONV_K ** -0.5),
        'conv_b': nrm(16, (L, B_W), 0.01),
        'conv_ln_g': 1.0 + nrm(17, (L, B_W), 0.1),
        'conv_ln_b': nrm(18, (L, B_W), 0.01),
        'rwkv_w0': nrm(19, (L, 2, C_W), 1.0),
        'rwkv_w_lora': nrm(20, (L, 2, W_RANK, C_W), W_RANK ** -0.5),
        'rwkv_a0': nrm(21, (L, 2, C_W), 0.5),
        'rwkv_a_lora': nrm(22, (L, 2, A_RANK, C_W), A_RANK ** -0.5),
        'rwkv_g_lora': nrm(23, (L, G_RANK, C_W), G_RANK ** -0.5),
        'rwkv_k_k': 1.0 + nrm(24, (L, C_W), 0.1),
        'rwkv_k_a': 1.0 + nrm(25, (L, C_W), 0.1),
        'rwkv_r_k': nrm(26, (L, HC, HEAD_DIM), 0.1),
        'rwkv_ln_g': 1.0 + nrm(27, (L, C_W), 0.1),
        'rwkv_ln_b': nrm(28, (L, C_W), 0.01),
        'w_up': nrm(29, (L, D_MODEL, 2 * D_FF), D_MODEL ** -0.5),
        'ffn_conv_w': nrm(30, (L, 3, D_FF), 3 ** -0.5),
        'ffn_conv_b': nrm(31, (L, D_FF), 0.01),
        'w_down': nrm(32, (L, D_FF, D_MODEL), D_FF ** -0.5),
        'final_g': 1.0 + nrm(33, (D_MODEL,), 0.1),
    }

def reference(x_prompt, x_sample, cache_k, cache_v, state_fwd, state_bwd, c, c_ctx,
              norm1_g, norm2_g, w_mod, b_mod, w_in, w_out, rpb, conv_w, conv_b, conv_ln_g, conv_ln_b,
              rwkv_w0, rwkv_w_lora, rwkv_a0, rwkv_a_lora, rwkv_g_lora, rwkv_k_k, rwkv_k_a, rwkv_r_k,
              rwkv_ln_g, rwkv_ln_b, w_up, ffn_conv_w, ffn_conv_b, w_down, final_g):
    xp, xs = x_prompt, x_sample
    c_prompt = c_ctx[None, :]
    zero_state = jnp.zeros((xp.shape[0], HC, HEAD_DIM, HEAD_DIM), xp.dtype)
    ks, vs, sfs, sbs = [], [], [], []
    for l in range(DEPTH):
        lp = {
            'n1': norm1_g[l], 'n2': norm2_g[l], 'w_mod': w_mod[l], 'b_mod': b_mod[l],
            'w_in': w_in[l], 'w_out': w_out[l],
            'conv_w': conv_w[l], 'conv_b': conv_b[l], 'conv_ln_g': conv_ln_g[l], 'conv_ln_b': conv_ln_b[l],
            'w0': rwkv_w0[l], 'w_lora': rwkv_w_lora[l], 'a0': rwkv_a0[l], 'a_lora': rwkv_a_lora[l],
            'g_lora': rwkv_g_lora[l], 'k_k': rwkv_k_k[l], 'k_a': rwkv_k_a[l], 'r_k': rwkv_r_k[l],
            'ln_g': rwkv_ln_g[l], 'ln_b': rwkv_ln_b[l],
            'w_up': w_up[l], 'ffn_conv_w': ffn_conv_w[l], 'ffn_conv_b': ffn_conv_b[l], 'w_down': w_down[l],
        }
        xp, k_ctx, v_ctx, s_f, s_b = trunk_layer(xp, c_prompt, context_attention, zero_state, zero_state, lp)
        ks.append(k_ctx)
        vs.append(v_ctx)
        sfs.append(s_f)
        sbs.append(s_b)
        attend = functools.partial(neighbourhood_attention, ctx_k=cache_k[:, l], ctx_v=cache_v[:, l], rpb=rpb[l])
        xs, _, _, _, _ = trunk_layer(xs, c, attend, state_fwd[:, l], state_bwd[:, l], lp)
    y_prompt = rmsnorm(xp, final_g)
    y_sample = rmsnorm(xs, final_g)
    new_cache_k = jnp.stack(ks, axis=1)
    new_cache_v = jnp.stack(vs, axis=1)
    new_state_fwd = jnp.stack(sfs, axis=1)
    new_state_bwd = jnp.stack(sbs, axis=1)
    return (y_prompt, y_sample, new_cache_k, new_cache_v, new_state_fwd, new_state_bwd)


_drawn_inputs = setup_inputs


def setup_inputs(seed=0):
    import zlib

    import numpy as np

    out = dict(_drawn_inputs(seed))
    spreads = {}
    factors = {'cache_k': 3.666,
     'cache_v': 3.022,
     'state_fwd': 8.0,
     'state_bwd': 8.0,
     'b_mod': 2.76,
     'rpb': 64.0,
     'conv_b': 8.0,
     'conv_ln_g': 5.575,
     'conv_ln_b': 64.0,
     'rwkv_k_k': 8.05,
     'rwkv_ln_g': 6.253,
     'rwkv_ln_b': 64.0,
     'ffn_conv_b': 37.925}
    for name, (base, spread) in spreads.items():
        noise = np.random.default_rng([zlib.crc32(name.encode()), seed]).standard_normal(out[name].shape)
        drawn = base * np.exp(spread * noise) if base else spread * noise
        out[name] = __import__('jax').numpy.asarray(drawn.astype(out[name].dtype))
    for name, factor in factors.items():
        out[name] = (out[name] * factor).astype(out[name].dtype)
    return out
```

```python
from contextlib import ExitStack

import concourse.bass as bass
from concourse import mybir

ALU = mybir.AluOpType
ACT = mybir.ActivationFunctionType
F32 = mybir.dt.float32
AX = mybir.AxisListType

P = 128
D = 2048
KT = D // P
TOK = 3 * P
HD = 64
HA = 12
HC = 12
CHUNK = 64
DFF = 11 * D // 4
FT = DFF // P
CONV_K = 31
PADC = CONV_K // 2
BT = 4
GRID = 64
BLK = 256
RING = 3
SLOT = KT * BLK
DECAY = 0.606531
SCALE = HD ** -0.5
LEVELS = 5

C_ID = 0
C_M4 = C_ID + P
C_BONES = C_M4 + 2 * 4 * P
C_XM = C_BONES + P
C_SAME2 = C_XM + 2 * LEVELS * P
C_COL = C_SAME2 + P
C_ZERO = C_COL + GRID
C_MEAN = C_ZERO + P
C_END = C_MEAN + P

N_MOD = 6 * D // BLK
IN_BLOCKS = ([("chan", "q", 256 * j, 256, 2 * j) for j in range(3)]
             + [("chan", "k", 768 + 256 * j, 256, 2 * j) for j in range(3)]
             + [("tok", "v", 1536 + 256 * j, 256, j) for j in range(3)]
             + [b for j in range(2) for b in (("chan", "glu_b", 2816 + 256 * j, 256, 2 * j),
                                              ("chan", "glu_a", 2304 + 256 * j, 256, 2 * j))]
             + [("chan", "lora", 5632, 256, 0), ("chan", "lora", 5888, 128, 2)]
             + [("tok", "rkv", 3328 + 256 * j, 256, j) for j in range(9)])
B_IN = N_MOD
B_OUT = B_IN + len(IN_BLOCKS)
B_UP = B_OUT + D // BLK
B_DOWN = B_UP + 2 * DFF // BLK
DOWN_KT = 4
DOWN_W = SLOT // DOWN_KT
B_END = B_DOWN + 2 * (FT // DOWN_KT)

ITEMS = []
for _n, (_kind, _what, _c, _w, _j) in enumerate(IN_BLOCKS):
    for _s in range(3 if _kind == "tok" else _w // P):
        _eng = "act" if _what in ("q", "v", "rkv", "glu_b", "lora") else "dve"
        ITEMS.append((_n, _kind, _what, _j, _s, _eng))
ATT = [(t, h) for t in range(3) for h in range(HA)]
UNITS = [(0, 0, 0), (0, 1, 0), (1, 0, 0), (2, 1, 0), (2, 0, 2), (1, 1, 2)]
FINAL = {1: (0, 0), 4: (1, 2), 5: (2, 1)}
HH = HC // 2
HW = HH * HD


def evacs(eng, m):
    return sum(1 for it in ITEMS[:m] if it[5] == eng)


def build(nc, a, out):
    ctx = ExitStack()
    with ctx:
        def sb(name, cols):
            return ctx.enter_context(nc.sbuf_tensor(name, [P, cols], F32))

        def sem(name):
            return ctx.enter_context(nc.semaphore(name))

        def carve(t, at, *dims):
            n = 1
            for d in dims:
                n *= d
            v = t[:, at:at + n]
            if len(dims) == 2:
                v = v.rearrange("p (a b) -> p a b", a=dims[0])
            if len(dims) == 3:
                v = v.rearrange("p (a b c) -> p a b c", a=dims[0], b=dims[1])
            if len(dims) == 4:
                v = v.rearrange("p (a b c d) -> p a b c d", a=dims[0], b=dims[1], c=dims[2])
            return v, at + n

        consts = sb("consts", C_END)
        vcol_t = sb("vcol", 4 * P)
        vcol = vcol_t[:, :].rearrange("p (g c) -> p g c", g=4)
        cT = sb("cT", 2 * KT)
        modcol_t = sb("modcol", 2 * 96)
        modcol = modcol_t[:, :].rearrange("p (t g) -> p t g", g=2)
        scol_t = sb("scol", 2 * KT)
        scol = scol_t[:, :].rearrange("p (t g) -> p t g", g=2)
        stat = sb("stat", 64)
        xbuf = sb("xbuf", 3 * D)
        x = xbuf[:, :].rearrange("p (t c) -> p t c", t=3)
        hT_t = sb("hT", KT * TOK)
        hT = hT_t[:, :].rearrange("p (k n) -> p k n", k=KT)
        yT = hT
        ring = sb("ring", RING * SLOT)
        arena = sb("arena", 24300)
        ps_t = ctx.enter_context(nc.psum_tensor("ps", [P, 8 * 512], F32))
        ps = ps_t[:, :].rearrange("p (b n) -> p b n", b=8)

        ident = consts[:, C_ID:C_ID + P]

        vrow, o = carve(arena, 0, 5, P)
        xn, o = carve(arena, o, 3, D)
        csig, o = carve(arena, o, 2 * KT)
        modrow, o = carve(arena, o, 2, BLK)
        junk, o = carve(arena, o, D)
        qkT, o = carve(arena, 0, 12, TOK)
        v_tok, o = carve(arena, o, 3, 768)
        upad, o_mix = carve(arena, o, BT, PADC * 3 + TOK)
        Bm, o = carve(arena, o_mix, HA, 6, GRID)
        ckT, o = carve(arena, o, 6, P)
        cv, o = carve(arena, o, 768)
        O_RKV = 24300 - 3 * 2304 - 3 * TOK
        assert o <= O_RKV, (o, O_RKV)
        rkv, o = carve(arena, O_RKV, 3, 2304)
        lora, o = carve(arena, o, 3, TOK)
        assert o == 24300
        CW = 2 * PADC + TOK + PADC - 2 * PADC
        cbuf, o = carve(xbuf, 0, BT, CW)
        csq, o = carve(xbuf, o, BT, CW)
        crstd, o = carve(xbuf, o, CW)
        sgt, o = carve(xbuf, o, 2, TOK)
        knew, o = carve(xbuf, o, 768)
        assert o <= 3 * D
        ss, o = carve(ring, 0, 3, TOK)
        PT, o = carve(ring, o, 2, TOK)
        ck, o = carve(ring, o, 768)
        Am, o = carve(ring, 0, HH, 4, P)
        Nm, o = carve(ring, o, HH, P)
        Tm, o = carve(ring, o, HH, P)
        TTm, o = carve(ring, o, HH, P)
        Xm, o = carve(ring, o, HH, P)
        ZA, o = carve(ring, o, HH, 2, HD)
        ZU, o = carve(ring, o, HH, 2, HD)
        QT, o = carve(ring, o, 3, P)
        zrT, o = carve(ring, o, 3, 2, P)
        bT, o = carve(ring, o, 3, P)
        kT, o = carve(ring, o, 3, P)
        MT, o = carve(ring, o, 2, 3, HD)
        Sh, o = carve(ring, o, 2, 3, HD)
        dP, o = carve(ring, o, 2, 3, HD)
        assert o <= RING * SLOT
        S, o = carve(arena, 0, 2 * 5, 3, HD)
        par, o = carve(arena, o, 12, HW)
        names = []
        for _ in range(17):
            t_, o = carve(arena, o, HW)
            names.append(t_)
        tW, tA, eE, eP, eN, eR, eT, kkn, b1, kd, btil, Bbar, ktil, Kbar, rtil, sq, tmp = names
        Oacc, o = carve(arena, o, 2, HW)
        bsum, o = carve(arena, o, 2, HH)
        st6, o = carve(arena, o, 4, HH)
        assert o <= O_RKV, (o, O_RKV)
        sraw = eE
        sraw2 = eP
        sout = eN
        act, o = carve(arena, 0, FT, TOK)
        xn2, _ = carve(arena, 0, 3, D)
        gb, o = carve(arena, o, 2, D)
        UPW = TOK + 3
        up2, o = carve(arena, o, 2, UPW)
        cv2, o = carve(arena, o, 2, TOK + 1)
        sg2, o = carve(arena, o, 2, TOK + 1)
        ytmp, o = carve(arena, o, BLK)
        assert o <= 24300, o
        ytmp2, _ = carve(hT_t, 0, 512)
        fg, _ = carve(hT_t, 512, D)
        junk2, _ = carve(hT_t, 512 + D, D)

        E_dram = nc.dram_tensor("rpb_padded", [HA, 7, P], F32, kind="Internal").ap()
        EL = HA * 7 * P
        R_dram = nc.dram_tensor("rpb_rows", [GRID, EL], F32, kind="Internal").ap()

        s_const, s_x, s_vrow, s_lnrow = sem("s_const"), sem("s_x"), sem("s_vrow"), sem("s_lnrow")
        s_w = [sem(f"s_w{i}") for i in range(RING)]
        s_blk = sem("s_blk")
        s_vt, s_vc, s_ct = sem("s_vt"), sem("s_vc"), sem("s_ct")
        s_csig = sem("s_csig")
        s_ssq, s_rstd, s_xn, s_xt, s_xc = sem("s_ssq"), sem("s_rstd"), sem("s_xn"), sem("s_xt"), sem("s_xc")
        s_mrow, s_mcT, s_mcol, s_h = sem("s_mrow"), sem("s_mcT"), sem("s_mcol"), sem("s_h")
        s_item, s_eact, s_edve = sem("s_item"), sem("s_eact"), sem("s_edve")
        s_d, s_a = sem("s_d"), sem("s_a")
        s_var, s_root = sem("s_var"), sem("s_root")
        s_pad = sem("s_pad")
        s_cbuf, s_cmean, s_ccen, s_csq, s_cvar, s_cn, s_cy = (sem(n) for n in (
            "s_cbuf", "s_cmean", "s_ccen", "s_csq", "s_cvar", "s_cn", "s_cy"))
        s_E0, s_E1, s_Bm, s_Bmask = sem("s_E0"), sem("s_E1"), sem("s_Bm"), sem("s_Bmask")
        s_cache, s_ckt, s_ckc, s_knt, s_knc, s_out = (sem(n) for n in (
            "s_cache", "s_ckt", "s_ckc", "s_knt", "s_knc", "s_out"))
        s_sc, s_sm, s_ex, s_nr, s_pt, s_ptc, s_pv, s_pvc = (sem(n) for n in (
            "s_sc", "s_sm", "s_ex", "s_nr", "s_pt", "s_ptc", "s_pv", "s_pvc"))
        s_par, s_S0, s_sraw, s_sT = sem("s_par"), sem("s_S0"), sem("s_sraw"), sem("s_sT")
        (s_rlora, s_rpre, s_rsig, s_rcum, s_rexp, s_rtil, s_rbar, s_rtr, s_rtc, s_rA, s_rAm, s_rN, s_rNc, s_rT0,
         s_rAV, s_rAVc, s_rX, s_rXm, s_rTp, s_rTu, s_rZU, s_rZUc, s_rQM, s_rQMc, s_rSp, s_rS, s_rO, s_rdone,
         s_fg, s_fy, s_fT, s_fc, s_stT, s_stc, s_stout) = (sem(n) for n in (
             "s_rlora", "s_rpre", "s_rsig", "s_rcum", "s_rexp", "s_rtil", "s_rbar", "s_rtr", "s_rtc", "s_rA",
             "s_rAm", "s_rN", "s_rNc", "s_rT0", "s_rAV", "s_rAVc", "s_rX", "s_rXm", "s_rTp", "s_rTu", "s_rZU",
             "s_rZUc", "s_rQM", "s_rQMc", "s_rSp", "s_rS", "s_rO", "s_rdone", "s_fg", "s_fy", "s_fT", "s_fc",
             "s_stT", "s_stc", "s_stout"))
        s_x2, s_gbp, s_gbc, s_o, s_oc = sem("s_x2"), sem("s_gbp"), sem("s_gbc"), sem("s_o"), sem("s_oc")
        s_ssq2, s_xn2, s_xt2, s_h2 = sem("s_ssq2"), sem("s_xn2"), sem("s_xt2"), sem("s_h2")
        s_gb2p, s_gb2c = sem("s_gb2p"), sem("s_gb2c")
        s_up, s_uc, s_ucv, s_usg, s_uact = sem("s_up"), sem("s_uc"), sem("s_ucv"), sem("s_usg"), sem("s_uact")
        s_dn, s_dc, s_fgl, s_fss, s_yf = sem("s_dn"), sem("s_dc"), sem("s_fgl"), sem("s_fss"), sem("s_yf")

        def toks(t):
            return slice(P * t, P * t + P)

        def half(p):
            return slice(64 * p, 64 * p + 64)

        def slot_of(n):
            return ring[:, (n % RING) * SLOT:(n % RING + 1) * SLOT]

        block = ctx.enter_context(nc.Block())
        N_ST = 2 * 2 * 1
        LOADS_PER_HALF = 12

        @block.sync
        def _(sp):
            def load(n, src, view):
                if n >= RING:
                    sp.wait_ge(s_blk, n - RING + 1)
                sp.dma_start(view, src).then_inc(s_w[n % RING], 16)

            def kview(n, w):
                return slot_of(n)[:, 0:KT * w].rearrange("p (k c) -> p k c", k=KT)

            def ksrc(w, c0, width):
                return w[:, c0:c0 + width].rearrange("(k p) c -> p k c", p=P)

            sp.dma_start(consts[:, :], a["consts"]).then_inc(s_const, 16)
            for t, src in ((0, a["x_prompt"][0]), (1, a["x_sample"][0, 0:P]), (2, a["x_sample"][0, P:2 * P])):
                sp.dma_start(x[:, t, :], src).then_inc(s_x, 16)
            for i in range(N_MOD):
                load(i, ksrc(a["w_mod"][0], BLK * i, BLK), kview(i, BLK))
            for j, (_, _, c0, w, _) in enumerate(IN_BLOCKS):
                load(B_IN + j, ksrc(a["w_in"][0], c0, w), kview(B_IN + j, w))
            sp.wait_ge(s_h, 1)
            sp.wait_ge(s_eact, evacs("act", len(ITEMS)))
            sp.dma_start(out["new_cache_v"][0, 0].rearrange("t h d -> t (h d)"), v_tok[:, 0, :]).then_inc(s_out, 16)
            sp.wait_ge(s_knc, 2)
            sp.dma_start(out["new_cache_k"][0, 0].rearrange("t h d -> t (h d)"), knew).then_inc(s_out, 16)
            for hf in range(2):
                cs = slice(HW * hf, HW * hf + HW)
                if hf == 0:
                    sp.wait_ge(s_pvc, len(ATT) // 2)
                    sp.wait_ge(s_out, 32)
                else:
                    sp.wait_ge(s_fy, 3)
                    sp.wait_ge(s_fg, 3)
                for i, src in enumerate((a["rwkv_w0"][0, 0:1, cs], a["rwkv_w0"][0, 1:2, cs],
                                         a["rwkv_a0"][0, 0:1, cs], a["rwkv_a0"][0, 1:2, cs],
                                         a["rwkv_k_k"][0:1, cs], a["rwkv_k_a"][0:1, cs],
                                         a["rwkv_r_k"].rearrange("l h d -> l (h d)")[0:1, cs],
                                         a["rwkv_ln_g"][0:1, cs], a["rwkv_ln_b"][0:1, cs])):
                    sp.dma_start(par[:, i, :], src.broadcast_to([P, HW])).then_inc(s_par, 16)
                sp.dma_start(par[:, 9, :], a["rwkv_w_lora"][0][:, :, cs].rearrange("d r c -> (d r) c")).then_inc(s_par, 16)
                sp.dma_start(par[:, 10, :], a["rwkv_a_lora"][0][:, :, cs].rearrange("d r c -> (d r) c")).then_inc(s_par, 16)
                sp.dma_start(par[:, 11, :], a["rwkv_g_lora"][0][:, cs]).then_inc(s_par, 16)
                for d in range(2):
                    sp.wait_ge(s_stc, 2 * hf + d + 1)
                    dst = out["new_state_fwd" if d == 0 else "new_state_bwd"][0, 0, HH * hf:HH * hf + HH]
                    sp.dma_start(dst.rearrange("h v k -> v h k"),
                                 sout[0:HD, :].rearrange("p (h k) -> p h k", h=HH)).then_inc(s_stout, 16)
                sp.wait_ge(s_stout, 32 * hf + 32)
                for d, dst in enumerate((sraw, sraw2)):
                    src = a["state_fwd" if d == 0 else "state_bwd"][0, 0, HH * hf:HH * hf + HH]
                    sp.dma_start(dst[0:HD, :].rearrange("p (h k) -> p h k", h=HH),
                                 src.rearrange("h v k -> v h k")).then_inc(s_sraw, 16)
            sp.wait_ge(s_fc, 6)
            for t, src in ((0, a["x_prompt"][0]), (1, a["x_sample"][0, 0:P]), (2, a["x_sample"][0, P:2 * P])):
                sp.dma_start(x[:, t, :], src).then_inc(s_x2, 16)
            for j in range(D // BLK):
                load(B_OUT + j, ksrc(a["w_out"][0], BLK * j, BLK), kview(B_OUT + j, BLK))
            for i in range(DFF // BLK):
                load(B_UP + 2 * i, ksrc(a["w_up"][0], BLK * i, BLK), kview(B_UP + 2 * i, BLK))
                load(B_UP + 2 * i + 1, ksrc(a["w_up"][0], DFF + BLK * i, BLK), kview(B_UP + 2 * i + 1, BLK))
            for q in range(2):
                for g in range(FT // DOWN_KT):
                    n = B_DOWN + q * (FT // DOWN_KT) + g
                    src = a["w_down"][0][DOWN_KT * P * g:DOWN_KT * P * (g + 1), DOWN_W * q:DOWN_W * (q + 1)]
                    load(n, src.rearrange("(k p) c -> p k c", p=P),
                         slot_of(n).rearrange("p (k c) -> p k c", k=DOWN_KT))
                    if q == 0 and g == 3:
                        sp.dma_start(fg, a["final_g"].rearrange("(o c) -> o c", o=1).broadcast_to([P, D])).then_inc(s_fgl, 16)
            for t in range(3):
                sp.wait_ge(s_yf, t + 1)
                dst = out["y_prompt"][0] if t == 0 else out["y_sample"][0, P * (t - 1):P * t]
                sp.dma_start(dst, x[:, t, :]).then_inc(s_out, 16)
            sp.wait_ge(s_out, 16 * 5)
            sp.wait_ge(s_stout, 16 * 4)

        @block.gpsimd
        def _(pool):
            pool.dma_start(vrow[0:KT, 0, :], a["c_ctx"].rearrange("(k p) -> k p", p=P)).then_inc(s_vrow, 16)
            pool.dma_start(vrow[KT:2 * KT, 0, :], a["c"][0].rearrange("(k p) -> k p", p=P)).then_inc(s_vrow, 16)
            pool.dma_start(vrow[0:16, 1, :], a["norm1_g"][0].rearrange("(k p) -> k p", p=P)).then_inc(s_vrow, 16)
            pool.dma_start(vrow[16:32, 1, :], a["norm2_g"][0].rearrange("(k p) -> k p", p=P)).then_inc(s_vrow, 16)
            pool.dma_start(vrow[32:128, 1, :], a["b_mod"][0].rearrange("(k p) -> k p", p=P)).then_inc(s_vrow, 16)
            pool.dma_start(vrow[0:124, 2, :], a["conv_w"][0].rearrange("j (k p) -> (j k) p", p=P)).then_inc(s_vrow, 16)
            pool.dma_start(vrow[0:88, 3, :], a["ffn_conv_w"][0, 0:2].rearrange("j (k p) -> (j k) p", p=P)).then_inc(s_vrow, 16)
            pool.dma_start(vrow[88:92, 3, :], a["conv_b"][0].rearrange("(k p) -> k p", p=P)).then_inc(s_vrow, 16)
            pool.dma_start(vrow[92:96, 3, :], a["conv_ln_g"][0].rearrange("(k p) -> k p", p=P)).then_inc(s_vrow, 16)
            pool.dma_start(vrow[96:100, 3, :], a["conv_ln_b"][0].rearrange("(k p) -> k p", p=P)).then_inc(s_vrow, 16)
            pool.dma_start(vrow[0:44, 4, :], a["ffn_conv_w"][0, 2].rearrange("(k p) -> k p", p=P)).then_inc(s_vrow, 16)
            pool.dma_start(vrow[44:88, 4, :], a["ffn_conv_b"][0].rearrange("(k p) -> k p", p=P)).then_inc(s_vrow, 16)
            pool.wait_ge(s_const, 16)
            pool.dma_start(E_dram.rearrange("h r c -> (h r) c"),
                           consts[0:HA * 7, C_ZERO:C_ZERO + P]).then_inc(s_E0, 16)
            pool.wait_ge(s_E0, 16)
            pool.dma_start(E_dram[:, :, 48:79], a["rpb"][0][:, 4:11, :]).then_inc(s_E1, 16)
            pool.wait_ge(s_E1, 16)
            pool.dma_start(R_dram, bass.AP(E_dram.tensor, 0, [[0, GRID], [1, EL]])).then_inc(s_E1, 16)
            pool.wait_ge(s_E1, 32)
            pool.wait_ge(s_h, 1)
            for i in range(2):
                for h in range(HA):
                    src = bass.AP(R_dram.tensor, h * 7 * P + (1 - i) * P + 63, [[EL - 1, GRID], [P, 6], [1, GRID]])
                    pool.dma_start(Bm[half(i), h], src).then_inc(s_Bm, 16)
            pool.dma_start(cv, a["cache_v"][0, 0].rearrange("t h d -> t (h d)")).then_inc(s_cache, 16)
            pool.wait_ge(s_blk, B_OUT)
            pool.dma_start(ck, a["cache_k"][0, 0].rearrange("t h d -> t (h d)")).then_inc(s_cache, 16)
            pool.wait_ge(s_cache, 32)

        @block.tensor
        def _(pe):
            mm, tr = nc.tensor.matmul, nc.tensor.transpose

            def arrived(n):
                pe.wait_ge(s_w[n % RING], 16 * (n // RING + 1))

            pe.wait_ge(s_const, 16)
            pe.wait_ge(s_vrow, 16 * 12)
            for g, rows in enumerate((2 * KT, 128, 124, 100, 88)):
                tr(ps[:, g, 0:rows], vrow[0:rows, g, :], ident[0:rows, 0:rows]).then_inc(s_vt, 1)
            for t in range(3):
                pe.wait_ge(s_xn, t + 1)
                for g in range(4):
                    n = 4 * t + g
                    bank = 5 + n % 3
                    if n >= 3:
                        pe.wait_ge(s_xc, n - 2)
                    for j in range(4):
                        last = tr(ps[:, bank, toks(j)], xn[:, t, toks(4 * g + j)], ident)
                    last.then_inc(s_xt, 1)

            def mod_block(i):
                arrived(i)
                if i >= 2:
                    pe.wait_ge(s_mrow, i - 1)
                wv = slot_of(i).rearrange("p (k c) -> p k c", k=KT)
                for k in range(KT):
                    last = mm(ps[0:2, i % 2, 0:BLK], cT[:, k:k + KT + 1:KT], wv[:, k, :], start=(k == 0), stop=(k == KT - 1))
                last.then_inc(s_blk, 1)

            def mod_cols(i):
                pe.wait_ge(s_mrow, i + 1)
                if i >= 2:
                    pe.wait_ge(s_mcol, i - 1)
                for j in range(2):
                    last = mm(ps[:, 2 + i % 2, 2 * j:2 * j + 2], modrow[0:2, i % 2, toks(j)], ident[0:2, 0:2], start=True, stop=True)
                last.then_inc(s_mcT, 1)

            pe.wait_ge(s_vc, 4)
            pe.wait_ge(s_ct, 1)
            for i in range(N_MOD):
                mod_block(i)
                if i:
                    mod_cols(i - 1)
            mod_cols(N_MOD - 1)

            pe.wait_ge(s_h, 1)
            m = 0
            for j, (kind, what, c0, w, _) in enumerate(IN_BLOCKS):
                n = B_IN + j
                arrived(n)
                wv = slot_of(n)[:, 0:KT * w].rearrange("p (k c) -> p k c", k=KT)
                for s in range(3 if kind == "tok" else w // P):
                    if m >= 8:
                        e = ITEMS[m - 8][5]
                        pe.wait_ge(s_eact if e == "act" else s_edve, evacs(e, m - 7))
                    for k in range(KT):
                        if kind == "tok":
                            last = mm(ps[:, m % 8, 0:w], hT[:, k, toks(s)], wv[:, k, :], start=(k == 0), stop=(k == KT - 1))
                        else:
                            last = mm(ps[:, m % 8, 0:TOK], wv[:, k, toks(s)], hT[:, k, :], start=(k == 0), stop=(k == KT - 1))
                    last.then_inc(s_item, 1)
                    m += 1
                pe.wait_ge(s_item, m)
                pe.sem_inc(s_blk, 1)

            pe.wait_ge(s_eact, evacs("act", len(ITEMS)))
            pe.wait_ge(s_edve, evacs("dve", len(ITEMS)))
            pe.wait_ge(s_cbuf, 1)
            for t in range(BT):
                last = mm(ps[:, 0, 0:CW], consts[:, C_MEAN:C_MEAN + P], cbuf[:, t, :], start=(t == 0), stop=(t == BT - 1))
            last.then_inc(s_cmean, 1)
            pe.wait_ge(s_csq, 1)
            for t in range(BT):
                last = mm(ps[:, 1, 0:CW], consts[:, C_MEAN:C_MEAN + P], csq[:, t, :], start=(t == 0), stop=(t == BT - 1))
            last.then_inc(s_cvar, 1)

            pe.wait_ge(s_cache, 32)
            for i in range(6):
                last = tr(ps[:, 6 + i // 3, toks(i % 3)], ck[:, toks(i)], ident)
            last.then_inc(s_ckt, 1)
            for i in range(6):
                last = tr(ps[:, 4 + i // 3, toks(i % 3)], qkT[:, 6 + i, 0:P], ident)
            last.then_inc(s_knt, 1)
            pe.wait_ge(s_cn, 1)
            pe.wait_ge(s_ckc, 2)
            pe.wait_ge(s_knc, 2)

            def scores(u):
                t, h = ATT[u]
                r = half(h % 2)
                if u >= 2:
                    pe.wait_ge(s_sm, u - 1)
                bank = u % 2
                q = qkT[r, h // 2, toks(t)]
                if t == 0:
                    last = mm(ps[:, bank, 0:P], q, qkT[r, 6 + h // 2, 0:P], start=True, stop=True)
                else:
                    mm(ps[:, bank, 0:2 * P], q, qkT[r, 6 + h // 2, P:TOK], start=True, stop=True)
                    last = mm(ps[:, bank, 2 * P:TOK], q, ckT[r, h // 2, :], start=True, stop=True)
                last.then_inc(s_sc, 1)

            def turn(u):
                t, h = ATT[u]
                pe.wait_ge(s_nr, u + 1)
                if u >= 2:
                    pe.wait_ge(s_ptc, u - 1)
                for k in range(1 if t == 0 else 3):
                    last = tr(ps[:, 2 + u % 2, toks(k)], ss[:, u % 3, toks(k)], ident)
                last.then_inc(s_pt, 1)

            def pv(u):
                t, h = ATT[u]
                pe.wait_ge(s_ptc, u + 1)
                if u >= 4 and h % 2 == 0:
                    pe.wait_ge(s_pvc, u // 2 - 1)
                o_ = ps[half(h % 2), 4 + (u // 2) % 2, 0:P]
                keys = [v_tok[:, 0, :]] if t == 0 else [v_tok[:, 1, :], v_tok[:, 2, :], cv]
                for k, vv in enumerate(keys):
                    last = mm(o_, vv[:, HD * h:HD * h + HD], PT[:, u % 2, toks(k)], start=(k == 0), stop=(k == len(keys) - 1))
                last.then_inc(s_pv, 1)

            for u in range(len(ATT) + 3):
                if u < len(ATT):
                    scores(u)
                if 0 <= u - 2 < len(ATT):
                    turn(u - 2)
                if 0 <= u - 3:
                    pv(u - 3)
            pe.wait_ge(s_pvc, len(ATT) // 2)

            for u in range(12):
                hf, u6 = u // 6, u % 6
                t, d, s0 = UNITS[u6]
                tk = toks(t)
                m4 = consts[:, C_M4 + 512 * d:C_M4 + 512 * d + 512]
                m4o = consts[:, C_M4 + 512 * (1 - d):C_M4 + 512 * (1 - d) + 512]
                v = rkv[:, t, 1536 + HW * hf:1536 + HW * hf + HW]
                if u6 == 0:
                    pe.wait_ge(s_par, 16 * LOADS_PER_HALF * (hf + 1))
                if u6 == 2:
                    pe.wait_ge(s_sraw, 32 * (hf + 1))
                    for dd, raw in enumerate((sraw, sraw2)):
                        for i in range(3):
                            last = tr(ps[:, 7, (3 * dd + i) * HD:(3 * dd + i + 1) * HD], raw[0:HD, toks(i)], ident[0:HD, 0:HD])
                    last.then_inc(s_sT, 1)
                    pe.wait_ge(s_S0, 2 * hf + 2)
                if u:
                    pe.wait_ge(s_rdone, u)
                mm(ps[:, 0, 0:HW], lora[half(d), 0, tk], par[half(d), 9, :], start=True, stop=True)
                mm(ps[:, 1, 0:HW], lora[half(d), 1, tk], par[half(d), 10, :], start=True, stop=True).then_inc(s_rlora, 1)
                pe.wait_ge(s_rsig, u + 1)
                mm(ps[:, 2, 0:HW], m4[:, P:2 * P], tW, start=True, stop=True)
                mm(ps[:, 3, 0:HW], m4[:, 0:P], tW, start=True, stop=True)
                mm(ps[:, 4, 0:HW], m4o[:, 0:P], tW, start=True, stop=True)
                mm(ps[:, 5, 0:HW], consts[:, C_BONES:C_BONES + P], tW, start=True, stop=True).then_inc(s_rcum, 1)
                pe.wait_ge(s_rtil, u + 1)
                for i in range(3):
                    tr(ps[:, 0, toks(i)], tmp[:, toks(i)], ident)
                for i in range(3):
                    tr(ps[:, 1, toks(i)], rtil[:, toks(i)], ident)
                for i in range(3):
                    tr(ps[:, 4, toks(i)], btil[:, toks(i)], ident)
                for i in range(3):
                    last = tr(ps[:, 5, toks(i)], ktil[:, toks(i)], ident)
                last.then_inc(s_rtr, 1)
                pe.wait_ge(s_rtc, u + 1)
                for h in range(HH):
                    r, i = half(h % 2), h // 2
                    if h >= 4:
                        pe.wait_ge(s_rAm, HH * u + h - 3)
                    zr = zrT[r, i, :, :].rearrange("p a b -> p (a b)")
                    mm(ps[:, h % 4, 0:2 * P], bT[r, i, :], zr, start=True, stop=True)
                    mm(ps[:, h % 4, 2 * P:4 * P], kT[r, i, :], zr, start=True, stop=True).then_inc(s_rA, 1)
                for h in range(HH):
                    pe.wait_ge(s_rAm, HH * u + h + 1)
                    last = tr(ps[:, 4 + h // 3, toks(h % 3)], Am[:, h, 0, :], ident)
                last.then_inc(s_rN, 1)
                for h in range(HH):
                    last = mm(ps[:, 6, HD * h:HD * h + HD], Am[:, h, 2, :], v[:, HD * h:HD * h + HD], start=True, stop=True)
                last.then_inc(s_rAV, 1)
                for l in range(LEVELS):
                    for g in range(2):
                        if l == 0 and g == 0:
                            pe.wait_ge(s_rT0, u + 1)
                        if l:
                            pe.wait_ge(s_rTu, 2 * LEVELS * u + 2 * (l - 1) + g + 1)
                        for h in range(3 * g, 3 * g + 3):
                            last = mm(ps[:, g, toks(h % 3)], Nm[:, h, :], TTm[:, h, :], start=True, stop=True)
                        last.then_inc(s_rX, 1)
                    for g in range(2):
                        pe.wait_ge(s_rXm, 2 * LEVELS * u + 2 * l + g + 1)
                        for h in range(3 * g, 3 * g + 3):
                            mm(ps[:, 2 + g, toks(h % 3)], Xm[:, h, :], Tm[:, h, :], start=True, stop=True)
                            last = mm(ps[:, 4 + g, toks(h % 3)], Tm[:, h, :], Xm[:, h, :], start=True, stop=True)
                        last.then_inc(s_rTp, 1)
                pe.wait_ge(s_rTu, 2 * LEVELS * (u + 1))
                pe.wait_ge(s_rAVc, u + 1)
                for h in range(HH):
                    last = mm(ps[:, h // 3, toks(h % 3)], TTm[:, h, :], ZA[:, h, :, :].rearrange("p a b -> p (a b)"), start=True, stop=True)
                last.then_inc(s_rZU, 1)
                pe.wait_ge(s_rZUc, u + 1)
                pe.wait_ge(s_rbar, u + 1)
                for h in range(HH):
                    r, i = half(h % 2), h // 2
                    mm(ps[r, 2, toks(i)], ZU[:, h, 0, :], Am[:, h, 1, :], start=True, stop=True)
                for p in range(2):
                    c = half(p)
                    for h in range(HH):
                        r, i = half(h % 2), h // 2
                        hs = slice(HD * h, HD * h + HD)
                        mm(ps[r, 3 + p, HD * i:HD * i + HD], ZU[c, h, 0, :], Bbar[c, hs], start=True, stop=True)
                        mm(ps[r, 3 + p, 192 + HD * i:192 + HD * i + HD], Bbar[c, hs], ZU[c, h, 1, :], start=True, stop=False)
                        last = mm(ps[r, 3 + p, 192 + HD * i:192 + HD * i + HD], Kbar[c, hs], v[c, hs], start=False, stop=True)
                last.then_inc(s_rQM, 1)
                pe.wait_ge(s_rQMc, u + 1)
                for s in range(2):
                    c = s if d == 0 else 1 - s
                    if s:
                        pe.wait_ge(s_rS, 2 * u + 1)
                    for h in range(HH):
                        r, i = half(h % 2), h // 2
                        last = mm(ps[r, 5 + h % 2, HD * i:HD * i + HD], MT[r, c, i, :], S[r, 5 * d + s0 + s, i, :], start=True, stop=True)
                    last.then_inc(s_rSp, 1)
                for h in range(HH):
                    r, i = half(h % 2), h // 2
                    o_ = ps[:, h % 2, HD * i:HD * i + HD]
                    mm(o_, Am[:, h, 1, :], ZU[:, h, 1, :], start=True, stop=False)
                    for c in range(2):
                        s = c if d == 0 else 1 - c
                        mm(ps[half(c), h % 2, HD * i:HD * i + HD], QT[r, i, half(c)], S[r, 5 * d + s0 + s, i, :],
                           start=False, stop=False)
                    last = mm(o_, Am[:, h, 3, :], v[:, HD * h:HD * h + HD], start=False, stop=True)
                last.then_inc(s_rO, 1)
                if u6 < 2:
                    pe.wait_ge(s_rS, 2 * u + 2)
                    if u6 == 1:
                        pe.wait_ge(s_stc, 2 * hf + 1)
                    for i in range(3):
                        last = tr(ps[0:HD, 7, toks(i)], S[:, 5 * d + 2, i, :], ident)
                    last.then_inc(s_stT, 1)
                if u6 in FINAL:
                    w_, t_ = FINAL[u6]
                    f = 3 * hf + w_
                    if u6 == 1:
                        pe.wait_ge(s_stc, 2 * hf + 2)
                    mm(ps[:, 7, 0:HW], lora[:, 2, toks(t_)], par[:, 11, :], start=True, stop=True).then_inc(s_fg, 1)
                    pe.wait_ge(s_fy, f + 1)
                    for i in range(3):
                        last = tr(ps[:, 6, toks(i)], Oacc[:, w_ % 2 if w_ < 2 else 0, toks(i)], ident)
                    last.then_inc(s_fT, 1)
                    pe.wait_ge(s_fc, f + 1)

            def gate_rows(col0, ready, read):
                for n in range(8):
                    g, q = n // 4, n % 4
                    if n >= 2:
                        pe.wait_ge(read, n - 1)
                    for j in range(4):
                        col = modcol[:, col0 + 4 * q + j, g:g + 1].broadcast_to([P, P])
                        last = mm(ps[:, 6 + n % 2, toks(j)], col, ident, start=True, stop=True)
                    last.then_inc(ready, 1)

            gate_rows(2 * KT, s_gbp, s_gbc)
            for j in range(D // BLK):
                n = B_OUT + j
                arrived(n)
                wv = slot_of(n).rearrange("p (k c) -> p k c", k=KT)
                for t in range(3):
                    if j >= 2:
                        pe.wait_ge(s_oc, 3 * (j - 2) + t + 1)
                    for k in range(KT):
                        last = mm(ps[:, 3 * (j % 2) + t, 0:BLK], yT[:, k, toks(t)], wv[:, k, :], start=(k == 0), stop=(k == KT - 1))
                    last.then_inc(s_o, 1)
                pe.wait_ge(s_o, 3 * j + 3)
                pe.sem_inc(s_blk, 1)
            pe.wait_ge(s_oc, 3 * (D // BLK))
            for t in range(3):
                pe.wait_ge(s_xn2, t + 1)
                for g in range(4):
                    n = 4 * t + g
                    if n >= 4:
                        pe.wait_ge(s_h2, n - 3)
                    for j in range(4):
                        last = tr(ps[:, n % 4, toks(j)], xn2[:, t, toks(4 * g + j)], ident)
                    last.then_inc(s_xt2, 1)
            gate_rows(5 * KT, s_gb2p, s_gb2c)
            pe.wait_ge(s_h2, 12)
            pe.wait_ge(s_gb2c, 8)
            for i in range(DFF // BLK):
                for w in range(2):
                    n = B_UP + 2 * i + w
                    arrived(n)
                    wv = slot_of(n).rearrange("p (k c) -> p k c", k=KT)
                    for s in range(2):
                        if i >= 2 - 0:
                            pe.wait_ge(s_uc if w == 0 else s_uact, 2 * (i - 2) + s + 1)
                        for k in range(KT):
                            last = mm(ps[:, 4 * (i % 2) + 2 * w + s, 0:TOK], wv[:, k, toks(s)], hT[:, k, :], start=(k == 0), stop=(k == KT - 1))
                        last.then_inc(s_up, 1)
                    pe.wait_ge(s_up, 4 * i + 2 * w + 2)
                    pe.sem_inc(s_blk, 1)
            pe.wait_ge(s_uact, FT)
            for q in range(2):
                for g in range(FT // DOWN_KT):
                    n = B_DOWN + q * (FT // DOWN_KT) + g
                    arrived(n)
                    wv = slot_of(n).rearrange("p (k c) -> p k c", k=DOWN_KT)
                    for k in range(DOWN_KT):
                        kk_ = DOWN_KT * g + k
                        for t in range(3):
                            for c in range(2):
                                if q == 1 and kk_ == 0:
                                    b_ = 2 * t + c - 2
                                    if b_ >= 0:
                                        pe.wait_ge(s_dc, b_ + 1)
                                last = mm(ps[:, (6 * q + 2 * t + c) % 8, :], act[:, kk_, toks(t)], wv[:, k, 512 * c:512 * c + 512],
                                          start=(kk_ == 0), stop=(kk_ == FT - 1), skip_group_check=True)
                    last.then_inc(s_blk, 1)

        @block.scalar
        def _(ac):
            AC = nc.scalar.activation
            cnt = [0]

            def link(ins):
                cnt[0] += 1
                ins.then_inc(s_a, 1)
                ac.wait_ge(s_a, cnt[0])

            roots = [0]

            def root(ap):
                roots[0] += 1
                ac.wait_ge(s_var, roots[0])
                AC(ap, ap, ACT.Sqrt).then_inc(s_root, 1)

            for t in range(3):
                ac.wait_ge(s_x, 48)
                AC(junk, x[:, t, :], ACT.Square, accum_out=stat[:, t:t + 1]).then_inc(s_ssq, 1)
                ac.wait_ge(s_ssq, t + 1)
            ac.wait_ge(s_vt, 1)
            AC(csig, ps[:, 0, 0:2 * KT], ACT.Sigmoid).then_inc(s_csig, 1)
            root(stat[:, 4:7])
            for n in range(12):
                t, g = n // 4, n % 4
                ac.wait_ge(s_xt, n + 1)
                AC(hT[:, 4 * g:4 * g + 4, toks(t)], ps[:, 5 + n % 3, :].rearrange("p (j c) -> p j c", j=4), ACT.Copy).then_inc(s_xc, 1)
            for i in range(N_MOD):
                ac.wait_ge(s_blk, i + 1)
                if i >= 2:
                    ac.wait_ge(s_mcT, i - 1)
                AC(modrow[0:2, i % 2, :], ps[0:2, i % 2, 0:BLK], ACT.Copy).then_inc(s_mrow, 1)
            for m, (n, kind, what, j, s, eng) in enumerate(ITEMS):
                if eng != "act":
                    continue
                ac.wait_ge(s_item, m + 1)
                if what == "q":
                    AC(qkT[:, j + s, :], ps[:, m % 8, 0:TOK], ACT.Copy).then_inc(s_eact, 1)
                elif what == "v":
                    AC(v_tok[:, s, BLK * j:BLK * j + BLK], ps[:, m % 8, 0:BLK], ACT.Copy).then_inc(s_eact, 1)
                elif what == "rkv":
                    AC(rkv[:, s, BLK * j:BLK * j + BLK], ps[:, m % 8, 0:BLK], ACT.Copy).then_inc(s_eact, 1)
                elif what == "glu_b":
                    if j:
                        ac.wait_ge(s_edve, evacs("dve", m))
                    AC(sgt[:, s, :], ps[:, m % 8, 0:TOK], ACT.Sigmoid).then_inc(s_eact, 1)
                else:
                    f = (ACT.Tanh, ACT.Copy, ACT.Sigmoid)[j + s]
                    AC(lora[:, j + s, :], ps[:, m % 8, 0:TOK], f).then_inc(s_eact, 1)
            ac.wait_ge(s_ccen, 1)
            AC(csq, cbuf, ACT.Square).then_inc(s_csq, 1)
            ac.wait_ge(s_ckt, 1)
            for i in range(2):
                AC(ckT[:, 3 * i:3 * i + 3, :], ps[:, 6 + i, 0:TOK].rearrange("p (j c) -> p j c", j=3), ACT.Copy).then_inc(s_ckc, 1)
            ac.wait_ge(s_knt, 1)
            for i in range(2):
                AC(knew[:, TOK * i:TOK * i + TOK], ps[:, 4 + i, 0:TOK], ACT.Copy).then_inc(s_knc, 1)
            root(crstd)
            ac.wait_ge(s_cn, 1)
            ac.wait_ge(s_blk, B_OUT)
            for t in range(BT):
                for (a0, b0, n) in ((0, 0, P), (P + PADC, P, 2 * P)):
                    AC(yT[:, 6 + t, b0:b0 + n], cbuf[:, t, a0:a0 + n], ACT.Silu,
                       scale=vcol[:, 2, 92 + t:93 + t], bias=vcol[:, 2, 96 + t:97 + t]).then_inc(s_cy, 1)

            def expo(u):
                t, h = ATT[u]
                n = P if t == 0 else TOK
                ac.wait_ge(s_sm, u + 1)
                AC(ss[:, u % 3, 0:n], ss[:, u % 3, 0:n], ACT.Exp, bias=stat[:, 8 + u % 4:9 + u % 4],
                   accum_out=stat[:, 16 + u % 4:17 + u % 4]).then_inc(s_ex, 1)

            def take(u):
                t, h = ATT[u]
                n = P if t == 0 else TOK
                ac.wait_ge(s_pt, u + 1)
                if u >= 2:
                    ac.wait_ge(s_pv, u - 1)
                AC(PT[:, u % 2, 0:n], ps[:, 2 + u % 2, 0:n], ACT.Copy).then_inc(s_ptc, 1)

            def result(u):
                t, h = ATT[u]
                ac.wait_ge(s_pv, u + 1)
                AC(yT[:, h // 2, toks(t)], ps[:, 4 + (u // 2) % 2, 0:P], ACT.Copy).then_inc(s_pvc, 1)

            for u in range(len(ATT) + 3):
                if u < len(ATT):
                    expo(u)
                if 0 <= u - 2 < len(ATT):
                    take(u - 2)
                if 0 <= u - 3 and (u - 3) % 2 == 1:
                    result(u - 3)

            for u in range(12):
                hf, u6 = u // 6, u % 6
                t, d, s0 = UNITS[u6]
                ac.wait_ge(s_rpre, u + 1)
                AC(tW, tW, ACT.Sigmoid)
                AC(tA, tA, ACT.Sigmoid).then_inc(s_rsig, 1)
                root(st6[:, 0, :])
                ac.wait_ge(s_rcum, u + 1)
                if u6 == 2:
                    ac.wait_ge(s_S0, 2 * hf + 2)
                AC(eE, ps[:, 3, 0:HW], ACT.Exp, scale=-DECAY)
                AC(eP, ps[:, 2, 0:HW], ACT.Exp, scale=-DECAY)
                if u6 in (1, 2):
                    ac.wait_ge(s_stout, 32 * hf + 16 * u6)
                AC(eN, ps[:, 2, 0:HW], ACT.Exp, scale=DECAY)
                AC(eR, ps[:, 4, 0:HW], ACT.Exp, scale=-DECAY)
                AC(eT, ps[:, 5, 0:HW], ACT.Exp, scale=-DECAY).then_inc(s_rexp, 1)
                ac.wait_ge(s_rtr, u + 1)
                tri = lambda b: ps[:, b, 0:HW].rearrange("p (j c) -> p j c", j=3)
                AC(zrT[:, :, 0, :], tri(0), ACT.Copy)
                AC(zrT[:, :, 1, :], tri(1), ACT.Copy)
                AC(bT, tri(4), ACT.Copy)
                AC(kT, tri(5), ACT.Copy).then_inc(s_rtc, 1)
                ac.wait_ge(s_rN, u + 1)
                for g in range(2):
                    AC(Nm[:, 3 * g:3 * g + 3, :], tri(4 + g), ACT.Copy).then_inc(s_rNc, 1)
                ac.wait_ge(s_rAV, u + 1)
                AC(ZA[:, :, 1, :], ps[:, 6, 0:HW].rearrange("p (h c) -> p h c", h=HH), ACT.Copy).then_inc(s_rAVc, 1)
                ac.wait_ge(s_rZU, u + 1)
                AC(ZU[:, 0:3, :, :].rearrange("p h a c -> p (h a c)"), ps[:, 0, 0:TOK], ACT.Copy)
                AC(ZU[:, 3:6, :, :].rearrange("p h a c -> p (h a c)"), ps[:, 1, 0:TOK], ACT.Copy).then_inc(s_rZUc, 1)
                if u6 < 2:
                    ac.wait_ge(s_stT, 2 * hf + u6 + 1)
                    ac.wait_ge(s_rdone, u + 1)
                    if u6 == 1:
                        ac.wait_ge(s_stout, 32 * hf + 16)
                    AC(sout[0:HD, :], ps[0:HD, 7, 0:HW], ACT.Copy).then_inc(s_stc, 1)
                if u6 in FINAL:
                    w_, t_ = FINAL[u6]
                    root(st6[:, 3, :])
                    ac.wait_ge(s_fT, 3 * hf + w_ + 1)
                    AC(yT[:, 10 + 3 * hf:13 + 3 * hf, toks(t_)], tri(6), ACT.Copy).then_inc(s_fc, 1)

            for n in range(8):
                ac.wait_ge(s_gbp, n + 1)
                AC(gb[:, n // 4, 512 * (n % 4):512 * (n % 4) + 512], ps[:, 6 + n % 2, :], ACT.Copy).then_inc(s_gbc, 1)
            ac.wait_ge(s_oc, 3 * (D // BLK))
            for t in range(3):
                AC(xn2[:, t, :], x[:, t, :], ACT.Square, accum_out=stat[:, 24 + t:25 + t]).then_inc(s_ssq2, 1)
            root(stat[:, 28:31])
            for n in range(8):
                ac.wait_ge(s_gb2p, n + 1)
                AC(gb[:, n // 4, 512 * (n % 4):512 * (n % 4) + 512], ps[:, 6 + n % 2, :], ACT.Copy).then_inc(s_gb2c, 1)
            for f in range(FT):
                i, s = f // 2, f % 2
                ac.wait_ge(s_up, 4 * i + s + 1)
                ac.wait_ge(s_pad, 2)
                if f >= 2:
                    ac.wait_ge(s_ucv, f - 1)
                b_ = 4 * (i % 2) + s
                AC(up2[:, s, 1:1 + P], ps[:, b_, 0:P], ACT.Copy)
                AC(up2[:, s, 2 + P:2 + TOK], ps[:, b_, P:TOK], ACT.Copy).then_inc(s_uc, 1)
                ac.wait_ge(s_ucv, f + 1)
                if f >= 2:
                    ac.wait_ge(s_uact, f - 1)
                AC(sg2[:, s, :], cv2[:, s, :], ACT.Silu).then_inc(s_usg, 1)
            for t in range(3):
                ac.wait_ge(s_dc, 6 + 2 * t + 2)
                AC(junk2, x[:, t, :], ACT.Square, accum_out=stat[:, 32 + t:33 + t]).then_inc(s_fss, 1)
                ac.wait_ge(s_fss, t + 1)
                root(stat[:, 36 + t:37 + t])

        @block.vector
        def _(dv):
            V = nc.vector
            cnt = [0]

            def link(ins):
                cnt[0] += 1
                ins.then_inc(s_d, 1)
                dv.wait_ge(s_d, cnt[0])

            roots = [0]

            def inv_root(ins, ap):
                roots[0] += 1
                ins.then_inc(s_var, 1)
                dv.wait_ge(s_root, roots[0])
                link(V.reciprocal(ap, ap))

            def mark(ins):
                cnt[0] += 1
                ins.then_inc(s_d, 1)
                return cnt[0]

            dv.wait_ge(s_csig, 1)
            V.tensor_tensor(cT[:, :], csig, ps[:, 0, 0:2 * KT], ALU.mult).then_inc(s_ct, 1)
            for g, rows in enumerate((128, 124, 100, 88)):
                dv.wait_ge(s_vt, g + 2)
                V.tensor_copy(vcol[:, g, 0:rows], ps[:, 1 + g, 0:rows]).then_inc(s_vc, 1)
            dv.wait_ge(s_ssq, 3)
            inv_root(V.tensor_scalar(stat[:, 4:7], stat[:, 0:3], 1.0 / D, 1e-6, ALU.mult, ALU.add), stat[:, 4:7])
            for t in range(3):
                V.tensor_scalar(xn[:, t, :], x[:, t, :], stat[:, 4 + t:5 + t], None, ALU.mult).then_inc(s_xn, 1)
            dv.wait_ge(s_vc, 4)
            for i in range(N_MOD):
                dv.wait_ge(s_mcT, i + 1)
                V.tensor_tensor(modcol[:, 2 * i:2 * i + 2, :], ps[:, 2 + i % 2, 0:4].rearrange("p (t g) -> p t g", g=2),
                                vcol[:, 0, 32 + 2 * i:34 + 2 * i].unsqueeze(2).broadcast_to([P, 2, 2]), ALU.add).then_inc(s_mcol, 1)
            dv.wait_ge(s_mcol, N_MOD)
            n1 = vcol[:, 0, 0:KT].unsqueeze(2).broadcast_to([P, KT, 2])
            n2 = vcol[:, 0, KT:2 * KT].unsqueeze(2).broadcast_to([P, KT, 2])
            link(V.tensor_scalar(scol, modcol[:, KT:2 * KT, :], 1.0, None, ALU.add))
            link(V.tensor_tensor(scol, scol, n1, ALU.mult))
            dv.wait_ge(s_xc, 12)
            for k in range(KT):
                for g, r in ((0, slice(0, P)), (1, slice(P, TOK))):
                    last = V.tensor_scalar(hT[:, k, r], hT[:, k, r], scol[:, k, g:g + 1], modcol[:, k, g:g + 1], ALU.mult, ALU.add)
            last.then_inc(s_h, 1)
            dv.wait_ge(s_h, 1)
            link(V.tensor_scalar(scol, modcol[:, 4 * KT:5 * KT, :], 1.0, None, ALU.add))
            link(V.tensor_tensor(scol, scol, n2, ALU.mult))
            for lo, n in ((0, PADC), (PADC + P, PADC), (PADC * 2 + TOK, PADC)):
                link(V.memset(upad[:, :, lo:lo + n], 0.0))
            for m, (n, kind, what, j, s, eng) in enumerate(ITEMS):
                if eng != "dve":
                    continue
                dv.wait_ge(s_item, m + 1)
                if what == "k":
                    V.tensor_copy(qkT[:, 6 + j + s, :], ps[:, m % 8, 0:TOK]).then_inc(s_edve, 1)
                else:
                    dv.wait_ge(s_eact, evacs("act", m))
                    V.tensor_tensor(upad[:, j + s, PADC:PADC + P], ps[:, m % 8, 0:P], sgt[:, s, 0:P], ALU.mult)
                    V.tensor_tensor(upad[:, j + s, 2 * PADC + P:2 * PADC + TOK], ps[:, m % 8, P:TOK], sgt[:, s, P:TOK],
                                    ALU.mult).then_inc(s_edve, 1)
            dv.wait_ge(s_edve, evacs("dve", len(ITEMS)))
            at = [0] * BT
            for j in range(CONV_K):
                for t in range(BT):
                    w = vcol[:, 1, 4 * j + t:4 * j + t + 1]
                    if j == 0:
                        at[t] = mark(V.tensor_scalar(cbuf[:, t, :], upad[:, t, 0:CW], w, vcol[:, 2, 88 + t:89 + t], ALU.mult, ALU.add))
                    else:
                        dv.wait_ge(s_d, at[t])
                        at[t] = mark(V.scalar_tensor_tensor(cbuf[:, t, :], upad[:, t, j:j + CW], w, cbuf[:, t, :], ALU.mult, ALU.add))
            dv.wait_ge(s_d, cnt[0])
            dv.sem_inc(s_cbuf, 1)
            dv.wait_ge(s_Bm, 16 * 2 * HA)
            V.tensor_tensor(Bm.rearrange("p h r c -> p (h r) c"), Bm.rearrange("p h r c -> p (h r) c"),
                            consts[:, C_COL:C_COL + GRID].unsqueeze(1).broadcast_to([P, 6 * HA, GRID]), ALU.add).then_inc(s_Bmask, 1)
            dv.wait_ge(s_cmean, 1)
            for t in range(BT):
                last = V.tensor_tensor(cbuf[:, t, :], cbuf[:, t, :], ps[:, 0, 0:CW], ALU.subtract)
            last.then_inc(s_ccen, 1)
            dv.wait_ge(s_cvar, 1)
            inv_root(V.tensor_scalar(crstd, ps[:, 1, 0:CW], 1e-5, None, ALU.add), crstd)
            for t in range(BT):
                last = V.tensor_tensor(cbuf[:, t, :], cbuf[:, t, :], crstd, ALU.mult)
            last.then_inc(s_cn, 1)

            dv.wait_ge(s_Bmask, 1)

            def softmax(u):
                t, h = ATT[u]
                n = P if t == 0 else TOK
                dv.wait_ge(s_sc, u + 1)
                if u >= 3:
                    dv.wait_ge(s_pt, u - 2)
                if t == 0:
                    link(V.tensor_scalar(ss[:, u % 3, 0:P], ps[:, u % 2, 0:P], SCALE, None, ALU.mult))
                else:
                    b_ = Bm[:, h, 4 - 2 * t:8 - 2 * t, :].rearrange("p r c -> p (r c)")
                    V.scalar_tensor_tensor(ss[:, u % 3, 0:2 * P], ps[:, u % 2, 0:2 * P], SCALE, b_, ALU.mult, ALU.add)
                    link(V.tensor_scalar(ss[:, u % 3, 2 * P:TOK], ps[:, u % 2, 2 * P:TOK], SCALE, None, ALU.mult))
                V.tensor_reduce(stat[:, 8 + u % 4:9 + u % 4], ss[:, u % 3, 0:n], AX.X, ALU.max, negate=True).then_inc(s_sm, 1)

            def norm(u):
                t, h = ATT[u]
                n = P if t == 0 else TOK
                dv.wait_ge(s_ex, u + 1)
                link(V.reciprocal(stat[:, 20 + u % 4:21 + u % 4], stat[:, 16 + u % 4:17 + u % 4]))
                V.tensor_scalar(ss[:, u % 3, 0:n], ss[:, u % 3, 0:n], stat[:, 20 + u % 4:21 + u % 4], None, ALU.mult).then_inc(s_nr, 1)

            for u in range(len(ATT) + 1):
                if u < len(ATT):
                    softmax(u)
                if u:
                    norm(u - 1)
            dv.wait_ge(s_pvc, len(ATT) // 2)

            def heads(ap):
                return ap.rearrange("p (h c) -> p h c", h=HH)

            for u in range(12):
                hf, u6 = u // 6, u % 6
                t, d, s0 = UNITS[u6]
                rr, kr, vr = (rkv[:, t, q + HW * hf:q + HW * hf + HW] for q in (0, 768, 1536))
                acc = 0 if t < 2 else 1
                if u6 == 0:
                    dv.wait_ge(s_par, 16 * LOADS_PER_HALF * (hf + 1))
                    for dd in range(2):
                        last = V.memset(S[:, 5 * dd, :, :], 0.0)
                    last.then_inc(s_S0, 1)
                    dv.wait_ge(s_S0, 2 * hf + 1)
                if u6 == 2:
                    dv.wait_ge(s_sT, hf + 1)
                    for dd in range(2):
                        last = V.tensor_copy(S[:, 5 * dd, :, :], ps[:, 7, 192 * dd:192 * dd + 192].rearrange("p (i c) -> p i c", i=3))
                    last.then_inc(s_S0, 1)
                dv.wait_ge(s_rlora, u + 1)
                V.tensor_tensor(tW, ps[:, 0, 0:HW], par[:, d, :], ALU.add)
                V.tensor_tensor(tA, ps[:, 1, 0:HW], par[:, 2 + d, :], ALU.add).then_inc(s_rpre, 1)
                link(V.tensor_tensor(kkn, kr, par[:, 4, :], ALU.mult))
                link(V.tensor_tensor(sq, kkn, kkn, ALU.mult))
                link(V.tensor_reduce(st6[:, 0, :], heads(sq), AX.X, ALU.add))
                inv_root(V.tensor_scalar(st6[:, 0, :], st6[:, 0, :], 1e-12, None, ALU.add), st6[:, 0, :])
                link(V.tensor_tensor(heads(kkn), heads(kkn), st6[:, 0, :].unsqueeze(2).broadcast_to([P, HH, HD]), ALU.mult))
                dv.wait_ge(s_rsig, u + 1)
                V.tensor_tensor(b1, kkn, tA, ALU.mult)
                link(V.scalar_tensor_tensor(kd, tA, 1.0, par[:, 5, :], ALU.subtract, ALU.mult))
                link(V.scalar_tensor_tensor(kd, kd, 1.0, kr, ALU.add, ALU.mult))
                link(V.tensor_tensor(sq, rr, kd, ALU.mult))
                link(V.tensor_tensor(sq, sq, par[:, 6, :], ALU.mult))
                if d == 0 or u6 == 3:
                    first = u6 in (0, 2, 3)
                else:
                    first = False
                if first:
                    link(V.tensor_reduce(bsum[:, acc, :], heads(sq), AX.X, ALU.add))
                else:
                    link(V.tensor_reduce(st6[:, 1, :], heads(sq), AX.X, ALU.add))
                    link(V.tensor_tensor(bsum[:, acc, :], bsum[:, acc, :], st6[:, 1, :], ALU.add))
                dv.wait_ge(s_rexp, u + 1)
                link(V.scalar_tensor_tensor(tmp, kkn, -1.0, eE, ALU.mult, ALU.mult))
                V.tensor_tensor(rtil, rr, eP, ALU.mult)
                V.tensor_tensor(btil, b1, eN, ALU.mult)
                V.tensor_tensor(ktil, kd, eN, ALU.mult).then_inc(s_rtil, 1)
                V.tensor_copy(ZA[:, :, 0, :], heads(tmp))
                V.tensor_tensor(Bbar, b1, eR, ALU.mult)
                V.tensor_tensor(Kbar, kd, eR, ALU.mult)
                for p in range(2):
                    for hp in range(2):
                        src = eT[half(p), :].rearrange("p (i a c) -> p i a c", i=3, a=2)[:, :, hp, :]
                        last = V.tensor_tensor(dP[half(hp), p, :, :], src,
                                               consts[half(p), C_ID + 64 * p:C_ID + 64 * p + 64].unsqueeze(1).broadcast_to([HD, 3, HD]), ALU.mult)
                last.then_inc(s_rbar, 1)
                m4 = consts[:, C_M4 + 512 * d:C_M4 + 512 * d + 512]
                for h in range(HH):
                    dv.wait_ge(s_rA, HH * u + h + 1)
                    V.tensor_tensor(Am[:, h, :, :].rearrange("p a b -> p (a b)"), ps[:, h % 4, :], m4, ALU.mult).then_inc(s_rAm, 1)
                same2 = consts[:, C_SAME2:C_SAME2 + P].unsqueeze(1).broadcast_to([P, HH, P])
                idb = ident.unsqueeze(1).broadcast_to([P, HH, P])
                dv.wait_ge(s_rAm, HH * (u + 1))
                link(V.tensor_tensor(TTm, Am[:, :, 0, :], same2, ALU.mult))
                V.tensor_tensor(TTm, TTm, idb, ALU.add)
                dv.wait_ge(s_rNc, 2 * u + 2)
                link(V.tensor_tensor(Tm, Nm, same2, ALU.mult))
                V.tensor_tensor(Tm, Tm, idb, ALU.add).then_inc(s_rT0, 1)
                tri = lambda b: ps[:, b, 0:HW].rearrange("p (j c) -> p j c", j=3)
                dv.wait_ge(s_rT0, u + 1)
                for l in range(LEVELS):
                    xm = consts[:, C_XM + (LEVELS * d + l) * P:C_XM + (LEVELS * d + l + 1) * P].unsqueeze(1).broadcast_to([P, 3, P])
                    for g in range(2):
                        dv.wait_ge(s_rX, 2 * LEVELS * u + 2 * l + g + 1)
                        V.tensor_tensor(Xm[:, 3 * g:3 * g + 3, :], tri(g), xm, ALU.mult).then_inc(s_rXm, 1)
                    for g in range(2):
                        dv.wait_ge(s_rTp, 2 * LEVELS * u + 2 * l + g + 1)
                        V.tensor_tensor(Tm[:, 3 * g:3 * g + 3, :], Tm[:, 3 * g:3 * g + 3, :], tri(2 + g), ALU.add)
                        V.tensor_tensor(TTm[:, 3 * g:3 * g + 3, :], TTm[:, 3 * g:3 * g + 3, :], tri(4 + g), ALU.add).then_inc(s_rTu, 1)
                dv.wait_ge(s_rQM, u + 1)
                V.tensor_tensor(QT, tri(2), zrT[:, :, 1, :], ALU.add)
                for p in range(2):
                    V.tensor_tensor(MT[:, p], ps[:, 3 + p, 0:192].rearrange("p (i c) -> p i c", i=3), dP[:, p], ALU.add)
                    last = V.tensor_copy(Sh[:, p], ps[:, 3 + p, 192:384].rearrange("p (i c) -> p i c", i=3))
                last.then_inc(s_rQMc, 1)
                dv.wait_ge(s_rQMc, u + 1)
                for s in range(2):
                    c = s if d == 0 else 1 - s
                    dv.wait_ge(s_rSp, 2 * u + s + 1)
                    for hp in range(2):
                        last = V.tensor_tensor(S[half(hp), 5 * d + s0 + s + 1], Sh[half(hp), c],
                                               ps[half(hp), 5 + hp, 0:192].rearrange("p (i c) -> p i c", i=3), ALU.add)
                    last.then_inc(s_rS, 1)
                dv.wait_ge(s_rO, u + 1)
                for hp in range(2):
                    dst = Oacc[:, acc, :].rearrange("p (i a c) -> p i a c", i=3, a=2)[:, :, hp, :]
                    src = ps[:, hp, 0:192].rearrange("p (i c) -> p i c", i=3)
                    if u6 in (0, 2, 3):
                        last = V.tensor_copy(dst, src)
                    else:
                        last = V.tensor_tensor(dst, dst, src, ALU.add)
                last.then_inc(s_rdone, 1)
                if u6 in FINAL:
                    w_, t_ = FINAL[u6]
                    f = 3 * hf + w_
                    O = Oacc[:, acc, :]
                    dv.wait_ge(s_rdone, u + 1)
                    link(V.tensor_reduce(st6[:, 2, :], heads(O), AX.X, ALU.add))
                    link(V.scalar_tensor_tensor(heads(O), st6[:, 2, :].unsqueeze(2).broadcast_to([P, HH, HD]), -1.0 / HD, heads(O), ALU.mult, ALU.add))
                    link(V.tensor_tensor(sq, O, O, ALU.mult))
                    link(V.tensor_reduce(st6[:, 3, :], heads(sq), AX.X, ALU.add))
                    inv_root(V.tensor_scalar(st6[:, 3, :], st6[:, 3, :], 1.0 / HD, 64e-5, ALU.mult, ALU.add), st6[:, 3, :])
                    link(V.tensor_tensor(heads(O), heads(O), st6[:, 3, :].unsqueeze(2).broadcast_to([P, HH, HD]), ALU.mult))
                    link(V.tensor_tensor(O, O, par[:, 7, :], ALU.mult))
                    V.tensor_tensor(heads(sq), heads(vr), bsum[:, acc, :].unsqueeze(2).broadcast_to([P, HH, HD]), ALU.mult)
                    link(V.tensor_tensor(O, O, par[:, 8, :], ALU.add))
                    link(V.tensor_tensor(O, O, sq, ALU.add))
                    dv.wait_ge(s_fg, f + 1)
                    V.tensor_tensor(O, O, ps[:, 7, 0:HW], ALU.mult).then_inc(s_fy, 1)
                    dv.wait_ge(s_fT, f + 1)

            dv.wait_ge(s_fc, 6)
            for lo in (0, 1 + P, 2 + TOK):
                last = V.memset(up2[:, :, lo:lo + 1], 0.0)
            last.then_inc(s_pad, 2)
            dv.wait_ge(s_x2, 48)
            dv.wait_ge(s_gbc, 8)
            for j in range(D // BLK):
                for t in range(3):
                    n = 3 * j + t
                    cs = slice(BLK * j, BLK * j + BLK)
                    dv.wait_ge(s_o, n + 1)
                    link(V.tensor_tensor(ytmp, ps[:, 3 * (j % 2) + t, 0:BLK], gb[:, min(t, 1), cs], ALU.mult))
                    V.tensor_tensor(x[:, t, cs], x[:, t, cs], ytmp, ALU.add).then_inc(s_oc, 1)
                    dv.wait_ge(s_oc, n + 1)
            dv.wait_ge(s_ssq2, 3)
            inv_root(V.tensor_scalar(stat[:, 28:31], stat[:, 24:27], 1.0 / D, 1e-6, ALU.mult, ALU.add), stat[:, 28:31])
            for t in range(3):
                V.tensor_scalar(xn2[:, t, :], x[:, t, :], stat[:, 28 + t:29 + t], None, ALU.mult).then_inc(s_xn2, 1)
            for n in range(12):
                t, q = n // 4, n % 4
                g = min(t, 1)
                dv.wait_ge(s_xt2, n + 1)
                for j in range(4):
                    k = 4 * q + j
                    last = V.tensor_scalar(hT[:, k, toks(t)], ps[:, n % 4, toks(j)], scol[:, k, g:g + 1],
                                           modcol[:, 3 * KT + k, g:g + 1], ALU.mult, ALU.add)
                last.then_inc(s_h2, 1)
            for f in range(FT):
                i, s = f // 2, f % 2
                dv.wait_ge(s_uc, f + 1)
                if f >= 2:
                    dv.wait_ge(s_usg, f - 1)
                W3 = TOK + 1
                link(V.tensor_scalar(cv2[:, s, :], up2[:, s, 0:W3], vcol[:, 2, f:f + 1], vcol[:, 3, 44 + f:45 + f], ALU.mult, ALU.add))
                link(V.scalar_tensor_tensor(cv2[:, s, :], up2[:, s, 1:1 + W3], vcol[:, 2, 44 + f:45 + f], cv2[:, s, :], ALU.mult, ALU.add))
                V.scalar_tensor_tensor(cv2[:, s, :], up2[:, s, 2:2 + W3], vcol[:, 3, f:f + 1], cv2[:, s, :], ALU.mult, ALU.add).then_inc(s_ucv, 1)
                dv.wait_ge(s_usg, f + 1)
                dv.wait_ge(s_up, 4 * i + 2 + s + 1)
                b_ = 4 * (i % 2) + 2 + s
                V.tensor_tensor(act[:, f, 0:P], ps[:, b_, 0:P], sg2[:, s, 0:P], ALU.mult)
                V.tensor_tensor(act[:, f, P:TOK], ps[:, b_, P:TOK], sg2[:, s, P + 1:TOK + 1], ALU.mult).then_inc(s_uact, 1)
            dv.wait_ge(s_gb2c, 8)
            for q in range(2):
                dv.wait_ge(s_blk, B_DOWN + (q + 1) * (FT // DOWN_KT))
                for t in range(3):
                    for c in range(2):
                        n = 6 * q + 2 * t + c
                        cs = slice(DOWN_W * q + 512 * c, DOWN_W * q + 512 * c + 512)
                        link(V.tensor_tensor(ytmp2, ps[:, n % 8, :], gb[:, min(t, 1), cs], ALU.mult))
                        V.tensor_tensor(x[:, t, cs], x[:, t, cs], ytmp2, ALU.add).then_inc(s_dc, 1)
                        dv.wait_ge(s_dc, n + 1)
            dv.wait_ge(s_fgl, 16)
            for t in range(3):
                dv.wait_ge(s_fss, t + 1)
                inv_root(V.tensor_scalar(stat[:, 36 + t:37 + t], stat[:, 32 + t:33 + t], 1.0 / D, 1e-6, ALU.mult, ALU.add), stat[:, 36 + t:37 + t])
                V.scalar_tensor_tensor(x[:, t, :], x[:, t, :], stat[:, 36 + t:37 + t], fg, ALU.mult, ALU.mult).then_inc(s_yf, 1)


_INS = ['x_prompt', 'x_sample', 'cache_k', 'cache_v', 'state_fwd', 'state_bwd', 'c', 'c_ctx', 'norm1_g', 'norm2_g',
        'w_mod', 'b_mod', 'w_in', 'w_out', 'rpb', 'conv_w', 'conv_b', 'conv_ln_g', 'conv_ln_b', 'rwkv_w0',
        'rwkv_w_lora', 'rwkv_a0', 'rwkv_a_lora', 'rwkv_g_lora', 'rwkv_k_k', 'rwkv_k_a', 'rwkv_r_k', 'rwkv_ln_g',
        'rwkv_ln_b', 'w_up', 'ffn_conv_w', 'ffn_conv_b', 'w_down', 'final_g']
_OUTS = [("y_prompt", (1, 128, 2048)), ("y_sample", (1, 256, 2048)), ("new_cache_k", (1, 1, 128, 12, 64)),
         ("new_cache_v", (1, 1, 128, 12, 64)), ("new_state_fwd", (1, 1, 12, 64, 64)), ("new_state_bwd", (1, 1, 12, 64, 64))]


def _constants():
    import numpy as np
    j, t = np.meshgrid(np.arange(P), np.arange(P), indexing="ij")
    same = (j // CHUNK) == (t // CHUNK)
    cols = [np.eye(P)]
    for before in ((j < t), (j > t)):
        strict = same & before
        incl = same & (before | (j == t))
        cols += [strict, incl, strict, incl]
    cols.append(same)
    for d in range(2):
        for l in range(LEVELS):
            n = 2 << l
            pair = (j // (2 * n)) == (t // (2 * n))
            a, b = (j // n) % 2, (t // n) % 2
            cols.append(pair & ((a == 0) & (b == 1) if d == 0 else (a == 1) & (b == 0)))
    cols.append((j // 2) == (t // 2))
    q = np.arange(P) % GRID
    start = np.clip(q - 8, 0, GRID - 16)
    kc = np.arange(GRID)
    cols.append(np.where((kc >= start[:, None]) & (kc < start[:, None] + 16), 0.0, -1e30))
    cols.append(np.zeros((P, P)))
    cols.append(np.full((P, P), 1.0 / (BT * P)))
    return np.concatenate([np.asarray(c, np.float32) for c in cols], axis=1)


def kernel(**inputs):
    import numpy as _np
    import concourse.bacc as _bacc
    from concourse import mybir as _mybir
    from concourse.bass_utils import run_bass_kernel_spmd as _run

    nc = _bacc.Bacc("TRN2", target_bir_lowering=False, num_devices=1)
    arrays, args, outs = {}, {}, {}
    for name in _INS + ["consts"]:
        a = _constants() if name == "consts" else _np.ascontiguousarray(inputs[name])
        arrays[f"in_{name}_dram"] = a
        args[name] = nc.dram_tensor(f"in_{name}_dram", a.shape, _mybir.dt.from_np(a.dtype), kind="ExternalInput").ap()
    for name, shape in _OUTS:
        outs[name] = nc.dram_tensor(f"out_{name}_dram", shape, F32, kind="ExternalOutput").ap()
    build(nc, args, outs)
    r = _run(nc, [arrays], core_ids=[0])
    return tuple(r.results[0][f"out_{name}_dram"] for name, _ in _OUTS)
```

```python
from contextlib import ExitStack

import concourse.bass as bass
from concourse import mybir

ALU = mybir.AluOpType
ACT = mybir.ActivationFunctionType
F32 = mybir.dt.float32
F32R = mybir.dt.float32r
AX = mybir.AxisListType

P = 128
D = 2048
KT = D // P
TOK = 3 * P
HD = 64
HA = 12
HC = 12
CHUNK = 64
DFF = 11 * D // 4
FT = DFF // P
CONV_K = 31
PADC = CONV_K // 2
BT = 4
GRID = 64
BLK = 256
KP = KT // 2
PIECE = KP * BLK
RING = 4
SPLITS = 2
DECAY = 0.606531
SCALE = HD ** -0.5
LEVELS = 5

C_ID = 0
C_M4 = C_ID + P
C_BONES = C_M4 + 2 * 4 * P
C_XM = C_BONES + P
C_SAME2 = C_XM + 2 * LEVELS * P
C_COL = C_SAME2 + P
C_ZERO = C_COL + GRID
C_MEAN = C_ZERO + P
C_SEL = C_MEAN + P
C_END = C_SEL + 4

N_MOD = 6 * D // BLK
IN_BLOCKS = ([("chan", "q", 256 * j, 256, 2 * j) for j in range(3)]
             + [("chan", "k", 768 + 256 * j, 256, 2 * j) for j in range(3)]
             + [("tok", "v", 1536 + 256 * j, 256, j) for j in range(3)]
             + [b for j in range(2) for b in (("chan", "glu_b", 2816 + 256 * j, 256, 2 * j),
                                              ("chan", "glu_a", 2304 + 256 * j, 256, 2 * j))]
             + [("chan", "lora", 5632, 256, 0), ("chan", "lora", 5888, 128, 2)]
             + [("tok", "rkv", 3328 + 256 * j, 256, j) for j in range(9)])
P_IN = 2 * N_MOD
P_OUT = P_IN + 2 * len(IN_BLOCKS)
P_UP = P_OUT + 2 * (D // BLK)
P_DOWN = P_UP + 4 * (DFF // BLK)
DOWN_KT = 2
DOWN_W = PIECE // DOWN_KT

ITEMS = []
for _n, (_kind, _what, _c, _w, _j) in enumerate(IN_BLOCKS):
    for _s in range(3 if _kind == "tok" else _w // P):
        _eng = "act" if _what in ("q", "v", "rkv", "glu_b", "lora") else "dve"
        ITEMS.append((_n, _kind, _what, _j, _s, _eng))
ATT = [(t, h) for t in range(3) for h in range(HA)]
UNITS = [(0, 0, 0), (0, 1, 0), (1, 0, 0), (2, 1, 0), (2, 0, 2), (1, 1, 2)]
FINAL = {1: (0, 0), 4: (1, 2), 5: (2, 1)}
HH = HC // 2
HW = HH * HD


def evacs(eng, m):
    return sum(1 for it in ITEMS[:m] if it[5] == eng)


def build(nc, a, out):
    ctx = ExitStack()
    with ctx:
        def sb(name, cols, dt=F32, where=ctx):
            return where.enter_context(nc.sbuf_tensor(name, [P, cols], dt))

        def sem(name):
            return ctx.enter_context(nc.semaphore(name))

        def carve(t, at, *dims):
            n = 1
            for d in dims:
                n *= d
            v = t[:, at:at + n]
            if len(dims) == 2:
                v = v.rearrange("p (a b) -> p a b", a=dims[0])
            if len(dims) == 3:
                v = v.rearrange("p (a b c) -> p a b c", a=dims[0], b=dims[1])
            if len(dims) == 4:
                v = v.rearrange("p (a b c d) -> p a b c d", a=dims[0], b=dims[1], c=dims[2])
            return v, at + n

        consts = sb("consts", C_END)
        vcol_t = sb("vcol", 4 * P)
        vcol = vcol_t[:, :].rearrange("p (g c) -> p g c", g=4)
        c4_t = sb("c4", 4 * KT, F32R)
        modcol_t = sb("modcol", 2 * 96)
        modcol = modcol_t[:, :].rearrange("p (t g) -> p t g", g=2)
        scol_t = sb("scol", 2 * KT)
        scol = scol_t[:, :].rearrange("p (t g) -> p t g", g=2)
        stat = sb("stat", 64)
        ring = sb("ring", RING * PIECE)
        NA = 52900 - C_END - 4 * P - 4 * KT - 192 - 2 * KT - 64 - RING * PIECE - 2 * SPLITS * PIECE - 2 * KT * TOK - 2400
        arena = sb("arena", NA)
        with ExitStack() as early:
            wsp = sb("w_split", 2 * SPLITS * PIECE, F32R, early)
            hsp = sb("h_split", 2 * KT * TOK, F32R, early)
            asp = sb("a_split", 2400, F32R, early)
        wmix = sb("w_mix", 2 * SPLITS * PIECE)
        hf = sb("h_f32", 2 * KT * TOK)
        ubuf = sb("u_buf", 2400)
        hh = hsp[:, 0:KT * TOK].rearrange("p (k n) -> p k n", k=KT)
        hl = hsp[:, KT * TOK:].rearrange("p (k n) -> p k n", k=KT)
        yh, yl = hh, hl
        wh = [wsp[:, PIECE * i:PIECE * i + PIECE] for i in range(SPLITS)]
        wl = [wsp[:, PIECE * (SPLITS + i):PIECE * (SPLITS + i + 1)] for i in range(SPLITS)]
        ah = [asp[:, TOK * i:TOK * i + TOK] for i in range(3)]
        al = [asp[:, TOK * (3 + i):TOK * (4 + i)] for i in range(3)]
        ps_t = ctx.enter_context(nc.psum_tensor("ps", [P, 8 * 512], F32))
        ps = ps_t[:, :].rearrange("p (b n) -> p b n", b=8)

        ident = consts[:, C_ID:C_ID + P]

        x, _ = carve(arena, 0, 3, D)
        xT, o = carve(arena, 0, KT, TOK)
        xn, o = carve(arena, o, 3, D)
        vrow, o = carve(arena, o, 5, P)
        csig, o = carve(arena, o, 2 * KT)
        cT, o = carve(arena, o, 2 * KT)
        modrow, o = carve(arena, o, 2, BLK)
        junk, o = carve(arena, o, D)
        assert o <= NA
        qkT, o = carve(arena, 0, 12, TOK)
        v_tok, o = carve(arena, o, 3, 768)
        upad, _ = carve(arena, o, BT, PADC * 3 + TOK)
        CW = TOK + PADC
        csq, _ = carve(arena, o, BT, CW)
        o += BT * (PADC * 3 + TOK)
        crstd, o = carve(arena, o, CW)
        knew, o = carve(arena, o, 768)
        O_RKV = NA - 3 * 2304 - 3 * TOK
        assert o <= O_RKV, (o, O_RKV)
        rkv, o = carve(arena, O_RKV, 3, 2304)
        lora, o = carve(arena, o, 3, TOK)
        cbuf, o = carve(ubuf, 0, BT, CW)
        sgt, o = carve(ubuf, o, 2, TOK)
        assert o <= 2400
        Bm, o = carve(ring, 0, HA, 6, GRID)
        ckT, o = carve(ring, o, 6, P)
        cv, o = carve(ring, o, 768)
        ck, o = carve(ring, o, 768)
        assert o <= RING * PIECE
        ss, o = carve(wmix, 0, 3, TOK)
        PT, o = carve(wmix, o, 2, TOK)
        Am, o = carve(ring, 0, HH, 4, P)
        Nm, o = carve(ring, o, HH, P)
        Tm, o = carve(ring, o, HH, P)
        TTm, o = carve(ring, o, HH, P)
        Xm, o = carve(ring, o, HH, P)
        ZA, o = carve(ring, o, HH, 2, HD)
        ZU, o = carve(ring, o, HH, 2, HD)
        QT, o = carve(ring, o, 3, P)
        assert o <= RING * PIECE
        zrT, o = carve(wmix, 0, 3, 2, P)
        bT, o = carve(wmix, o, 3, P)
        kT, o = carve(wmix, o, 3, P)
        MT, o = carve(wmix, o, 2, 3, HD)
        Sh, o = carve(wmix, o, 2, 3, HD)
        dP, o = carve(wmix, o, 2, 3, HD)
        S, o = carve(wmix, o, 2 * 5, 3, HD)
        (btil, o), (ktil, _), (rtil, _), (tmp, _) = (carve(wmix, o + HW * i, HW) for i in range(4))
        o += 3 * HW
        (tW, _), (tA, _), (eE, _), (eP, _), (eN, _) = (carve(wmix, o + HW * i, HW) for i in range(5))
        o += 5 * HW
        assert o <= 2 * SPLITS * PIECE
        par, o = carve(arena, 0, 12, HW)
        Oacc, o = carve(arena, o, 2, HW)
        bsum, o = carve(arena, o, 2, HH)
        st6, o = carve(arena, o, 4, HH)
        (eR, _), (eT, _), (kkn, _), (b1, _), (kd, _), (Bbar, _), (Kbar, _), (sq, _) = (
            carve(arena, o + HW * i, HW) for i in range(8))
        assert o + 8 * HW <= O_RKV
        sraw, sraw2 = eE, eP
        sout = eN
        x2, o = carve(arena, 0, 3, D)
        gb, o = carve(arena, o, 2, D)
        xn2, o = carve(arena, o, 3, D)
        assert o <= NA
        ytmp, o = carve(ubuf, 0, 2, BLK)
        mtmp, o = carve(ubuf, o, 2, 4, P)
        act, o = carve(arena, 0, FT, TOK)
        assert o <= NA
        UPW = TOK + 3
        up2, o = carve(ubuf, 0, 2, UPW)
        cv2, o = carve(ubuf, o, 2, TOK + 1)
        sg2, o = carve(ubuf, o, 2, TOK + 1)
        assert o <= 2400
        x3, o = carve(hf, 0, 3, D)
        gb2, o = carve(hf, o, 2, D)
        fg, o = carve(hf, o, D)
        ytmp2, _ = carve(ring, 0, 2, 512)
        ytmp1, _ = carve(arena, FT * TOK, 2, 256)
        junk2, _ = carve(arena, 0, D)

        X_dram = nc.dram_tensor("x_mid", [3, P, D], F32, kind="Internal").ap()
        E_dram = nc.dram_tensor("rpb_padded", [HA, 7, P], F32, kind="Internal").ap()
        EL = HA * 7 * P
        R_dram = nc.dram_tensor("rpb_rows", [GRID, EL], F32, kind="Internal").ap()

        s_const, s_x, s_vrow, s_lnrow = sem("s_const"), sem("s_x"), sem("s_vrow"), sem("s_lnrow")
        s_w = [sem(f"s_w{i}") for i in range(RING)]
        s_hi, s_lo = sem("s_hi"), sem("s_lo")
        s_blk, s_kd = sem("s_blk"), sem("s_kd")
        s_ah, s_al, s_c4, s_hm, s_hh, s_xs, s_x3 = (sem(n) for n in ("s_ah", "s_al", "s_c4", "s_hm", "s_hh", "s_xs", "s_x3"))
        s_cs, s_cyh, s_pvh, s_fh, s_hm2, s_hh2 = (sem(n) for n in ("s_cs", "s_cyh", "s_pvh", "s_fh", "s_hm2", "s_hh2"))
        s_vt, s_vc, s_ct = sem("s_vt"), sem("s_vc"), sem("s_ct")
        s_csig = sem("s_csig")
        s_ssq, s_rstd, s_xn, s_xt, s_xc = sem("s_ssq"), sem("s_rstd"), sem("s_xn"), sem("s_xt"), sem("s_xc")
        s_mrow, s_mcT, s_mcol, s_h = sem("s_mrow"), sem("s_mcT"), sem("s_mcol"), sem("s_h")
        s_eact, s_edve = sem("s_eact"), sem("s_edve")
        s_d, s_a = sem("s_d"), sem("s_a")
        s_var, s_root = sem("s_var"), sem("s_root")
        s_pad = sem("s_pad")
        s_cbuf, s_cmean, s_ccen, s_csq, s_cvar, s_cn, s_cy = (sem(n) for n in (
            "s_cbuf", "s_cmean", "s_ccen", "s_csq", "s_cvar", "s_cn", "s_cy"))
        s_E0, s_E1, s_Bm, s_Bmask = sem("s_E0"), sem("s_E1"), sem("s_Bm"), sem("s_Bmask")
        s_cache, s_ckt, s_ckc, s_knt, s_knc, s_out = (sem(n) for n in (
            "s_cache", "s_ckt", "s_ckc", "s_knt", "s_knc", "s_out"))
        s_sc, s_sm, s_ex, s_nr, s_pt, s_ptc, s_pv, s_pvc = (sem(n) for n in (
            "s_sc", "s_sm", "s_ex", "s_nr", "s_pt", "s_ptc", "s_pv", "s_pvc"))
        s_par, s_S0, s_sraw, s_sT = sem("s_par"), sem("s_S0"), sem("s_sraw"), sem("s_sT")
        (s_rlora, s_rpre, s_rsig, s_rcum, s_rexp, s_rtil, s_rbar, s_rtr, s_rtc, s_rA, s_rAm, s_rN, s_rNc, s_rT0,
         s_rAV, s_rAVc, s_rX, s_rXm, s_rTp, s_rTu, s_rZU, s_rZUc, s_rQM, s_rQMc, s_rSp, s_rS, s_rO, s_rdone,
         s_fg, s_fy, s_fT, s_fc, s_stT, s_stc, s_stout) = (sem(n) for n in (
             "s_rlora", "s_rpre", "s_rsig", "s_rcum", "s_rexp", "s_rtil", "s_rbar", "s_rtr", "s_rtc", "s_rA",
             "s_rAm", "s_rN", "s_rNc", "s_rT0", "s_rAV", "s_rAVc", "s_rX", "s_rXm", "s_rTp", "s_rTu", "s_rZU",
             "s_rZUc", "s_rQM", "s_rQMc", "s_rSp", "s_rS", "s_rO", "s_rdone", "s_fg", "s_fy", "s_fT", "s_fc",
             "s_stT", "s_stc", "s_stout"))
        s_x2, s_gbp, s_gbc, s_oc = sem("s_x2"), sem("s_gbp"), sem("s_gbc"), sem("s_oc")
        s_ssq2, s_xn2, s_xt2, s_h2 = sem("s_ssq2"), sem("s_xn2"), sem("s_xt2"), sem("s_h2")
        s_gb2p, s_gb2c = sem("s_gb2p"), sem("s_gb2c")
        s_uc, s_ucv, s_usg, s_uact = sem("s_uc"), sem("s_ucv"), sem("s_usg"), sem("s_uact")
        s_dc, s_fgl, s_fss, s_yf = sem("s_dc"), sem("s_fgl"), sem("s_fss"), sem("s_yf")

        def toks(t):
            return slice(P * t, P * t + P)

        def half(p):
            return slice(64 * p, 64 * p + 64)

        def slot_of(n):
            return ring[:, (n % RING) * PIECE:(n % RING + 1) * PIECE]

        def width(n):
            full = P_IN <= n < P_OUT
            return KP * IN_BLOCKS[(n - P_IN) // 2][3] if full else PIECE

        def used(eng, n):
            if n < P_DOWN:
                eng.wait_ge(s_blk, n + 1)
            else:
                eng.wait_ge(s_kd, DOWN_KT * (n - P_DOWN + 1))

        block = ctx.enter_context(nc.Block())
        LOADS_PER_HALF = 12

        @block.sync
        def _(sp):
            def load(n, src, k):
                if n >= RING:
                    sp.wait_ge(s_lo, n - RING + 1)
                sp.dma_start(slot_of(n)[:, 0:width(n)].rearrange("p (k c) -> p k c", k=k), src).then_inc(s_w[n % RING], 16)

            def load_block(n, w, c0, cols):
                for p in range(2):
                    src = w[KP * P * p:KP * P * (p + 1), c0:c0 + cols]
                    load(n + p, src.rearrange("(k p) c -> p k c", p=P), KP)

            sp.dma_start(consts[:, :], a["consts"]).then_inc(s_const, 16)
            for t, src in ((0, a["x_prompt"][0]), (1, a["x_sample"][0, 0:P]), (2, a["x_sample"][0, P:2 * P])):
                sp.dma_start(x[:, t, :], src).then_inc(s_x, 16)
            for i in range(N_MOD):
                load_block(2 * i, a["w_mod"][0], BLK * i, BLK)
            for j, (_, _, c0, w, _) in enumerate(IN_BLOCKS):
                load_block(P_IN + 2 * j, a["w_in"][0], c0, w)
            sp.wait_ge(s_eact, evacs("act", len(ITEMS)))
            sp.dma_start(out["new_cache_v"][0, 0].rearrange("t h d -> t (h d)"), v_tok[:, 0, :]).then_inc(s_out, 16)
            sp.wait_ge(s_knc, 2)
            sp.dma_start(out["new_cache_k"][0, 0].rearrange("t h d -> t (h d)"), knew).then_inc(s_out, 16)
            for hf in range(2):
                cs = slice(HW * hf, HW * hf + HW)
                if hf == 0:
                    sp.wait_ge(s_pvc, len(ATT) // 2)
                    sp.wait_ge(s_out, 32)
                else:
                    sp.wait_ge(s_fy, 3)
                    sp.wait_ge(s_fg, 3)
                for i, src in enumerate((a["rwkv_w0"][0, 0:1, cs], a["rwkv_w0"][0, 1:2, cs],
                                         a["rwkv_a0"][0, 0:1, cs], a["rwkv_a0"][0, 1:2, cs],
                                         a["rwkv_k_k"][0:1, cs], a["rwkv_k_a"][0:1, cs],
                                         a["rwkv_r_k"].rearrange("l h d -> l (h d)")[0:1, cs],
                                         a["rwkv_ln_g"][0:1, cs], a["rwkv_ln_b"][0:1, cs])):
                    sp.dma_start(par[:, i, :], src.broadcast_to([P, HW])).then_inc(s_par, 16)
                sp.dma_start(par[:, 9, :], a["rwkv_w_lora"][0][:, :, cs].rearrange("d r c -> (d r) c")).then_inc(s_par, 16)
                sp.dma_start(par[:, 10, :], a["rwkv_a_lora"][0][:, :, cs].rearrange("d r c -> (d r) c")).then_inc(s_par, 16)
                sp.dma_start(par[:, 11, :], a["rwkv_g_lora"][0][:, cs]).then_inc(s_par, 16)
                for d in range(2):
                    sp.wait_ge(s_stc, 2 * hf + d + 1)
                    dst = out["new_state_fwd" if d == 0 else "new_state_bwd"][0, 0, HH * hf:HH * hf + HH]
                    sp.dma_start(dst.rearrange("h v k -> v h k"),
                                 sout[0:HD, :].rearrange("p (h k) -> p h k", h=HH)).then_inc(s_stout, 16)
                sp.wait_ge(s_stout, 32 * hf + 32)
                for d, dst in enumerate((sraw, sraw2)):
                    src = a["state_fwd" if d == 0 else "state_bwd"][0, 0, HH * hf:HH * hf + HH]
                    sp.dma_start(dst[0:HD, :].rearrange("p (h k) -> p h k", h=HH),
                                 src.rearrange("h v k -> v h k")).then_inc(s_sraw, 16)
            sp.wait_ge(s_fc, 6)
            for t, src in ((0, a["x_prompt"][0]), (1, a["x_sample"][0, 0:P]), (2, a["x_sample"][0, P:2 * P])):
                sp.dma_start(x2[:, t, :], src).then_inc(s_x2, 16)
            for j in range(D // BLK):
                load_block(P_OUT + 2 * j, a["w_out"][0], BLK * j, BLK)
            for i in range(DFF // BLK):
                load_block(P_UP + 4 * i, a["w_up"][0], BLK * i, BLK)
                if i == 0:
                    sp.wait_ge(s_oc, 3 * (D // BLK))
                    sp.dma_start(X_dram.rearrange("t p c -> p t c"), x2).then_inc(s_xs, 16)
                load_block(P_UP + 4 * i + 2, a["w_up"][0], DFF + BLK * i, BLK)
            for q in range(2):
                for g in range(FT // DOWN_KT):
                    n = P_DOWN + q * (FT // DOWN_KT) + g
                    src = a["w_down"][0][DOWN_KT * P * g:DOWN_KT * P * (g + 1), DOWN_W * q:DOWN_W * (q + 1)]
                    load(n, src.rearrange("(k p) c -> p k c", p=P), DOWN_KT)
                    if q == 0 and g == RING:
                        used(sp, P_DOWN - 1)
                        sp.wait_ge(s_xs, 16)
                        sp.dma_start(x3, X_dram.rearrange("t p c -> p t c")).then_inc(s_x3, 16)
                        sp.dma_start(fg, a["final_g"].rearrange("(o c) -> o c", o=1).broadcast_to([P, D])).then_inc(s_fgl, 16)
            for t in range(3):
                sp.wait_ge(s_yf, t + 1)
                dst = out["y_prompt"][0] if t == 0 else out["y_sample"][0, P * (t - 1):P * t]
                sp.dma_start(dst, x3[:, t, :]).then_inc(s_out, 16)
            sp.wait_ge(s_out, 16 * 5)
            sp.wait_ge(s_stout, 16 * 4)

        @block.gpsimd
        def _(pool):
            pool.dma_start(vrow[0:KT, 0, :], a["c_ctx"].rearrange("(k p) -> k p", p=P)).then_inc(s_vrow, 16)
            pool.dma_start(vrow[KT:2 * KT, 0, :], a["c"][0].rearrange("(k p) -> k p", p=P)).then_inc(s_vrow, 16)
            pool.dma_start(vrow[0:16, 1, :], a["norm1_g"][0].rearrange("(k p) -> k p", p=P)).then_inc(s_vrow, 16)
            pool.dma_start(vrow[16:32, 1, :], a["norm2_g"][0].rearrange("(k p) -> k p", p=P)).then_inc(s_vrow, 16)
            pool.dma_start(vrow[32:128, 1, :], a["b_mod"][0].rearrange("(k p) -> k p", p=P)).then_inc(s_vrow, 16)
            pool.dma_start(vrow[0:124, 2, :], a["conv_w"][0].rearrange("j (k p) -> (j k) p", p=P)).then_inc(s_vrow, 16)
            pool.dma_start(vrow[0:88, 3, :], a["ffn_conv_w"][0, 0:2].rearrange("j (k p) -> (j k) p", p=P)).then_inc(s_vrow, 16)
            pool.dma_start(vrow[88:92, 3, :], a["conv_b"][0].rearrange("(k p) -> k p", p=P)).then_inc(s_vrow, 16)
            pool.dma_start(vrow[92:96, 3, :], a["conv_ln_g"][0].rearrange("(k p) -> k p", p=P)).then_inc(s_vrow, 16)
            pool.dma_start(vrow[96:100, 3, :], a["conv_ln_b"][0].rearrange("(k p) -> k p", p=P)).then_inc(s_vrow, 16)
            pool.dma_start(vrow[0:44, 4, :], a["ffn_conv_w"][0, 2].rearrange("(k p) -> k p", p=P)).then_inc(s_vrow, 16)
            pool.dma_start(vrow[44:88, 4, :], a["ffn_conv_b"][0].rearrange("(k p) -> k p", p=P)).then_inc(s_vrow, 16)
            pool.wait_ge(s_const, 16)
            pool.dma_start(E_dram.rearrange("h r c -> (h r) c"),
                           consts[0:HA * 7, C_ZERO:C_ZERO + P]).then_inc(s_E0, 16)
            pool.wait_ge(s_E0, 16)
            pool.dma_start(E_dram[:, :, 48:79], a["rpb"][0][:, 4:11, :]).then_inc(s_E1, 16)
            pool.wait_ge(s_E1, 16)
            pool.dma_start(R_dram, bass.AP(E_dram.tensor, 0, [[0, GRID], [1, EL]])).then_inc(s_E1, 16)
            pool.wait_ge(s_E1, 32)
            pool.wait_ge(s_blk, P_OUT)
            pool.dma_start(cv, a["cache_v"][0, 0].rearrange("t h d -> t (h d)")).then_inc(s_cache, 16)
            pool.dma_start(ck, a["cache_k"][0, 0].rearrange("t h d -> t (h d)")).then_inc(s_cache, 16)
            for i in range(2):
                for h in range(HA):
                    src = bass.AP(R_dram.tensor, h * 7 * P + (1 - i) * P + 63, [[EL - 1, GRID], [P, 6], [1, GRID]])
                    pool.dma_start(Bm[half(i), h], src).then_inc(s_Bm, 16)
            pool.wait_ge(s_cache, 32)

        @block.tensor
        def _(pe):
            mm, tr = nc.tensor.matmul, nc.tensor.transpose

            def three(o_, lh, ll, rh, rl, start, stop):
                mm(o_, lh, rh, start=start, stop=False)
                mm(o_, lh, rl, start=False, stop=False)
                return mm(o_, ll, rh, start=False, stop=stop)

            def parts(n, k):
                w = width(n)
                return (wh[n % SPLITS][:, 0:w].rearrange("p (k c) -> p k c", k=k),
                        wl[n % SPLITS][:, 0:w].rearrange("p (k c) -> p k c", k=k))

            pe.wait_ge(s_const, 16)
            pe.wait_ge(s_vrow, 16 * 12)
            for g, rows in enumerate((2 * KT, 128, 124, 100, 88)):
                tr(ps[:, g, 0:rows], vrow[0:rows, g, :], ident[0:rows, 0:rows]).then_inc(s_vt, 1)
            for t in range(3):
                pe.wait_ge(s_xn, t + 1)
                for g in range(4):
                    n = 4 * t + g
                    bank = 5 + n % 3
                    if n >= 3:
                        pe.wait_ge(s_xc, n - 2)
                    for j in range(4):
                        last = tr(ps[:, bank, toks(j)], xn[:, t, toks(4 * g + j)], ident)
                    last.then_inc(s_xt, 1)

            def mod_block(i):
                if i >= 2:
                    pe.wait_ge(s_mrow, i - 1)
                for p in range(2):
                    n = 2 * i + p
                    pe.wait_ge(s_lo, n + 1)
                    w_hi, w_lo = parts(n, KP)
                    for k in range(KP):
                        kk_ = KP * p + k
                        c4 = c4_t[:, 4 * kk_:4 * kk_ + 4]
                        mm(ps[0:4, i % 2, 0:BLK], c4, w_hi[:, k, :], start=(kk_ == 0), stop=False)
                        last = mm(ps[0:4, i % 2, 0:BLK], c4, w_lo[:, k, :], start=False, stop=(kk_ == KT - 1))
                    last.then_inc(s_blk, 1)

            def mod_cols(i):
                pe.wait_ge(s_mrow, i + 1)
                if i >= 2:
                    pe.wait_ge(s_mcol, i - 1)
                for j in range(2):
                    last = mm(ps[:, 2 + i % 2, 2 * j:2 * j + 2], modrow[0:4, i % 2, toks(j)], consts[0:4, C_SEL:C_SEL + 2], start=True, stop=True)
                last.then_inc(s_mcT, 1)

            pe.wait_ge(s_vc, 4)
            pe.wait_ge(s_c4, 2)
            for i in range(N_MOD):
                mod_block(i)
                if i:
                    mod_cols(i - 1)
            mod_cols(N_MOD - 1)

            pe.wait_ge(s_h, 1)
            m = 0
            for j, (kind, what, c0, w, _) in enumerate(IN_BLOCKS):
                tiles = 3 if kind == "tok" else w // P
                for s in range(tiles):
                    if m + s >= 8:
                        e = ITEMS[m + s - 8][5]
                        pe.wait_ge(s_eact if e == "act" else s_edve, evacs(e, m + s - 7))
                for p in range(2):
                    n = P_IN + 2 * j + p
                    pe.wait_ge(s_lo, n + 1)
                    w_hi, w_lo = parts(n, KP)
                    for s in range(tiles):
                        for k in range(KP):
                            q = KP * p + k
                            at = dict(start=(q == 0), stop=(q == KT - 1))
                            if kind == "tok":
                                last = three(ps[:, (m + s) % 8, 0:w], hh[:, q, toks(s)], hl[:, q, toks(s)],
                                             w_hi[:, k, :], w_lo[:, k, :], **at)
                            else:
                                last = three(ps[:, (m + s) % 8, 0:TOK], w_hi[:, k, toks(s)], w_lo[:, k, toks(s)],
                                             hh[:, q, :], hl[:, q, :], **at)
                    last.then_inc(s_blk, 1)
                m += tiles

            pe.wait_ge(s_eact, evacs("act", len(ITEMS)))
            pe.wait_ge(s_edve, evacs("dve", len(ITEMS)))
            pe.wait_ge(s_cbuf, 1)
            for t in range(BT):
                last = mm(ps[:, 0, 0:CW], consts[:, C_MEAN:C_MEAN + P], cbuf[:, t, :], start=(t == 0), stop=(t == BT - 1))
            last.then_inc(s_cmean, 1)
            pe.wait_ge(s_csq, 1)
            for t in range(BT):
                last = mm(ps[:, 1, 0:CW], consts[:, C_MEAN:C_MEAN + P], csq[:, t, :], start=(t == 0), stop=(t == BT - 1))
            last.then_inc(s_cvar, 1)

            pe.wait_ge(s_cache, 32)
            for i in range(6):
                last = tr(ps[:, 6 + i // 3, toks(i % 3)], ck[:, toks(i)], ident)
            last.then_inc(s_ckt, 1)
            for i in range(6):
                last = tr(ps[:, 4 + i // 3, toks(i % 3)], qkT[:, 6 + i, 0:P], ident)
            last.then_inc(s_knt, 1)
            pe.wait_ge(s_cn, 1)
            pe.wait_ge(s_cyh, 8)
            pe.wait_ge(s_ckc, 2)
            pe.wait_ge(s_knc, 2)

            def scores(u):
                t, h = ATT[u]
                r = half(h % 2)
                if u >= 2:
                    pe.wait_ge(s_sm, u - 1)
                bank = u % 2
                q = qkT[r, h // 2, toks(t)]
                if t == 0:
                    last = mm(ps[:, bank, 0:P], q, qkT[r, 6 + h // 2, 0:P], start=True, stop=True)
                else:
                    mm(ps[:, bank, 0:2 * P], q, qkT[r, 6 + h // 2, P:TOK], start=True, stop=True)
                    last = mm(ps[:, bank, 2 * P:TOK], q, ckT[r, h // 2, :], start=True, stop=True)
                last.then_inc(s_sc, 1)

            def turn(u):
                t, h = ATT[u]
                pe.wait_ge(s_nr, u + 1)
                if u >= 2:
                    pe.wait_ge(s_ptc, u - 1)
                for k in range(1 if t == 0 else 3):
                    last = tr(ps[:, 2 + u % 2, toks(k)], ss[:, u % 3, toks(k)], ident)
                last.then_inc(s_pt, 1)

            def pv(u):
                t, h = ATT[u]
                pe.wait_ge(s_ptc, u + 1)
                if u >= 4 and h % 2 == 0:
                    pe.wait_ge(s_pvc, u // 2 - 1)
                o_ = ps[half(h % 2), 4 + (u // 2) % 2, 0:P]
                keys = [v_tok[:, 0, :]] if t == 0 else [v_tok[:, 1, :], v_tok[:, 2, :], cv]
                for k, vv in enumerate(keys):
                    last = mm(o_, vv[:, HD * h:HD * h + HD], PT[:, u % 2, toks(k)], start=(k == 0), stop=(k == len(keys) - 1))
                last.then_inc(s_pv, 1)

            for u in range(len(ATT) + 3):
                if u < len(ATT):
                    scores(u)
                if 0 <= u - 2 < len(ATT):
                    turn(u - 2)
                if 0 <= u - 3:
                    pv(u - 3)
            pe.wait_ge(s_pvc, len(ATT) // 2)

            for u in range(12):
                hf, u6 = u // 6, u % 6
                t, d, s0 = UNITS[u6]
                tk = toks(t)
                m4 = consts[:, C_M4 + 512 * d:C_M4 + 512 * d + 512]
                m4o = consts[:, C_M4 + 512 * (1 - d):C_M4 + 512 * (1 - d) + 512]
                v = rkv[:, t, 1536 + HW * hf:1536 + HW * hf + HW]
                if u6 == 0:
                    pe.wait_ge(s_par, 16 * LOADS_PER_HALF * (hf + 1))
                if u6 == 2:
                    pe.wait_ge(s_sraw, 32 * (hf + 1))
                    for dd, raw in enumerate((sraw, sraw2)):
                        for i in range(3):
                            last = tr(ps[:, 7, (3 * dd + i) * HD:(3 * dd + i + 1) * HD], raw[0:HD, toks(i)], ident[0:HD, 0:HD])
                    last.then_inc(s_sT, 1)
                    pe.wait_ge(s_S0, 2 * hf + 2)
                if u:
                    pe.wait_ge(s_rdone, u)
                mm(ps[:, 0, 0:HW], lora[half(d), 0, tk], par[half(d), 9, :], start=True, stop=True)
                mm(ps[:, 1, 0:HW], lora[half(d), 1, tk], par[half(d), 10, :], start=True, stop=True).then_inc(s_rlora, 1)
                pe.wait_ge(s_rsig, u + 1)
                mm(ps[:, 2, 0:HW], m4[:, P:2 * P], tW, start=True, stop=True)
                mm(ps[:, 3, 0:HW], m4[:, 0:P], tW, start=True, stop=True)
                mm(ps[:, 4, 0:HW], m4o[:, 0:P], tW, start=True, stop=True)
                mm(ps[:, 5, 0:HW], consts[:, C_BONES:C_BONES + P], tW, start=True, stop=True).then_inc(s_rcum, 1)
                pe.wait_ge(s_rtil, u + 1)
                for i in range(3):
                    tr(ps[:, 0, toks(i)], tmp[:, toks(i)], ident)
                for i in range(3):
                    tr(ps[:, 1, toks(i)], rtil[:, toks(i)], ident)
                for i in range(3):
                    tr(ps[:, 4, toks(i)], btil[:, toks(i)], ident)
                for i in range(3):
                    last = tr(ps[:, 5, toks(i)], ktil[:, toks(i)], ident)
                last.then_inc(s_rtr, 1)
                pe.wait_ge(s_rtc, u + 1)
                for h in range(HH):
                    r, i = half(h % 2), h // 2
                    if h >= 4:
                        pe.wait_ge(s_rAm, HH * u + h - 3)
                    zr = zrT[r, i, :, :].rearrange("p a b -> p (a b)")
                    mm(ps[:, h % 4, 0:2 * P], bT[r, i, :], zr, start=True, stop=True)
                    mm(ps[:, h % 4, 2 * P:4 * P], kT[r, i, :], zr, start=True, stop=True).then_inc(s_rA, 1)
                for h in range(HH):
                    pe.wait_ge(s_rAm, HH * u + h + 1)
                    last = tr(ps[:, 4 + h // 3, toks(h % 3)], Am[:, h, 0, :], ident)
                last.then_inc(s_rN, 1)
                for h in range(HH):
                    last = mm(ps[:, 6, HD * h:HD * h + HD], Am[:, h, 2, :], v[:, HD * h:HD * h + HD], start=True, stop=True)
                last.then_inc(s_rAV, 1)
                for l in range(LEVELS):
                    for g in range(2):
                        if l == 0 and g == 0:
                            pe.wait_ge(s_rT0, u + 1)
                        if l:
                            pe.wait_ge(s_rTu, 2 * LEVELS * u + 2 * (l - 1) + g + 1)
                        for h in range(3 * g, 3 * g + 3):
                            last = mm(ps[:, g, toks(h % 3)], Nm[:, h, :], TTm[:, h, :], start=True, stop=True)
                        last.then_inc(s_rX, 1)
                    for g in range(2):
                        pe.wait_ge(s_rXm, 2 * LEVELS * u + 2 * l + g + 1)
                        for h in range(3 * g, 3 * g + 3):
                            mm(ps[:, 2 + g, toks(h % 3)], Xm[:, h, :], Tm[:, h, :], start=True, stop=True)
                            last = mm(ps[:, 4 + g, toks(h % 3)], Tm[:, h, :], Xm[:, h, :], start=True, stop=True)
                        last.then_inc(s_rTp, 1)
                pe.wait_ge(s_rTu, 2 * LEVELS * (u + 1))
                pe.wait_ge(s_rAVc, u + 1)
                for h in range(HH):
                    last = mm(ps[:, h // 3, toks(h % 3)], TTm[:, h, :], ZA[:, h, :, :].rearrange("p a b -> p (a b)"), start=True, stop=True)
                last.then_inc(s_rZU, 1)
                pe.wait_ge(s_rZUc, u + 1)
                pe.wait_ge(s_rbar, u + 1)
                for h in range(HH):
                    r, i = half(h % 2), h // 2
                    mm(ps[r, 2, toks(i)], ZU[:, h, 0, :], Am[:, h, 1, :], start=True, stop=True)
                for p in range(2):
                    c = half(p)
                    for h in range(HH):
                        r, i = half(h % 2), h // 2
                        hs = slice(HD * h, HD * h + HD)
                        mm(ps[r, 3 + p, HD * i:HD * i + HD], ZU[c, h, 0, :], Bbar[c, hs], start=True, stop=True)
                        mm(ps[r, 3 + p, 192 + HD * i:192 + HD * i + HD], Bbar[c, hs], ZU[c, h, 1, :], start=True, stop=False)
                        last = mm(ps[r, 3 + p, 192 + HD * i:192 + HD * i + HD], Kbar[c, hs], v[c, hs], start=False, stop=True)
                last.then_inc(s_rQM, 1)
                pe.wait_ge(s_rQMc, u + 1)
                for s in range(2):
                    c = s if d == 0 else 1 - s
                    if s:
                        pe.wait_ge(s_rS, 2 * u + 1)
                    for h in range(HH):
                        r, i = half(h % 2), h // 2
                        last = mm(ps[r, 5 + h % 2, HD * i:HD * i + HD], MT[r, c, i, :], S[r, 5 * d + s0 + s, i, :], start=True, stop=True)
                    last.then_inc(s_rSp, 1)
                for h in range(HH):
                    r, i = half(h % 2), h // 2
                    o_ = ps[:, h % 2, HD * i:HD * i + HD]
                    mm(o_, Am[:, h, 1, :], ZU[:, h, 1, :], start=True, stop=False)
                    for c in range(2):
                        s = c if d == 0 else 1 - c
                        mm(ps[half(c), h % 2, HD * i:HD * i + HD], QT[r, i, half(c)], S[r, 5 * d + s0 + s, i, :],
                           start=False, stop=False)
                    last = mm(o_, Am[:, h, 3, :], v[:, HD * h:HD * h + HD], start=False, stop=True)
                last.then_inc(s_rO, 1)
                if u6 < 2:
                    pe.wait_ge(s_rS, 2 * u + 2)
                    if u6 == 1:
                        pe.wait_ge(s_stc, 2 * hf + 1)
                    for i in range(3):
                        last = tr(ps[0:HD, 7, toks(i)], S[:, 5 * d + 2, i, :], ident)
                    last.then_inc(s_stT, 1)
                if u6 in FINAL:
                    w_, t_ = FINAL[u6]
                    f = 3 * hf + w_
                    if u6 == 1:
                        pe.wait_ge(s_stc, 2 * hf + 2)
                    mm(ps[:, 7, 0:HW], lora[:, 2, toks(t_)], par[:, 11, :], start=True, stop=True).then_inc(s_fg, 1)
                    pe.wait_ge(s_fy, f + 1)
                    for i in range(3):
                        last = tr(ps[:, 6, toks(i)], Oacc[:, w_ % 2 if w_ < 2 else 0, toks(i)], ident)
                    last.then_inc(s_fT, 1)
                    pe.wait_ge(s_fc, f + 1)

            def gate_rows(col0, ready, read):
                for n in range(8):
                    g, q = n // 4, n % 4
                    if n >= 2:
                        pe.wait_ge(read, n - 1)
                    for j in range(4):
                        col = modcol[:, col0 + 4 * q + j, g:g + 1].broadcast_to([P, P])
                        last = mm(ps[:, 6 + n % 2, toks(j)], col, ident, start=True, stop=True)
                    last.then_inc(ready, 1)

            gate_rows(2 * KT, s_gbp, s_gbc)
            for j in range(D // BLK):
                for p in range(2):
                    n = P_OUT + 2 * j + p
                    pe.wait_ge(s_lo, n + 1)
                    w_hi, w_lo = parts(n, KP)
                    for t in range(3):
                        if j >= 2 and p == 0:
                            pe.wait_ge(s_oc, 3 * (j - 2) + t + 1)
                        for k in range(KP):
                            q = KP * p + k
                            last = three(ps[:, 3 * (j % 2) + t, 0:BLK], yh[:, q, toks(t)], yl[:, q, toks(t)],
                                         w_hi[:, k, :], w_lo[:, k, :], start=(q == 0), stop=(q == KT - 1))
                    last.then_inc(s_blk, 1)
            pe.wait_ge(s_oc, 3 * (D // BLK))
            for t in range(3):
                pe.wait_ge(s_xn2, t + 1)
                for g in range(4):
                    n = 4 * t + g
                    if n >= 4:
                        pe.wait_ge(s_hm2, n - 3)
                    for j in range(4):
                        last = tr(ps[:, n % 4, toks(j)], xn2[:, t, toks(4 * g + j)], ident)
                    last.then_inc(s_xt2, 1)
            pe.wait_ge(s_h2, 12)
            for i in range(DFF // BLK):
                for w in range(2):
                    if i >= 2:
                        pe.wait_ge(s_uc if w == 0 else s_uact, 2 * (i - 1))
                    for p in range(2):
                        n = P_UP + 4 * i + 2 * w + p
                        pe.wait_ge(s_lo, n + 1)
                        w_hi, w_lo = parts(n, KP)
                        for s in range(2):
                            for k in range(KP):
                                q = KP * p + k
                                last = three(ps[:, 4 * (i % 2) + 2 * w + s, 0:TOK], w_hi[:, k, toks(s)], w_lo[:, k, toks(s)],
                                             hh[:, q, :], hl[:, q, :], start=(q == 0), stop=(q == KT - 1))
                        last.then_inc(s_blk, 1)
            pe.wait_ge(s_uact, FT)
            gate_rows(5 * KT, s_gb2p, s_gb2c)
            pe.wait_ge(s_gb2c, 8)
            for q in range(2):
                for f in range(FT):
                    i = q * FT + f
                    n = P_DOWN + i // DOWN_KT
                    pe.wait_ge(s_lo, n + 1)
                    pe.wait_ge(s_al, i + 1)
                    w_hi, w_lo = parts(n, DOWN_KT)
                    for t in range(3):
                        for c in range(2):
                            if q == 1 and f == 0 and 2 * t + c >= 2:
                                pe.wait_ge(s_dc, 2 * t + c - 1)
                            cs = slice(512 * c, 512 * c + 512)
                            last = three(ps[:, (6 * q + 2 * t + c) % 8, :], ah[i % 3][:, toks(t)], al[i % 3][:, toks(t)],
                                         w_hi[:, f % DOWN_KT, cs], w_lo[:, f % DOWN_KT, cs], start=(f == 0), stop=(f == FT - 1))
                    last.then_inc(s_kd, 1)

        @block.scalar
        def _(ac):
            AC = nc.scalar.activation
            cnt = [0]

            def link(ins):
                cnt[0] += 1
                ins.then_inc(s_a, 1)
                ac.wait_ge(s_a, cnt[0])

            roots = [0]

            def root(ap):
                roots[0] += 1
                ac.wait_ge(s_var, roots[0])
                AC(ap, ap, ACT.Sqrt).then_inc(s_root, 1)

            def hi(n):
                ac.wait_ge(s_w[n % RING], 16 * (n // RING + 1))
                if n >= SPLITS:
                    used(ac, n - SPLITS)
                AC(wh[n % SPLITS][:, 0:width(n)], slot_of(n)[:, 0:width(n)], ACT.Copy).then_inc(s_hi, 1)

            for t in range(3):
                ac.wait_ge(s_x, 48)
                AC(junk, x[:, t, :], ACT.Square, accum_out=stat[:, t:t + 1]).then_inc(s_ssq, 1)
                ac.wait_ge(s_ssq, t + 1)
            ac.wait_ge(s_vt, 1)
            AC(csig, ps[:, 0, 0:2 * KT], ACT.Sigmoid).then_inc(s_csig, 1)
            root(stat[:, 4:7])
            ac.wait_ge(s_ct, 1)
            c4v = c4_t[:, :].rearrange("p (k r g) -> p r k g", r=2, g=2)
            AC(c4v[:, 0], cT.rearrange("p (g k) -> p k g", g=2), ACT.Copy).then_inc(s_c4, 1)
            ac.wait_ge(s_xn, 3)
            for n in range(12):
                t, g = n // 4, n % 4
                ac.wait_ge(s_xt, n + 1)
                AC(xT[:, 4 * g:4 * g + 4, toks(t)], ps[:, 5 + n % 3, :].rearrange("p (j c) -> p j c", j=4), ACT.Copy).then_inc(s_xc, 1)
            def mod_row(i):
                ac.wait_ge(s_blk, 2 * i + 2)
                if i >= 2:
                    ac.wait_ge(s_mcT, i - 1)
                AC(modrow[0:4, i % 2, :], ps[0:4, i % 2, 0:BLK], ACT.Copy).then_inc(s_mrow, 1)

            for i in range(N_MOD):
                hi(2 * i)
                hi(2 * i + 1)
                if i:
                    mod_row(i - 1)
            mod_row(N_MOD - 1)
            for q in range(4):
                ac.wait_ge(s_hm, q + 1)
                AC(hh[:, 4 * q:4 * q + 4, :], xT[:, 4 * q:4 * q + 4, :], ACT.Copy).then_inc(s_hh, 1)

            def take_items(b):
                for m, (n, kind, what, j, s, eng) in enumerate(ITEMS):
                    if eng != "act" or n != b:
                        continue
                    ac.wait_ge(s_blk, P_IN + 2 * n + 2)
                    if what == "q":
                        AC(qkT[:, j + s, :], ps[:, m % 8, 0:TOK], ACT.Copy).then_inc(s_eact, 1)
                    elif what == "v":
                        AC(v_tok[:, s, BLK * j:BLK * j + BLK], ps[:, m % 8, 0:BLK], ACT.Copy).then_inc(s_eact, 1)
                    elif what == "rkv":
                        AC(rkv[:, s, BLK * j:BLK * j + BLK], ps[:, m % 8, 0:BLK], ACT.Copy).then_inc(s_eact, 1)
                    elif what == "glu_b":
                        if j:
                            ac.wait_ge(s_edve, evacs("dve", m))
                        AC(sgt[:, s, :], ps[:, m % 8, 0:TOK], ACT.Sigmoid).then_inc(s_eact, 1)
                    else:
                        f = (ACT.Tanh, ACT.Copy, ACT.Sigmoid)[j + s]
                        AC(lora[:, j + s, :], ps[:, m % 8, 0:TOK], f).then_inc(s_eact, 1)

            for j in range(len(IN_BLOCKS)):
                hi(P_IN + 2 * j)
                hi(P_IN + 2 * j + 1)
                if j:
                    take_items(j - 1)
            take_items(len(IN_BLOCKS) - 1)
            ac.wait_ge(s_ccen, 1)
            AC(csq, cbuf, ACT.Square).then_inc(s_csq, 1)
            ac.wait_ge(s_ckt, 1)
            for i in range(2):
                AC(ckT[:, 3 * i:3 * i + 3, :], ps[:, 6 + i, 0:TOK].rearrange("p (j c) -> p j c", j=3), ACT.Copy).then_inc(s_ckc, 1)
            ac.wait_ge(s_knt, 1)
            for i in range(2):
                AC(knew[:, TOK * i:TOK * i + TOK], ps[:, 4 + i, 0:TOK], ACT.Copy).then_inc(s_knc, 1)
            root(crstd)
            ac.wait_ge(s_cn, 1)
            for t in range(BT):
                AC(cbuf[:, t, :], cbuf[:, t, :], ACT.Silu,
                   scale=vcol[:, 2, 92 + t:93 + t], bias=vcol[:, 2, 96 + t:97 + t]).then_inc(s_cs, 1)
            ac.wait_ge(s_blk, P_OUT)
            for t in range(BT):
                ac.wait_ge(s_cs, t + 1)
                for (a0, b0, n) in ((0, 0, P), (P + PADC, P, 2 * P)):
                    AC(yh[:, 6 + t, b0:b0 + n], cbuf[:, t, a0:a0 + n], ACT.Copy).then_inc(s_cy, 1)

            def expo(u):
                t, h = ATT[u]
                n = P if t == 0 else TOK
                ac.wait_ge(s_sm, u + 1)
                AC(ss[:, u % 3, 0:n], ss[:, u % 3, 0:n], ACT.Exp, bias=stat[:, 8 + u % 4:9 + u % 4],
                   accum_out=stat[:, 16 + u % 4:17 + u % 4]).then_inc(s_ex, 1)

            def take(u):
                t, h = ATT[u]
                n = P if t == 0 else TOK
                ac.wait_ge(s_pt, u + 1)
                if u >= 2:
                    ac.wait_ge(s_pv, u - 1)
                AC(PT[:, u % 2, 0:n], ps[:, 2 + u % 2, 0:n], ACT.Copy).then_inc(s_ptc, 1)

            def result(u):
                t, h = ATT[u]
                ac.wait_ge(s_pv, u + 1)
                AC(yh[:, h // 2, toks(t)], ps[:, 4 + (u // 2) % 2, 0:P], ACT.Copy).then_inc(s_pvh, 1)

            for u in range(len(ATT) + 3):
                if u < len(ATT):
                    expo(u)
                if 0 <= u - 2 < len(ATT):
                    take(u - 2)
                if 0 <= u - 3 and (u - 3) % 2 == 1:
                    result(u - 3)

            for u in range(12):
                hf, u6 = u // 6, u % 6
                t, d, s0 = UNITS[u6]
                ac.wait_ge(s_rpre, u + 1)
                AC(tW, tW, ACT.Sigmoid)
                AC(tA, tA, ACT.Sigmoid).then_inc(s_rsig, 1)
                root(st6[:, 0, :])
                ac.wait_ge(s_rcum, u + 1)
                if u6 == 2:
                    ac.wait_ge(s_S0, 2 * hf + 2)
                AC(eE, ps[:, 3, 0:HW], ACT.Exp, scale=-DECAY)
                AC(eP, ps[:, 2, 0:HW], ACT.Exp, scale=-DECAY)
                if u6 in (1, 2):
                    ac.wait_ge(s_stout, 32 * hf + 16 * u6)
                AC(eN, ps[:, 2, 0:HW], ACT.Exp, scale=DECAY)
                AC(eR, ps[:, 4, 0:HW], ACT.Exp, scale=-DECAY)
                AC(eT, ps[:, 5, 0:HW], ACT.Exp, scale=-DECAY).then_inc(s_rexp, 1)
                ac.wait_ge(s_rtr, u + 1)
                tri = lambda b: ps[:, b, 0:HW].rearrange("p (j c) -> p j c", j=3)
                AC(zrT[:, :, 0, :], tri(0), ACT.Copy)
                AC(zrT[:, :, 1, :], tri(1), ACT.Copy)
                AC(bT, tri(4), ACT.Copy)
                AC(kT, tri(5), ACT.Copy).then_inc(s_rtc, 1)
                ac.wait_ge(s_rN, u + 1)
                for g in range(2):
                    AC(Nm[:, 3 * g:3 * g + 3, :], tri(4 + g), ACT.Copy).then_inc(s_rNc, 1)
                ac.wait_ge(s_rAV, u + 1)
                AC(ZA[:, :, 1, :], ps[:, 6, 0:HW].rearrange("p (h c) -> p h c", h=HH), ACT.Copy).then_inc(s_rAVc, 1)
                ac.wait_ge(s_rZU, u + 1)
                AC(ZU[:, 0:3, :, :].rearrange("p h a c -> p (h a c)"), ps[:, 0, 0:TOK], ACT.Copy)
                AC(ZU[:, 3:6, :, :].rearrange("p h a c -> p (h a c)"), ps[:, 1, 0:TOK], ACT.Copy).then_inc(s_rZUc, 1)
                if u6 < 2:
                    ac.wait_ge(s_stT, 2 * hf + u6 + 1)
                    ac.wait_ge(s_rdone, u + 1)
                    if u6 == 1:
                        ac.wait_ge(s_stout, 32 * hf + 16)
                    AC(sout[0:HD, :], ps[0:HD, 7, 0:HW], ACT.Copy).then_inc(s_stc, 1)
                if u6 in FINAL:
                    w_, t_ = FINAL[u6]
                    root(st6[:, 3, :])
                    ac.wait_ge(s_fT, 3 * hf + w_ + 1)
                    AC(yh[:, 10 + 3 * hf:13 + 3 * hf, toks(t_)], tri(6), ACT.Copy).then_inc(s_fh, 1)

            for n in range(8):
                ac.wait_ge(s_gbp, n + 1)
                AC(gb[:, n // 4, 512 * (n % 4):512 * (n % 4) + 512], ps[:, 6 + n % 2, :], ACT.Copy).then_inc(s_gbc, 1)
            for j in range(D // BLK):
                hi(P_OUT + 2 * j)
                hi(P_OUT + 2 * j + 1)
            ac.wait_ge(s_oc, 3 * (D // BLK))
            for t in range(3):
                AC(xn2[:, t, :], x2[:, t, :], ACT.Square, accum_out=stat[:, 24 + t:25 + t]).then_inc(s_ssq2, 1)
            root(stat[:, 28:31])
            for n in range(12):
                ac.wait_ge(s_hm2, n + 1)
                AC(hh[:, 4 * (n % 4):4 * (n % 4) + 4, toks(n // 4)], mtmp[:, n % 2], ACT.Copy).then_inc(s_hh2, 1)
            for b in range(2 * (DFF // BLK) + 1):
                if b < 2 * (DFF // BLK):
                    hi(P_UP + 2 * b)
                    hi(P_UP + 2 * b + 1)
                if b % 2:
                    i = b // 2
                    ac.wait_ge(s_blk, P_UP + 2 * b)
                    ac.wait_ge(s_pad, 2)
                    for s in range(2):
                        if i:
                            ac.wait_ge(s_ucv, 2 * (i - 1) + s + 1)
                        b_ = 4 * (i % 2) + s
                        AC(up2[:, s, 1:1 + P], ps[:, b_, 0:P], ACT.Copy)
                        AC(up2[:, s, 2 + P:2 + TOK], ps[:, b_, P:TOK], ACT.Copy).then_inc(s_uc, 1)
                elif b:
                    i = b // 2 - 1
                    for s in range(2):
                        ac.wait_ge(s_ucv, 2 * i + s + 1)
                        if i:
                            ac.wait_ge(s_uact, 2 * (i - 1) + s + 1)
                        AC(sg2[:, s, :], cv2[:, s, :], ACT.Silu).then_inc(s_usg, 1)
            for n in range(8):
                ac.wait_ge(s_gb2p, n + 1)
                AC(gb2[:, n // 4, 512 * (n % 4):512 * (n % 4) + 512], ps[:, 6 + n % 2, :], ACT.Copy).then_inc(s_gb2c, 1)
            ac.wait_ge(s_uact, FT)
            for i in range(2 * FT):
                if i % DOWN_KT == 0:
                    hi(P_DOWN + i // DOWN_KT)
                if i >= 3:
                    ac.wait_ge(s_kd, i - 2)
                AC(ah[i % 3], act[:, i % FT, :], ACT.Copy).then_inc(s_ah, 1)
            for t in range(3):
                ac.wait_ge(s_dc, 6 + 2 * t + 2)
                AC(junk2, x3[:, t, :], ACT.Square, accum_out=stat[:, 32 + t:33 + t]).then_inc(s_fss, 1)
                ac.wait_ge(s_fss, t + 1)
                root(stat[:, 36 + t:37 + t])

        @block.vector
        def _(dv):
            V = nc.vector
            cnt = [0]

            def link(ins):
                cnt[0] += 1
                ins.then_inc(s_d, 1)
                dv.wait_ge(s_d, cnt[0])

            roots = [0]

            def inv_root(ins, ap):
                roots[0] += 1
                ins.then_inc(s_var, 1)
                dv.wait_ge(s_root, roots[0])
                link(V.reciprocal(ap, ap))

            def mark(ins):
                cnt[0] += 1
                ins.then_inc(s_d, 1)
                return cnt[0]

            def lo(n):
                dv.wait_ge(s_hi, n + 1)
                w = width(n)
                V.tensor_tensor(wl[n % SPLITS][:, 0:w], slot_of(n)[:, 0:w], wh[n % SPLITS][:, 0:w].bitcast(F32),
                                ALU.subtract).then_inc(s_lo, 1)

            dv.wait_ge(s_csig, 1)
            V.tensor_tensor(cT, csig, ps[:, 0, 0:2 * KT], ALU.mult).then_inc(s_ct, 1)
            for g, rows in enumerate((128, 124, 100, 88)):
                dv.wait_ge(s_vt, g + 2)
                V.tensor_copy(vcol[:, g, 0:rows], ps[:, 1 + g, 0:rows]).then_inc(s_vc, 1)
            dv.wait_ge(s_ssq, 3)
            inv_root(V.tensor_scalar(stat[:, 4:7], stat[:, 0:3], 1.0 / D, 1e-6, ALU.mult, ALU.add), stat[:, 4:7])
            for t in range(3):
                V.tensor_scalar(xn[:, t, :], x[:, t, :], stat[:, 4 + t:5 + t], None, ALU.mult).then_inc(s_xn, 1)
            dv.wait_ge(s_c4, 1)
            c4v = c4_t[:, :].rearrange("p (k r g) -> p r k g", r=2, g=2)
            V.tensor_tensor(c4v[:, 1], cT.rearrange("p (g k) -> p k g", g=2), c4v[:, 0].bitcast(F32), ALU.subtract).then_inc(s_c4, 1)
            dv.wait_ge(s_vc, 4)

            def mod_col(i):
                dv.wait_ge(s_mcT, i + 1)
                V.tensor_tensor(modcol[:, 2 * i:2 * i + 2, :], ps[:, 2 + i % 2, 0:4].rearrange("p (t g) -> p t g", g=2),
                                vcol[:, 0, 32 + 2 * i:34 + 2 * i].unsqueeze(2).broadcast_to([P, 2, 2]), ALU.add).then_inc(s_mcol, 1)
            for i in range(N_MOD):
                lo(2 * i)
                lo(2 * i + 1)
                if i >= 2:
                    mod_col(i - 2)
            mod_col(N_MOD - 2)
            mod_col(N_MOD - 1)
            dv.wait_ge(s_mcol, N_MOD)
            n1 = vcol[:, 0, 0:KT].unsqueeze(2).broadcast_to([P, KT, 2])
            n2 = vcol[:, 0, KT:2 * KT].unsqueeze(2).broadcast_to([P, KT, 2])
            link(V.tensor_scalar(scol, modcol[:, KT:2 * KT, :], 1.0, None, ALU.add))
            link(V.tensor_tensor(scol, scol, n1, ALU.mult))
            dv.wait_ge(s_xc, 12)
            for k in range(KT):
                for g, r in ((0, slice(0, P)), (1, slice(P, TOK))):
                    last = V.tensor_scalar(xT[:, k, r], xT[:, k, r], scol[:, k, g:g + 1], modcol[:, k, g:g + 1], ALU.mult, ALU.add)
                if k % 4 == 3:
                    last.then_inc(s_hm, 1)
            for q in range(4):
                dv.wait_ge(s_hh, q + 1)
                last = V.tensor_tensor(hl[:, 4 * q:4 * q + 4, :], xT[:, 4 * q:4 * q + 4, :],
                                       hh[:, 4 * q:4 * q + 4, :].bitcast(F32), ALU.subtract)
            last.then_inc(s_h, 1)
            dv.wait_ge(s_h, 1)
            link(V.tensor_scalar(scol, modcol[:, 4 * KT:5 * KT, :], 1.0, None, ALU.add))
            link(V.tensor_tensor(scol, scol, n2, ALU.mult))
            for c_, n in ((0, PADC), (PADC + P, PADC), (PADC * 2 + TOK, PADC)):
                link(V.memset(upad[:, :, c_:c_ + n], 0.0))
            def take_items(b):
                for m, (n, kind, what, j, s, eng) in enumerate(ITEMS):
                    if eng != "dve" or n != b:
                        continue
                    dv.wait_ge(s_blk, P_IN + 2 * n + 2)
                    if what == "k":
                        V.tensor_copy(qkT[:, 6 + j + s, :], ps[:, m % 8, 0:TOK]).then_inc(s_edve, 1)
                    else:
                        dv.wait_ge(s_eact, evacs("act", m))
                        V.tensor_tensor(upad[:, j + s, PADC:PADC + P], ps[:, m % 8, 0:P], sgt[:, s, 0:P], ALU.mult)
                        V.tensor_tensor(upad[:, j + s, 2 * PADC + P:2 * PADC + TOK], ps[:, m % 8, P:TOK], sgt[:, s, P:TOK],
                                        ALU.mult).then_inc(s_edve, 1)

            at = [0] * BT

            def conv(first, last_):
                for n in range(first, min(last_, CONV_K * BT)):
                    j, t = n // BT, n % BT
                    w = vcol[:, 1, n:n + 1]
                    if j == 0:
                        at[t] = mark(V.tensor_scalar(cbuf[:, t, :], upad[:, t, 0:CW], w, vcol[:, 2, 88 + t:89 + t], ALU.mult, ALU.add))
                    else:
                        dv.wait_ge(s_d, at[t])
                        at[t] = mark(V.scalar_tensor_tensor(cbuf[:, t, :], upad[:, t, j:j + CW], w, cbuf[:, t, :], ALU.mult, ALU.add))

            glu_end = max(it[0] for it in ITEMS if it[2] == "glu_a") + 1
            per = -(-CONV_K * BT // (len(IN_BLOCKS) - glu_end - 1))
            for j in range(len(IN_BLOCKS)):
                lo(P_IN + 2 * j)
                lo(P_IN + 2 * j + 1)
                if j:
                    take_items(j - 1)
                if j == glu_end:
                    dv.wait_ge(s_edve, evacs("dve", len(ITEMS)))
                if j >= glu_end:
                    conv(per * (j - glu_end), per * (j - glu_end + 1))
            dv.wait_ge(s_d, cnt[0])
            dv.sem_inc(s_cbuf, 1)
            dv.wait_ge(s_cmean, 1)
            for t in range(BT):
                last = V.tensor_tensor(cbuf[:, t, :], cbuf[:, t, :], ps[:, 0, 0:CW], ALU.subtract)
            last.then_inc(s_ccen, 1)
            dv.wait_ge(s_cvar, 1)
            inv_root(V.tensor_scalar(crstd, ps[:, 1, 0:CW], 1e-5, None, ALU.add), crstd)
            for t in range(BT):
                last = V.tensor_tensor(cbuf[:, t, :], cbuf[:, t, :], crstd, ALU.mult)
            last.then_inc(s_cn, 1)

            for t in range(BT):
                for i, (a0, b0, n) in enumerate(((0, 0, P), (P + PADC, P, 2 * P))):
                    dv.wait_ge(s_cy, 2 * t + i + 1)
                    V.tensor_tensor(yl[:, 6 + t, b0:b0 + n], cbuf[:, t, a0:a0 + n], yh[:, 6 + t, b0:b0 + n].bitcast(F32),
                                    ALU.subtract).then_inc(s_cyh, 1)


            def softmax(u):
                t, h = ATT[u]
                n = P if t == 0 else TOK
                dv.wait_ge(s_sc, u + 1)
                if u >= 3:
                    dv.wait_ge(s_pt, u - 2)
                if t == 0:
                    link(V.tensor_scalar(ss[:, u % 3, 0:P], ps[:, u % 2, 0:P], SCALE, None, ALU.mult))
                else:
                    b_ = Bm[:, h, 4 - 2 * t:8 - 2 * t, :].rearrange("p r c -> p (r c)")
                    V.scalar_tensor_tensor(ss[:, u % 3, 0:2 * P], ps[:, u % 2, 0:2 * P], SCALE, b_, ALU.mult, ALU.add)
                    link(V.tensor_scalar(ss[:, u % 3, 2 * P:TOK], ps[:, u % 2, 2 * P:TOK], SCALE, None, ALU.mult))
                V.tensor_reduce(stat[:, 8 + u % 4:9 + u % 4], ss[:, u % 3, 0:n], AX.X, ALU.max, negate=True).then_inc(s_sm, 1)

            def norm(u):
                t, h = ATT[u]
                n = P if t == 0 else TOK
                dv.wait_ge(s_ex, u + 1)
                link(V.reciprocal(stat[:, 20 + u % 4:21 + u % 4], stat[:, 16 + u % 4:17 + u % 4]))
                V.tensor_scalar(ss[:, u % 3, 0:n], ss[:, u % 3, 0:n], stat[:, 20 + u % 4:21 + u % 4], None, ALU.mult).then_inc(s_nr, 1)

            def result(u):
                t, h = ATT[u]
                dv.wait_ge(s_pvh, u // 2 + 1)
                V.tensor_tensor(yl[:, h // 2, toks(t)], ps[:, 4 + (u // 2) % 2, 0:P], yh[:, h // 2, toks(t)].bitcast(F32),
                                ALU.subtract).then_inc(s_pvc, 1)

            for u in range(len(ATT) + 4):
                if u == HA:
                    dv.wait_ge(s_Bm, 16 * 2 * HA)
                    V.tensor_tensor(Bm.rearrange("p h r c -> p (h r) c"), Bm.rearrange("p h r c -> p (h r) c"),
                                    consts[:, C_COL:C_COL + GRID].unsqueeze(1).broadcast_to([P, 6 * HA, GRID]), ALU.add).then_inc(s_Bmask, 1)
                    dv.wait_ge(s_Bmask, 1)
                if u < len(ATT):
                    softmax(u)
                if 0 < u <= len(ATT):
                    norm(u - 1)
                if u >= 4 and (u - 4) % 2 == 1:
                    result(u - 4)
            dv.wait_ge(s_pvc, len(ATT) // 2)

            def heads(ap):
                return ap.rearrange("p (h c) -> p h c", h=HH)

            for u in range(12):
                hf, u6 = u // 6, u % 6
                t, d, s0 = UNITS[u6]
                rr, kr, vr = (rkv[:, t, q + HW * hf:q + HW * hf + HW] for q in (0, 768, 1536))
                acc = 0 if t < 2 else 1
                if u6 == 0:
                    dv.wait_ge(s_par, 16 * LOADS_PER_HALF * (hf + 1))
                    for dd in range(2):
                        last = V.memset(S[:, 5 * dd, :, :], 0.0)
                    last.then_inc(s_S0, 1)
                    dv.wait_ge(s_S0, 2 * hf + 1)
                if u6 == 2:
                    dv.wait_ge(s_sT, hf + 1)
                    for dd in range(2):
                        last = V.tensor_copy(S[:, 5 * dd, :, :], ps[:, 7, 192 * dd:192 * dd + 192].rearrange("p (i c) -> p i c", i=3))
                    last.then_inc(s_S0, 1)
                dv.wait_ge(s_rlora, u + 1)
                V.tensor_tensor(tW, ps[:, 0, 0:HW], par[:, d, :], ALU.add)
                V.tensor_tensor(tA, ps[:, 1, 0:HW], par[:, 2 + d, :], ALU.add).then_inc(s_rpre, 1)
                link(V.tensor_tensor(kkn, kr, par[:, 4, :], ALU.mult))
                link(V.tensor_tensor(sq, kkn, kkn, ALU.mult))
                link(V.tensor_reduce(st6[:, 0, :], heads(sq), AX.X, ALU.add))
                inv_root(V.tensor_scalar(st6[:, 0, :], st6[:, 0, :], 1e-12, None, ALU.add), st6[:, 0, :])
                link(V.tensor_tensor(heads(kkn), heads(kkn), st6[:, 0, :].unsqueeze(2).broadcast_to([P, HH, HD]), ALU.mult))
                dv.wait_ge(s_rsig, u + 1)
                V.tensor_tensor(b1, kkn, tA, ALU.mult)
                link(V.scalar_tensor_tensor(kd, tA, 1.0, par[:, 5, :], ALU.subtract, ALU.mult))
                link(V.scalar_tensor_tensor(kd, kd, 1.0, kr, ALU.add, ALU.mult))
                link(V.tensor_tensor(sq, rr, kd, ALU.mult))
                link(V.tensor_tensor(sq, sq, par[:, 6, :], ALU.mult))
                if d == 0 or u6 == 3:
                    first = u6 in (0, 2, 3)
                else:
                    first = False
                if first:
                    link(V.tensor_reduce(bsum[:, acc, :], heads(sq), AX.X, ALU.add))
                else:
                    link(V.tensor_reduce(st6[:, 1, :], heads(sq), AX.X, ALU.add))
                    link(V.tensor_tensor(bsum[:, acc, :], bsum[:, acc, :], st6[:, 1, :], ALU.add))
                dv.wait_ge(s_rexp, u + 1)
                link(V.scalar_tensor_tensor(tmp, kkn, -1.0, eE, ALU.mult, ALU.mult))
                V.tensor_tensor(rtil, rr, eP, ALU.mult)
                V.tensor_tensor(btil, b1, eN, ALU.mult)
                V.tensor_tensor(ktil, kd, eN, ALU.mult).then_inc(s_rtil, 1)
                V.tensor_copy(ZA[:, :, 0, :], heads(tmp))
                V.tensor_tensor(Bbar, b1, eR, ALU.mult)
                V.tensor_tensor(Kbar, kd, eR, ALU.mult)
                for p in range(2):
                    for hp in range(2):
                        src = eT[half(p), :].rearrange("p (i a c) -> p i a c", i=3, a=2)[:, :, hp, :]
                        last = V.tensor_tensor(dP[half(hp), p, :, :], src,
                                               consts[half(p), C_ID + 64 * p:C_ID + 64 * p + 64].unsqueeze(1).broadcast_to([HD, 3, HD]), ALU.mult)
                last.then_inc(s_rbar, 1)
                m4 = consts[:, C_M4 + 512 * d:C_M4 + 512 * d + 512]
                for h in range(HH):
                    dv.wait_ge(s_rA, HH * u + h + 1)
                    V.tensor_tensor(Am[:, h, :, :].rearrange("p a b -> p (a b)"), ps[:, h % 4, :], m4, ALU.mult).then_inc(s_rAm, 1)
                same2 = consts[:, C_SAME2:C_SAME2 + P].unsqueeze(1).broadcast_to([P, HH, P])
                idb = ident.unsqueeze(1).broadcast_to([P, HH, P])
                dv.wait_ge(s_rAm, HH * (u + 1))
                link(V.tensor_tensor(TTm, Am[:, :, 0, :], same2, ALU.mult))
                V.tensor_tensor(TTm, TTm, idb, ALU.add)
                dv.wait_ge(s_rNc, 2 * u + 2)
                link(V.tensor_tensor(Tm, Nm, same2, ALU.mult))
                V.tensor_tensor(Tm, Tm, idb, ALU.add).then_inc(s_rT0, 1)
                tri = lambda b: ps[:, b, 0:HW].rearrange("p (j c) -> p j c", j=3)
                dv.wait_ge(s_rT0, u + 1)
                for l in range(LEVELS):
                    xm = consts[:, C_XM + (LEVELS * d + l) * P:C_XM + (LEVELS * d + l + 1) * P].unsqueeze(1).broadcast_to([P, 3, P])
                    for g in range(2):
                        dv.wait_ge(s_rX, 2 * LEVELS * u + 2 * l + g + 1)
                        V.tensor_tensor(Xm[:, 3 * g:3 * g + 3, :], tri(g), xm, ALU.mult).then_inc(s_rXm, 1)
                    for g in range(2):
                        dv.wait_ge(s_rTp, 2 * LEVELS * u + 2 * l + g + 1)
                        V.tensor_tensor(Tm[:, 3 * g:3 * g + 3, :], Tm[:, 3 * g:3 * g + 3, :], tri(2 + g), ALU.add)
                        V.tensor_tensor(TTm[:, 3 * g:3 * g + 3, :], TTm[:, 3 * g:3 * g + 3, :], tri(4 + g), ALU.add).then_inc(s_rTu, 1)
                dv.wait_ge(s_rQM, u + 1)
                V.tensor_tensor(QT, tri(2), zrT[:, :, 1, :], ALU.add)
                for p in range(2):
                    V.tensor_tensor(MT[:, p], ps[:, 3 + p, 0:192].rearrange("p (i c) -> p i c", i=3), dP[:, p], ALU.add)
                    last = V.tensor_copy(Sh[:, p], ps[:, 3 + p, 192:384].rearrange("p (i c) -> p i c", i=3))
                last.then_inc(s_rQMc, 1)
                dv.wait_ge(s_rQMc, u + 1)
                for s in range(2):
                    c = s if d == 0 else 1 - s
                    dv.wait_ge(s_rSp, 2 * u + s + 1)
                    for hp in range(2):
                        last = V.tensor_tensor(S[half(hp), 5 * d + s0 + s + 1], Sh[half(hp), c],
                                               ps[half(hp), 5 + hp, 0:192].rearrange("p (i c) -> p i c", i=3), ALU.add)
                    last.then_inc(s_rS, 1)
                dv.wait_ge(s_rO, u + 1)
                for hp in range(2):
                    dst = Oacc[:, acc, :].rearrange("p (i a c) -> p i a c", i=3, a=2)[:, :, hp, :]
                    src = ps[:, hp, 0:192].rearrange("p (i c) -> p i c", i=3)
                    if u6 in (0, 2, 3):
                        last = V.tensor_copy(dst, src)
                    else:
                        last = V.tensor_tensor(dst, dst, src, ALU.add)
                last.then_inc(s_rdone, 1)
                if u6 in FINAL:
                    w_, t_ = FINAL[u6]
                    f = 3 * hf + w_
                    O = Oacc[:, acc, :]
                    dv.wait_ge(s_rdone, u + 1)
                    link(V.tensor_reduce(st6[:, 2, :], heads(O), AX.X, ALU.add))
                    link(V.scalar_tensor_tensor(heads(O), st6[:, 2, :].unsqueeze(2).broadcast_to([P, HH, HD]), -1.0 / HD, heads(O), ALU.mult, ALU.add))
                    link(V.tensor_tensor(sq, O, O, ALU.mult))
                    link(V.tensor_reduce(st6[:, 3, :], heads(sq), AX.X, ALU.add))
                    inv_root(V.tensor_scalar(st6[:, 3, :], st6[:, 3, :], 1.0 / HD, 64e-5, ALU.mult, ALU.add), st6[:, 3, :])
                    link(V.tensor_tensor(heads(O), heads(O), st6[:, 3, :].unsqueeze(2).broadcast_to([P, HH, HD]), ALU.mult))
                    link(V.tensor_tensor(O, O, par[:, 7, :], ALU.mult))
                    V.tensor_tensor(heads(sq), heads(vr), bsum[:, acc, :].unsqueeze(2).broadcast_to([P, HH, HD]), ALU.mult)
                    link(V.tensor_tensor(O, O, par[:, 8, :], ALU.add))
                    link(V.tensor_tensor(O, O, sq, ALU.add))
                    dv.wait_ge(s_fg, f + 1)
                    V.tensor_tensor(O, O, ps[:, 7, 0:HW], ALU.mult).then_inc(s_fy, 1)
                    dv.wait_ge(s_fh, f + 1)
                    ydst = slice(10 + 3 * hf, 13 + 3 * hf)
                    V.tensor_tensor(yl[:, ydst, toks(t_)], tri(6), yh[:, ydst, toks(t_)].bitcast(F32), ALU.subtract).then_inc(s_fc, 1)

            dv.wait_ge(s_fc, 6)

            def residual(j):
                used(dv, P_OUT + 2 * j + 1)
                for t in range(3):
                    n = 3 * j + t
                    cs = slice(BLK * j, BLK * j + BLK)
                    link(V.tensor_tensor(ytmp[:, t % 2], ps[:, 3 * (j % 2) + t, 0:BLK], gb[:, min(t, 1), cs], ALU.mult))
                    V.tensor_tensor(x2[:, t, cs], x2[:, t, cs], ytmp[:, t % 2], ALU.add).then_inc(s_oc, 1)
                    dv.wait_ge(s_oc, n + 1)

            for j in range(D // BLK):
                lo(P_OUT + 2 * j)
                lo(P_OUT + 2 * j + 1)
                if j == 0:
                    dv.wait_ge(s_x2, 48)
                    dv.wait_ge(s_gbc, 8)
                else:
                    residual(j - 1)
            residual(D // BLK - 1)
            dv.wait_ge(s_ssq2, 3)
            inv_root(V.tensor_scalar(stat[:, 28:31], stat[:, 24:27], 1.0 / D, 1e-6, ALU.mult, ALU.add), stat[:, 28:31])
            for t in range(3):
                V.tensor_scalar(xn2[:, t, :], x2[:, t, :], stat[:, 28 + t:29 + t], None, ALU.mult).then_inc(s_xn2, 1)

            def h2_lo(n):
                dv.wait_ge(s_hh2, n + 1)
                at_ = (slice(4 * (n % 4), 4 * (n % 4) + 4), toks(n // 4))
                V.tensor_tensor(hl[:, at_[0], at_[1]], mtmp[:, n % 2], hh[:, at_[0], at_[1]].bitcast(F32), ALU.subtract).then_inc(s_h2, 1)

            for n in range(12):
                t, q = n // 4, n % 4
                g = min(t, 1)
                if n >= 2:
                    h2_lo(n - 2)
                    dv.wait_ge(s_h2, n - 1)
                dv.wait_ge(s_xt2, n + 1)
                for j in range(4):
                    k = 4 * q + j
                    last = V.tensor_scalar(mtmp[:, n % 2, j], ps[:, n % 4, toks(j)], scol[:, k, g:g + 1],
                                           modcol[:, 3 * KT + k, g:g + 1], ALU.mult, ALU.add)
                last.then_inc(s_hm2, 1)
            h2_lo(10)
            h2_lo(11)
            dv.wait_ge(s_h2, 12)
            for c_ in (0, 1 + P, 2 + TOK):
                last = V.memset(up2[:, :, c_:c_ + 1], 0.0)
            last.then_inc(s_pad, 2)
            dv.wait_ge(s_xs, 16)
            W3 = TOK + 1
            for b in range(2 * (DFF // BLK) + 1):
                if b < 2 * (DFF // BLK):
                    lo(P_UP + 2 * b)
                    lo(P_UP + 2 * b + 1)
                if b % 2:
                    for s in range(2):
                        f = b - 1 + s
                        dv.wait_ge(s_uc, f + 1)
                        if f >= 2:
                            dv.wait_ge(s_usg, f - 1)
                        link(V.tensor_scalar(cv2[:, s, :], up2[:, s, 0:W3], vcol[:, 2, f:f + 1], vcol[:, 3, 44 + f:45 + f], ALU.mult, ALU.add))
                        link(V.scalar_tensor_tensor(cv2[:, s, :], up2[:, s, 1:1 + W3], vcol[:, 2, 44 + f:45 + f], cv2[:, s, :], ALU.mult, ALU.add))
                        V.scalar_tensor_tensor(cv2[:, s, :], up2[:, s, 2:2 + W3], vcol[:, 3, f:f + 1], cv2[:, s, :], ALU.mult, ALU.add).then_inc(s_ucv, 1)
                elif b:
                    i = b // 2 - 1
                    dv.wait_ge(s_blk, P_UP + 2 * b)
                    for s in range(2):
                        f = 2 * i + s
                        dv.wait_ge(s_usg, f + 1)
                        b_ = 4 * (i % 2) + 2 + s
                        V.tensor_tensor(act[:, f, 0:P], ps[:, b_, 0:P], sg2[:, s, 0:P], ALU.mult)
                        V.tensor_tensor(act[:, f, P:TOK], ps[:, b_, P:TOK], sg2[:, s, P + 1:TOK + 1], ALU.mult).then_inc(s_uact, 1)

            def residual2(q):
                dv.wait_ge(s_kd, FT * (q + 1))
                tmp2 = ytmp1 if q == 0 else ytmp2
                w = 256 if q == 0 else 512
                for t in range(3):
                    for c in range(2):
                        n = 6 * q + 2 * t + c
                        for e in range(512 // w):
                            cs = slice(DOWN_W * q + 512 * c + w * e, DOWN_W * q + 512 * c + w * (e + 1))
                            link(V.tensor_tensor(tmp2[:, e % 2 if q == 0 else c], ps[:, n % 8, w * e:w * (e + 1)], gb2[:, min(t, 1), cs], ALU.mult))
                            last = V.tensor_tensor(x3[:, t, cs], x3[:, t, cs], tmp2[:, e % 2 if q == 0 else c], ALU.add)
                            if e < 512 // w - 1:
                                link(last)
                        last.then_inc(s_dc, 1)
                        dv.wait_ge(s_dc, n + 1)

            for i in range(2 * FT):
                if i % DOWN_KT == 0:
                    lo(P_DOWN + i // DOWN_KT)
                dv.wait_ge(s_ah, i + 1)
                V.tensor_tensor(al[i % 3], act[:, i % FT, :], ah[i % 3].bitcast(F32), ALU.subtract).then_inc(s_al, 1)
                if i == FT + 2:
                    dv.wait_ge(s_x3, 16)
                    dv.wait_ge(s_gb2c, 8)
                    residual2(0)
            residual2(1)
            dv.wait_ge(s_fgl, 16)
            for t in range(3):
                dv.wait_ge(s_fss, t + 1)
                inv_root(V.tensor_scalar(stat[:, 36 + t:37 + t], stat[:, 32 + t:33 + t], 1.0 / D, 1e-6, ALU.mult, ALU.add),
                         stat[:, 36 + t:37 + t])
                V.scalar_tensor_tensor(x3[:, t, :], x3[:, t, :], stat[:, 36 + t:37 + t], fg, ALU.mult, ALU.mult).then_inc(s_yf, 1)


_INS = ['x_prompt', 'x_sample', 'cache_k', 'cache_v', 'state_fwd', 'state_bwd', 'c', 'c_ctx', 'norm1_g', 'norm2_g',
        'w_mod', 'b_mod', 'w_in', 'w_out', 'rpb', 'conv_w', 'conv_b', 'conv_ln_g', 'conv_ln_b', 'rwkv_w0',
        'rwkv_w_lora', 'rwkv_a0', 'rwkv_a_lora', 'rwkv_g_lora', 'rwkv_k_k', 'rwkv_k_a', 'rwkv_r_k', 'rwkv_ln_g',
        'rwkv_ln_b', 'w_up', 'ffn_conv_w', 'ffn_conv_b', 'w_down', 'final_g']
_OUTS = [("y_prompt", (1, 128, 2048)), ("y_sample", (1, 256, 2048)), ("new_cache_k", (1, 1, 128, 12, 64)),
         ("new_cache_v", (1, 1, 128, 12, 64)), ("new_state_fwd", (1, 1, 12, 64, 64)), ("new_state_bwd", (1, 1, 12, 64, 64))]


def _constants():
    import numpy as np
    j, t = np.meshgrid(np.arange(P), np.arange(P), indexing="ij")
    same = (j // CHUNK) == (t // CHUNK)
    cols = [np.eye(P)]
    for before in ((j < t), (j > t)):
        strict = same & before
        incl = same & (before | (j == t))
        cols += [strict, incl, strict, incl]
    cols.append(same)
    for d in range(2):
        for l in range(LEVELS):
            n = 2 << l
            pair = (j // (2 * n)) == (t // (2 * n))
            a, b = (j // n) % 2, (t // n) % 2
            cols.append(pair & ((a == 0) & (b == 1) if d == 0 else (a == 1) & (b == 0)))
    cols.append((j // 2) == (t // 2))
    q = np.arange(P) % GRID
    start = np.clip(q - 8, 0, GRID - 16)
    kc = np.arange(GRID)
    cols.append(np.where((kc >= start[:, None]) & (kc < start[:, None] + 16), 0.0, -1e30))
    cols.append(np.zeros((P, P)))
    cols.append(np.full((P, P), 1.0 / (BT * P)))
    cols.append((np.arange(P)[:, None] % 2 == np.arange(4)) & (np.arange(P)[:, None] < 4))
    return np.concatenate([np.asarray(c, np.float32) for c in cols], axis=1)


def kernel(**inputs):
    import numpy as _np
    import concourse.bacc as _bacc
    from concourse import mybir as _mybir
    from concourse.bass_utils import run_bass_kernel_spmd as _run

    nc = _bacc.Bacc("TRN2", target_bir_lowering=False, num_devices=1)
    arrays, args, outs = {}, {}, {}
    for name in _INS + ["consts"]:
        a = _constants() if name == "consts" else _np.ascontiguousarray(inputs[name])
        arrays[f"in_{name}_dram"] = a
        args[name] = nc.dram_tensor(f"in_{name}_dram", a.shape, _mybir.dt.from_np(a.dtype), kind="ExternalInput").ap()
    for name, shape in _OUTS:
        outs[name] = nc.dram_tensor(f"out_{name}_dram", shape, F32, kind="ExternalOutput").ap()
    build(nc, args, outs)
    r = _run(nc, [arrays], core_ids=[0])
    return tuple(r.results[0][f"out_{name}_dram"] for name, _ in _OUTS)
```

```python
from contextlib import ExitStack

import concourse.bass as bass
from concourse import mybir

ALU = mybir.AluOpType
ACT = mybir.ActivationFunctionType
F32 = mybir.dt.float32
F32R = mybir.dt.float32r
AX = mybir.AxisListType

P = 128
D = 2048
KT = D // P
TOK = 3 * P
HD = 64
HA = 12
HC = 12
CHUNK = 64
DFF = 11 * D // 4
FT = DFF // P
CONV_K = 31
PADC = CONV_K // 2
BT = 4
GRID = 64
BLK = 256
KP = KT // 2
PIECE = KP * BLK
RING = 4
KQ = KP // 2
PART = KQ * BLK
PARTS = KT // KQ
SPLITS = 4
DECAY = 0.606531
SCALE = HD ** -0.5
LEVELS = 5

C_ID = 0
C_M4 = C_ID + P
C_BONES = C_M4 + 2 * 4 * P
C_XM = C_BONES + P
C_SAME2 = C_XM + 2 * LEVELS * P
C_COL = C_SAME2 + P
C_ZERO = C_COL + GRID
C_MEAN = C_ZERO + P
C_SEL = C_MEAN + P
C_END = C_SEL + 4

N_MOD = 6 * D // BLK
IN_BLOCKS = ([("chan", "q", 256 * j, 256, 2 * j) for j in range(3)]
             + [("chan", "k", 768 + 256 * j, 256, 2 * j) for j in range(3)]
             + [("tok", "v", 1536 + 256 * j, 256, j) for j in range(3)]
             + [b for j in range(2) for b in (("chan", "glu_b", 2816 + 256 * j, 256, 2 * j),
                                              ("chan", "glu_a", 2304 + 256 * j, 256, 2 * j))]
             + [("chan", "lora", 5632, 256, 0), ("chan", "lora", 5888, 128, 2)]
             + [("tok", "rkv", 3328 + 256 * j, 256, j) for j in range(9)])
N_EARLY = 2 * D // BLK
MIXED = [("mod", N_EARLY, 0), ("mod", N_EARLY, 1)]
_left = [("mod", i, p) for i in range(N_EARLY + 1, N_MOD) for p in range(2)]
_in = [("in", j, p) for j in range(len(IN_BLOCKS)) for p in range(2)]
for _i, _piece in enumerate(_in):
    MIXED.append(_piece)
    MIXED += _left[_i * len(_left) // len(_in):(_i + 1) * len(_left) // len(_in)]
STREAM = [("mod", i, p) for i in range(N_EARLY) for p in range(2)] + MIXED
P_MIX = PARTS * N_EARLY
P_OUT = 2 * len(STREAM)
P_UP = P_OUT + PARTS * (D // BLK)
P_DOWN = P_UP + 2 * PARTS * (DFF // BLK)
DOWN_KT = 2
DOWN_W = PIECE // DOWN_KT
MOD_LAST = {2 * n + 1: i for n, (kind, i, p) in enumerate(STREAM) if kind == "mod" and p == 1}
IN_LAST = {2 * n + 1: i for n, (kind, i, p) in enumerate(STREAM) if kind == "in" and p == 1}
IN_END = {i: n + 1 for n, i in IN_LAST.items()}
MOD_END = {i: n + 1 for n, i in MOD_LAST.items()}

BANKS = 6
ITEMS = []
for _n, (_kind, _what, _c, _w, _j) in enumerate(IN_BLOCKS):
    for _s in range(3 if _kind == "tok" else _w // P):
        _eng = "act" if _what in ("q", "v", "rkv", "glu_b", "lora") else "dve"
        ITEMS.append((_n, _kind, _what, _j, _s, _eng))
ATT = [(t, h) for t in range(3) for h in range(HA)]
GROUPS = 3
UNITS = [(0, 0, 0, True), (0, 1, 0, False), (1, 0, 0, True), (2, 1, 0, True), (2, 0, 2, False), (1, 1, 2, False)]
NG = len(UNITS)
NU = GROUPS * NG
FINAL = {1: (0, 0, (0, 1)), 4: (1, 2, (3, 4)), 5: (2, 1, (2, 5))}
HH = HC // GROUPS
HW = HH * HD
CT = HW // P


def steps(u):
    plan = [("X", 0), ("ZU", 0), ("lora", 0), ("T", 0), ("QM", 0), ("kk", 0),
            ("X", 1), ("S", 0), ("cum", 0), ("T", 1), ("S", 1), ("cum", 1),
            ("X", 2), ("O", 0), ("T", 2), ("tr", 0), ("out", 0), ("F", 0),
            ("X", 3), ("A", 0), ("in", 0), ("F", 1), ("T", 3), ("A", 1),
            ("X", 4), ("N", 0), ("F", 2), ("T", 4)]
    shift = dict(X=0, T=0, ZU=-1, QM=-1, S=-1, O=-1, lora=1, kk=1, cum=1, tr=1, A=1, N=1, out=0, F=-2)
    shift["in"] = 0
    picked = []
    for step, l in plan:
        v = u + shift[step]
        if not 0 <= v < NU:
            continue
        if (step == "kk" and v % NG) or (step in ("out", "in") and v % NG != 2) or (step == "F" and v % NG not in FINAL):
            continue
        picked.append((step, l, v))
    return picked


PERIODS = range(-1, NU + 2)


def unit(v):
    return (v % 2, v // NG, *UNITS[v % NG])


def bank_of(m):
    return 2 + m % BANKS


def evacs(eng, m):
    return sum(1 for it in ITEMS[:m] if it[5] == eng)


def build(nc, a, out):
    ctx = ExitStack()
    with ctx:
        def sb(name, cols, dt=F32, where=ctx):
            return where.enter_context(nc.sbuf_tensor(name, [P, cols], dt))

        def sem(name):
            return ctx.enter_context(nc.semaphore(name))

        def carve(t, at, *dims):
            n = 1
            for d in dims:
                n *= d
            v = t[:, at:at + n]
            if len(dims) == 2:
                v = v.rearrange("p (a b) -> p a b", a=dims[0])
            if len(dims) == 3:
                v = v.rearrange("p (a b c) -> p a b c", a=dims[0], b=dims[1])
            if len(dims) == 4:
                v = v.rearrange("p (a b c d) -> p a b c d", a=dims[0], b=dims[1], c=dims[2])
            return v, at + n

        consts = sb("consts", C_END)
        vcol_t = sb("vcol", 4 * P)
        vcol = vcol_t[:, :].rearrange("p (g c) -> p g c", g=4)
        c4_t = sb("c4", 4 * KT, F32R)
        modcol_t = sb("modcol", 2 * 96)
        modcol = modcol_t[:, :].rearrange("p (t g) -> p t g", g=2)
        scol_t = sb("scol", 2 * KT)
        scol = scol_t[:, :].rearrange("p (t g) -> p t g", g=2)
        stat = sb("stat", 64)
        ring = sb("ring", RING * PIECE)
        NA = 52900 - C_END - 4 * P - 4 * KT - 192 - 2 * KT - 64 - RING * PIECE - 2 * SPLITS * PART - 2 * KT * TOK - 2400
        arena = sb("arena", NA)
        with ExitStack() as early:
            wsp = sb("w_split", 2 * SPLITS * PART, F32R, early)
            hsp = sb("h_split", 2 * KT * TOK, F32R, early)
            asp = sb("a_split", 2400, F32R, early)
        wmix = sb("w_mix", 2 * SPLITS * PART)
        hf = sb("h_f32", 2 * KT * TOK)
        ubuf = sb("u_buf", 2400)
        hh = hsp[:, 0:KT * TOK].rearrange("p (k n) -> p k n", k=KT)
        hl = hsp[:, KT * TOK:].rearrange("p (k n) -> p k n", k=KT)
        yh, yl = hh, hl
        wh = [wsp[:, PART * i:PART * i + PART] for i in range(SPLITS)]
        wl = [wsp[:, PART * (SPLITS + i):PART * (SPLITS + i + 1)] for i in range(SPLITS)]
        ah = [asp[:, TOK * i:TOK * i + TOK] for i in range(3)]
        al = [asp[:, TOK * (3 + i):TOK * (4 + i)] for i in range(3)]
        ps_t = ctx.enter_context(nc.psum_tensor("ps", [P, 8 * 512], F32))
        ps = ps_t[:, :].rearrange("p (b n) -> p b n", b=8)

        ident = consts[:, C_ID:C_ID + P]

        x, _ = carve(arena, 0, 3, D)
        xT, o = carve(arena, 0, KT, TOK)
        xn, o = carve(arena, o, 3, D)
        vrow, o = carve(arena, o, 5, P)
        csig, o = carve(arena, o, 2 * KT)
        cT, o = carve(arena, o, 2 * KT)
        junk, o = carve(arena, o, D)
        assert o <= NA
        qkT, o = carve(arena, 0, 12, TOK)
        v_tok, o = carve(arena, o, 3, 768)
        upad, _ = carve(arena, o, BT, PADC * 3 + TOK)
        CW = TOK + PADC
        csq, _ = carve(arena, o, BT, CW)
        o += BT * (PADC * 3 + TOK)
        crstd, o = carve(arena, o, CW)
        modrow, _ = carve(arena, o, 2, BLK)
        knew, o = carve(arena, o, 768)
        O_RKV = NA - 3 * 2304 - 3 * TOK
        assert o <= O_RKV, (o, O_RKV)
        rkv, o = carve(arena, O_RKV, 3, 2304)
        lora, o = carve(arena, o, 3, TOK)
        cbuf, o = carve(ubuf, 0, BT, CW)
        sgt, o = carve(ubuf, o, 2, TOK)
        assert o <= 2400
        Bm, o = carve(ring, 0, HA, 6, GRID)
        ckT, o = carve(ring, o, 6, P)
        cv, o = carve(ring, o, 768)
        ck, o = carve(ring, o, 768)
        assert o <= RING * PIECE
        ss, o = carve(wmix, 0, 3, TOK)
        PT, o = carve(wmix, o, 2, TOK)
        Am, Nm, Tm, TTm, Xm, ZA, ZU, QT, zrT, bT, kT, MT, Sh, dP = ([None, None] for _ in range(14))
        for z, region in enumerate((ring, wmix)):
            Am[z], o = carve(region, 0, HH, 4, P)
            Nm[z], o = carve(region, o, HH, P)
            Tm[z], o = carve(region, o, HH, P)
            TTm[z], o = carve(region, o, HH, P)
            Xm[z], o = carve(region, o, HH, P)
            ZA[z], o = carve(region, o, HH, 2, HD)
            ZU[z], o = carve(region, o, HH, 2, HD)
            QT[z], o = carve(region, o, CT, P)
            zrT[z], o = carve(region, o, CT, 2, P)
            bT[z], o = carve(region, o, CT, P)
            kT[z], o = carve(region, o, CT, P)
            MT[z], o = carve(region, o, 2, CT, HD)
            Sh[z], o = carve(region, o, 2, CT, HD)
            dP[z], o = carve(region, o, 2, CT, HD)
        O_TOK = o
        par, o = carve(arena, 0, 12, HW)
        S, o = carve(arena, o, 2 * 5, CT, HD)
        bonus, o = carve(arena, o, 2 * NG, HH)
        st6, o = carve(arena, o, 4, HH)
        kss, o = carve(arena, o, 3, HH)
        free = [(r_, O_TOK + HW * i) for r_ in (ring, wmix) for i in range((RING * PIECE - O_TOK) // HW)]
        free += [(arena, o + HW * i) for i in range((O_RKV - o) // HW)]
        free += [(ubuf, HW * i) for i in range(2400 // HW)]
        (tW, tA, eE, eP, eN, eR, eT, b1, kd, btil, Bbar, ktil, Kbar, sq) = (
            [carve(*free.pop(0), HW)[0] for z in range(2)] for _ in range(14))
        kkn, Oacc = ([carve(*free.pop(0), HW)[0] for t in range(3)] for _ in range(2))
        sraw, sout = (carve(*free.pop(0), HW)[0] for _ in range(2))
        x2, o = carve(arena, 0, 3, D)
        gb, o = carve(arena, o, 2, D)
        xn2, o = carve(arena, o, 3, D)
        assert o <= NA
        ytmp, o = carve(ubuf, 0, 2, BLK)
        mtmp, o = carve(ubuf, o, 2, 4, P)
        act, o = carve(arena, 0, FT, TOK)
        assert o <= NA
        UPW = TOK + 3
        up2, o = carve(ubuf, 0, 2, UPW)
        cv2, o = carve(ubuf, o, 2, TOK + 1)
        sg2, o = carve(ubuf, o, 2, TOK + 1)
        assert o <= 2400
        x3, o = carve(hf, 0, 3, D)
        gb2, o = carve(hf, o, 2, D)
        fg, o = carve(hf, o, D)
        ytmp2, _ = carve(ring, 0, 2, 512)
        ytmp1, _ = carve(arena, FT * TOK, 2, 256)
        junk2, _ = carve(arena, 0, D)

        X_dram = nc.dram_tensor("x_mid", [3, P, D], F32, kind="Internal").ap()
        E_dram = nc.dram_tensor("rpb_padded", [HA, 7, P], F32, kind="Internal").ap()
        EL = HA * 7 * P
        R_dram = nc.dram_tensor("rpb_rows", [GRID, EL], F32, kind="Internal").ap()

        s_const, s_x, s_vrow, s_lnrow = sem("s_const"), sem("s_x"), sem("s_vrow"), sem("s_lnrow")
        s_w = [sem(f"s_w{i}") for i in range(RING)]
        s_hi, s_lo = sem("s_hi"), sem("s_lo")
        s_blk, s_kd = sem("s_blk"), sem("s_kd")
        s_ah, s_al, s_c4, s_hm, s_hh, s_xs, s_x3 = (sem(n) for n in ("s_ah", "s_al", "s_c4", "s_hm", "s_hh", "s_xs", "s_x3"))
        s_cs, s_cyh, s_pvh, s_fh, s_hm2, s_hh2 = (sem(n) for n in ("s_cs", "s_cyh", "s_pvh", "s_fh", "s_hm2", "s_hh2"))
        s_vt, s_vc, s_ct = sem("s_vt"), sem("s_vc"), sem("s_ct")
        s_csig = sem("s_csig")
        s_ssq, s_rstd, s_xn, s_xt, s_xc = sem("s_ssq"), sem("s_rstd"), sem("s_xn"), sem("s_xt"), sem("s_xc")
        s_mrow, s_mcT, s_mcol, s_h = sem("s_mrow"), sem("s_mcT"), sem("s_mcol"), sem("s_h")
        s_eact, s_edve = sem("s_eact"), sem("s_edve")
        s_d, s_a = sem("s_d"), sem("s_a")
        s_rpl, s_rdp = sem("s_rpl"), sem("s_rdp")
        s_var, s_root = sem("s_var"), sem("s_root")
        s_pad = sem("s_pad")
        s_cbuf, s_cmean, s_ccen, s_csq, s_cvar, s_cn, s_cy = (sem(n) for n in (
            "s_cbuf", "s_cmean", "s_ccen", "s_csq", "s_cvar", "s_cn", "s_cy"))
        s_E0, s_E1, s_Bm, s_Bmask = sem("s_E0"), sem("s_E1"), sem("s_Bm"), sem("s_Bmask")
        s_cache, s_ckt, s_ckc, s_knt, s_knc, s_out = (sem(n) for n in (
            "s_cache", "s_ckt", "s_ckc", "s_knt", "s_knc", "s_out"))
        s_sc, s_sm, s_ex, s_nr, s_pt, s_ptc, s_pv, s_pvc = (sem(n) for n in (
            "s_sc", "s_sm", "s_ex", "s_nr", "s_pt", "s_ptc", "s_pv", "s_pvc"))
        s_par, s_parf, s_S0, s_sraw, s_sT = sem("s_par"), sem("s_parf"), sem("s_S0"), sem("s_sraw"), sem("s_sT")
        s_rexp2, s_rbon, s_rT0p, s_pc = sem("s_rexp2"), sem("s_rbon"), sem("s_rT0p"), sem("s_pc")
        (s_rlora, s_rpre, s_rsig, s_rcum, s_rexp, s_rtil, s_rbar, s_rtr, s_rtc, s_rA, s_rAm, s_rN, s_rNc, s_rT0,
         s_rAV, s_rAVc, s_rX, s_rXm, s_rTp, s_rTu, s_rZU, s_rZUc, s_rQM, s_rQMc, s_rSp, s_rS, s_rO, s_rdone,
         s_fg, s_fy, s_fT, s_fc, s_stT, s_stc, s_stout) = (sem(n) for n in (
             "s_rlora", "s_rpre", "s_rsig", "s_rcum", "s_rexp", "s_rtil", "s_rbar", "s_rtr", "s_rtc", "s_rA",
             "s_rAm", "s_rN", "s_rNc", "s_rT0", "s_rAV", "s_rAVc", "s_rX", "s_rXm", "s_rTp", "s_rTu", "s_rZU",
             "s_rZUc", "s_rQM", "s_rQMc", "s_rSp", "s_rS", "s_rO", "s_rdone", "s_fg", "s_fy", "s_fT", "s_fc",
             "s_stT", "s_stc", "s_stout"))
        s_x2, s_gbp, s_gbc, s_oc = sem("s_x2"), sem("s_gbp"), sem("s_gbc"), sem("s_oc")
        s_ssq2, s_xn2, s_xt2, s_h2 = sem("s_ssq2"), sem("s_xn2"), sem("s_xt2"), sem("s_h2")
        s_gb2p, s_gb2c = sem("s_gb2p"), sem("s_gb2c")
        s_uc, s_ucv, s_usg, s_uact = sem("s_uc"), sem("s_ucv"), sem("s_usg"), sem("s_uact")
        s_dc, s_fgl, s_fss, s_yf = sem("s_dc"), sem("s_fgl"), sem("s_fss"), sem("s_yf")

        def toks(t):
            return slice(P * t, P * t + P)

        def half(p):
            return slice(64 * p, 64 * p + 64)

        def width(n):
            kind, i, _ = STREAM[n // 2] if n < P_OUT else ("", 0, 0)
            return KQ * IN_BLOCKS[i][3] if kind == "in" else PART

        def arrived(n):
            w = width(n)
            return ring[:, (n // 2 % RING) * PIECE + (n % 2) * w:(n // 2 % RING) * PIECE + (n % 2 + 1) * w]

        def used(eng, n):
            if n < P_DOWN:
                eng.wait_ge(s_blk, n + 1)
            else:
                eng.wait_ge(s_kd, n - P_DOWN + 1)

        block = ctx.enter_context(nc.Block())

        @block.sync
        def _(sp):
            def load(n, src, k):
                if n >= RING:
                    sp.wait_ge(s_lo, 2 * (n - RING) + 2)
                at = (n % RING) * PIECE
                sp.dma_start(ring[:, at:at + 2 * width(2 * n)].rearrange("p (k c) -> p k c", k=k), src).then_inc(s_w[n % RING], 16)

            def load_piece(n, w, c0, cols, p):
                src = w[KP * P * p:KP * P * (p + 1), c0:c0 + cols]
                load(n, src.rearrange("(k p) c -> p k c", p=P), KP)

            def load_block(part, w, c0, cols):
                for p in range(2):
                    load_piece(part // 2 + p, w, c0, cols, p)

            sp.dma_start(consts[:, :], a["consts"]).then_inc(s_const, 16)
            for t, src in ((0, a["x_prompt"][0]), (1, a["x_sample"][0, 0:P]), (2, a["x_sample"][0, P:2 * P])):
                sp.dma_start(x[:, t, :], src).then_inc(s_x, 16)
            for n, (kind, i, p) in enumerate(STREAM):
                if kind == "mod":
                    load_piece(n, a["w_mod"][0], BLK * i, BLK, p)
                else:
                    load_piece(n, a["w_in"][0], IN_BLOCKS[i][2], IN_BLOCKS[i][3], p)
            sp.wait_ge(s_eact, evacs("act", len(ITEMS)))
            sp.dma_start(out["new_cache_v"][0, 0].rearrange("t h d -> t (h d)"), v_tok[:, 0, :]).then_inc(s_out, 16)
            sp.wait_ge(s_knc, 2)
            sp.dma_start(out["new_cache_k"][0, 0].rearrange("t h d -> t (h d)"), knew).then_inc(s_out, 16)
            for gr in range(GROUPS):
                cs = slice(HW * gr, HW * gr + HW)
                if gr == 0:
                    sp.wait_ge(s_pvc, len(ATT) // 2)
                    sp.wait_ge(s_out, 32)
                else:
                    sp.wait_ge(s_rbon, NG * gr)
                    sp.wait_ge(s_rlora, NG * gr)
                for i, src in enumerate((a["rwkv_w0"][0, 0:1, cs], a["rwkv_w0"][0, 1:2, cs],
                                         a["rwkv_a0"][0, 0:1, cs], a["rwkv_a0"][0, 1:2, cs],
                                         a["rwkv_k_k"][0:1, cs], a["rwkv_k_a"][0:1, cs],
                                         a["rwkv_r_k"].rearrange("l h d -> l (h d)")[0:1, cs])):
                    sp.dma_start(par[:, i, :], src.broadcast_to([P, HW])).then_inc(s_par, 16)
                sp.dma_start(par[:, 7, :], a["rwkv_w_lora"][0][:, :, cs].rearrange("d r c -> (d r) c")).then_inc(s_par, 16)
                sp.dma_start(par[:, 8, :], a["rwkv_a_lora"][0][:, :, cs].rearrange("d r c -> (d r) c")).then_inc(s_par, 16)
                if gr:
                    sp.wait_ge(s_sT, 2 * gr)
                for d in range(2):
                    src = a["state_fwd" if d == 0 else "state_bwd"][0, 0, HH * gr:HH * gr + HH]
                    sp.dma_start(sraw[half(d), :].rearrange("p (h k) -> p h k", h=HH),
                                 src.rearrange("h v k -> v h k")).then_inc(s_sraw, 16)
                if gr:
                    sp.wait_ge(s_fy, 3 * gr)
                    sp.wait_ge(s_fg, 3 * gr)
                sp.dma_start(par[:, 9, :], a["rwkv_ln_g"][0:1, cs].broadcast_to([P, HW])).then_inc(s_parf, 16)
                sp.dma_start(par[:, 10, :], a["rwkv_ln_b"][0:1, cs].broadcast_to([P, HW])).then_inc(s_parf, 16)
                sp.dma_start(par[:, 11, :], a["rwkv_g_lora"][0][:, cs]).then_inc(s_parf, 16)
                sp.wait_ge(s_stc, gr + 1)
                for d in range(2):
                    dst = out["new_state_fwd" if d == 0 else "new_state_bwd"][0, 0, HH * gr:HH * gr + HH]
                    sp.dma_start(dst.rearrange("h v k -> v h k"),
                                 sout[half(d), :].rearrange("p (h k) -> p h k", h=HH)).then_inc(s_stout, 16)
            sp.wait_ge(s_fc, 3 * GROUPS)
            for t, src in ((0, a["x_prompt"][0]), (1, a["x_sample"][0, 0:P]), (2, a["x_sample"][0, P:2 * P])):
                sp.dma_start(x2[:, t, :], src).then_inc(s_x2, 16)
            for j in range(D // BLK):
                load_block(P_OUT + PARTS * j, a["w_out"][0], BLK * j, BLK)
            for i in range(DFF // BLK):
                load_block(P_UP + 2 * PARTS * i, a["w_up"][0], BLK * i, BLK)
                if i == 0:
                    sp.wait_ge(s_oc, 3 * (D // BLK))
                    sp.dma_start(X_dram.rearrange("t p c -> p t c"), x2).then_inc(s_xs, 16)
                load_block(P_UP + 2 * PARTS * i + PARTS, a["w_up"][0], DFF + BLK * i, BLK)
            for q in range(2):
                for g in range(FT // DOWN_KT):
                    n = P_DOWN // 2 + q * (FT // DOWN_KT) + g
                    src = a["w_down"][0][DOWN_KT * P * g:DOWN_KT * P * (g + 1), DOWN_W * q:DOWN_W * (q + 1)]
                    load(n, src.rearrange("(k p) c -> p k c", p=P), DOWN_KT)
                    if q == 0 and g == RING:
                        used(sp, P_DOWN - 1)
                        sp.wait_ge(s_xs, 16)
                        sp.dma_start(x3, X_dram.rearrange("t p c -> p t c")).then_inc(s_x3, 16)
                        sp.dma_start(fg, a["final_g"].rearrange("(o c) -> o c", o=1).broadcast_to([P, D])).then_inc(s_fgl, 16)
            for t in range(3):
                sp.wait_ge(s_yf, t + 1)
                dst = out["y_prompt"][0] if t == 0 else out["y_sample"][0, P * (t - 1):P * t]
                sp.dma_start(dst, x3[:, t, :]).then_inc(s_out, 16)
            sp.wait_ge(s_out, 16 * 5)
            sp.wait_ge(s_stout, 16 * 2 * GROUPS)

        @block.gpsimd
        def _(pool):
            pool.dma_start(vrow[0:KT, 0, :], a["c_ctx"].rearrange("(k p) -> k p", p=P)).then_inc(s_vrow, 16)
            pool.dma_start(vrow[KT:2 * KT, 0, :], a["c"][0].rearrange("(k p) -> k p", p=P)).then_inc(s_vrow, 16)
            pool.dma_start(vrow[0:16, 1, :], a["norm1_g"][0].rearrange("(k p) -> k p", p=P)).then_inc(s_vrow, 16)
            pool.dma_start(vrow[16:32, 1, :], a["norm2_g"][0].rearrange("(k p) -> k p", p=P)).then_inc(s_vrow, 16)
            pool.dma_start(vrow[32:128, 1, :], a["b_mod"][0].rearrange("(k p) -> k p", p=P)).then_inc(s_vrow, 16)
            pool.dma_start(vrow[0:124, 2, :], a["conv_w"][0].rearrange("j (k p) -> (j k) p", p=P)).then_inc(s_vrow, 16)
            pool.dma_start(vrow[0:88, 3, :], a["ffn_conv_w"][0, 0:2].rearrange("j (k p) -> (j k) p", p=P)).then_inc(s_vrow, 16)
            pool.dma_start(vrow[88:92, 3, :], a["conv_b"][0].rearrange("(k p) -> k p", p=P)).then_inc(s_vrow, 16)
            pool.dma_start(vrow[92:96, 3, :], a["conv_ln_g"][0].rearrange("(k p) -> k p", p=P)).then_inc(s_vrow, 16)
            pool.dma_start(vrow[96:100, 3, :], a["conv_ln_b"][0].rearrange("(k p) -> k p", p=P)).then_inc(s_vrow, 16)
            pool.dma_start(vrow[0:44, 4, :], a["ffn_conv_w"][0, 2].rearrange("(k p) -> k p", p=P)).then_inc(s_vrow, 16)
            pool.dma_start(vrow[44:88, 4, :], a["ffn_conv_b"][0].rearrange("(k p) -> k p", p=P)).then_inc(s_vrow, 16)
            pool.wait_ge(s_const, 16)
            pool.dma_start(E_dram.rearrange("h r c -> (h r) c"),
                           consts[0:HA * 7, C_ZERO:C_ZERO + P]).then_inc(s_E0, 16)
            pool.wait_ge(s_E0, 16)
            pool.dma_start(E_dram[:, :, 48:79], a["rpb"][0][:, 4:11, :]).then_inc(s_E1, 16)
            pool.wait_ge(s_E1, 16)
            pool.dma_start(R_dram, bass.AP(E_dram.tensor, 0, [[0, GRID], [1, EL]])).then_inc(s_E1, 16)
            pool.wait_ge(s_E1, 32)
            pool.wait_ge(s_blk, P_OUT)
            pool.dma_start(cv, a["cache_v"][0, 0].rearrange("t h d -> t (h d)")).then_inc(s_cache, 16)
            pool.dma_start(ck, a["cache_k"][0, 0].rearrange("t h d -> t (h d)")).then_inc(s_cache, 16)
            for i in range(2):
                for h in range(HA):
                    src = bass.AP(R_dram.tensor, h * 7 * P + (1 - i) * P + 63, [[EL - 1, GRID], [P, 6], [1, GRID]])
                    pool.dma_start(Bm[half(i), h], src).then_inc(s_Bm, 16)
            pool.wait_ge(s_cache, 32)
            for v in range(NU):
                z = v % 2
                pool.wait_ge(s_rexp2, v + 1)
                pool.wait_ge(s_rtil, v + 1)
                nc.gpsimd.tensor_copy(ZA[z][:, :, 0, :], eE[z].rearrange("p (h c) -> p h c", h=HH))
                nc.gpsimd.tensor_tensor(Bbar[z], b1[z], eR[z], ALU.mult)
                nc.gpsimd.tensor_tensor(Kbar[z], kd[z], eR[z], ALU.mult).then_inc(s_rpl, 1)
                pool.wait_ge(s_rAm, HH * (v + 1))
                nc.gpsimd.tensor_tensor(TTm[z], Am[z][:, :, 0, :], consts[:, C_SAME2:C_SAME2 + P].unsqueeze(1).broadcast_to([P, HH, P]),
                                        ALU.mult).then_inc(s_pc, 1)
                pool.wait_ge(s_pc, v + 1)
                nc.gpsimd.tensor_tensor(TTm[z], TTm[z], ident.unsqueeze(1).broadcast_to([P, HH, P]), ALU.add).then_inc(s_rT0p, 1)

        @block.tensor
        def _(pe):
            mm, tr = nc.tensor.matmul, nc.tensor.transpose

            def three(o_, lh, ll, rh, rl, start, stop):
                mm(o_, lh, rh, start=start, stop=False)
                mm(o_, lh, rl, start=False, stop=False)
                return mm(o_, ll, rh, start=False, stop=stop)

            def parts(n, k):
                w = width(n)
                return (wh[n % SPLITS][:, 0:w].rearrange("p (k c) -> p k c", k=k),
                        wl[n % SPLITS][:, 0:w].rearrange("p (k c) -> p k c", k=k))

            pe.wait_ge(s_const, 16)
            pe.wait_ge(s_vrow, 16 * 12)
            for g, rows in enumerate((2 * KT, 128, 124, 100, 88)):
                tr(ps[:, g, 0:rows], vrow[0:rows, g, :], ident[0:rows, 0:rows]).then_inc(s_vt, 1)
            for t in range(3):
                pe.wait_ge(s_xn, t + 1)
                for g in range(4):
                    n = 4 * t + g
                    bank = 5 + n % 3
                    if n >= 3:
                        pe.wait_ge(s_xc, n - 2)
                    for j in range(4):
                        last = tr(ps[:, bank, toks(j)], xn[:, t, toks(4 * g + j)], ident)
                    last.then_inc(s_xt, 1)

            def mod_part(n, i, p):
                if n % 2 == 0 and p == 0 and i >= 2:
                    if i - 2 < N_EARLY:
                        pe.wait_ge(s_mrow, i - 1)
                    else:
                        pe.wait_ge(s_mcol, i - 1)
                w_hi, w_lo = parts(n, KQ)
                for k in range(KQ):
                    q = KP * p + KQ * (n % 2) + k
                    c4 = c4_t[:, 4 * q:4 * q + 4]
                    mm(ps[0:4, i % 2, 0:BLK], c4, w_hi[:, k, :], start=(q == 0), stop=False)
                    last = mm(ps[0:4, i % 2, 0:BLK], c4, w_lo[:, k, :], start=False, stop=(q == KT - 1))
                last.then_inc(s_blk, 1)

            def mod_cols(i):
                pe.wait_ge(s_mrow, i + 1)
                if i >= 2:
                    pe.wait_ge(s_mcol, i - 1)
                bank, at = (2 + i % 2, 0) if i < N_EARLY else (i % 2, BLK)
                for j in range(2):
                    last = mm(ps[:, bank, at + 2 * j:at + 2 * j + 2], modrow[0:4, i % 2, toks(j)], consts[0:4, C_SEL:C_SEL + 2], start=True, stop=True)
                last.then_inc(s_mcT, 1)

            def in_part(n, j, p):
                kind, what, c0, w, _ = IN_BLOCKS[j]
                m = next(m_ for m_, it in enumerate(ITEMS) if it[0] == j)
                tiles = 3 if kind == "tok" else w // P
                if n % 2 == 0 and p == 0:
                    if j == 0:
                        pe.wait_ge(s_h, 1)
                        pe.wait_ge(s_mcol, N_EARLY)
                    for s in range(tiles):
                        if m + s >= BANKS:
                            e = ITEMS[m + s - BANKS][5]
                            pe.wait_ge(s_eact if e == "act" else s_edve, evacs(e, m + s - BANKS + 1))
                w_hi, w_lo = parts(n, KQ)
                for s in range(tiles):
                    for k in range(KQ):
                        q = KP * p + KQ * (n % 2) + k
                        at = dict(start=(q == 0), stop=(q == KT - 1))
                        if kind == "tok":
                            last = three(ps[:, bank_of(m + s), 0:w], hh[:, q, toks(s)], hl[:, q, toks(s)],
                                         w_hi[:, k, :], w_lo[:, k, :], **at)
                        else:
                            last = three(ps[:, bank_of(m + s), 0:TOK], w_hi[:, k, toks(s)], w_lo[:, k, toks(s)],
                                         hh[:, q, :], hl[:, q, :], **at)
                last.then_inc(s_blk, 1)

            pe.wait_ge(s_vc, 4)
            pe.wait_ge(s_c4, 2)
            for n in range(P_OUT + 3):
                if n < P_OUT:
                    kind, i, p = STREAM[n // 2]
                    pe.wait_ge(s_lo, n + 1)
                    (mod_part if kind == "mod" else in_part)(n, i, p)
                if n - 3 in MOD_LAST:
                    mod_cols(MOD_LAST[n - 3])

            pe.wait_ge(s_eact, evacs("act", len(ITEMS)))
            pe.wait_ge(s_edve, evacs("dve", len(ITEMS)))
            pe.wait_ge(s_mcol, N_MOD)
            pe.wait_ge(s_cbuf, 1)
            for t in range(BT):
                last = mm(ps[:, 0, 0:CW], consts[:, C_MEAN:C_MEAN + P], cbuf[:, t, :], start=(t == 0), stop=(t == BT - 1))
            last.then_inc(s_cmean, 1)
            pe.wait_ge(s_csq, 1)
            for t in range(BT):
                last = mm(ps[:, 1, 0:CW], consts[:, C_MEAN:C_MEAN + P], csq[:, t, :], start=(t == 0), stop=(t == BT - 1))
            last.then_inc(s_cvar, 1)

            pe.wait_ge(s_cache, 32)
            for i in range(6):
                last = tr(ps[:, 6 + i // 3, toks(i % 3)], ck[:, toks(i)], ident)
            last.then_inc(s_ckt, 1)
            for i in range(6):
                last = tr(ps[:, 4 + i // 3, toks(i % 3)], qkT[:, 6 + i, 0:P], ident)
            last.then_inc(s_knt, 1)
            pe.wait_ge(s_cn, 1)
            pe.wait_ge(s_cyh, 8)
            pe.wait_ge(s_ckc, 2)
            pe.wait_ge(s_knc, 2)

            def scores(u):
                t, h = ATT[u]
                r = half(h % 2)
                if u >= 2:
                    pe.wait_ge(s_sm, u - 1)
                bank = u % 2
                q = qkT[r, h // 2, toks(t)]
                if t == 0:
                    last = mm(ps[:, bank, 0:P], q, qkT[r, 6 + h // 2, 0:P], start=True, stop=True)
                else:
                    mm(ps[:, bank, 0:2 * P], q, qkT[r, 6 + h // 2, P:TOK], start=True, stop=True)
                    last = mm(ps[:, bank, 2 * P:TOK], q, ckT[r, h // 2, :], start=True, stop=True)
                last.then_inc(s_sc, 1)

            def turn(u):
                t, h = ATT[u]
                pe.wait_ge(s_nr, u + 1)
                if u >= 2:
                    pe.wait_ge(s_ptc, u - 1)
                for k in range(1 if t == 0 else 3):
                    last = tr(ps[:, 2 + u % 2, toks(k)], ss[:, u % 3, toks(k)], ident)
                last.then_inc(s_pt, 1)

            def pv(u):
                t, h = ATT[u]
                pe.wait_ge(s_ptc, u + 1)
                if u >= 4 and h % 2 == 0:
                    pe.wait_ge(s_pvc, u // 2 - 1)
                o_ = ps[half(h % 2), 4 + (u // 2) % 2, 0:P]
                keys = [v_tok[:, 0, :]] if t == 0 else [v_tok[:, 1, :], v_tok[:, 2, :], cv]
                for k, vv in enumerate(keys):
                    last = mm(o_, vv[:, HD * h:HD * h + HD], PT[:, u % 2, toks(k)], start=(k == 0), stop=(k == len(keys) - 1))
                last.then_inc(s_pv, 1)

            for u in range(len(ATT) + 3):
                if u < len(ATT):
                    scores(u)
                if 0 <= u - 2 < len(ATT):
                    turn(u - 2)
                if 0 <= u - 3:
                    pv(u - 3)
            pe.wait_ge(s_pvc, len(ATT) // 2)

            masks = [consts[:, C_M4 + 512 * d:C_M4 + 512 * d + 512] for d in range(2)]

            def rwkv_step(u, step, l, v):
                z, gr, t, d, s0, first = unit(v)
                spare = 4 * (u % 2) + 3
                vals = rkv[:, t, 1536 + HW * gr:1536 + HW * gr + HW]
                if step == "X":
                    if l == 0:
                        pe.wait_ge(s_rT0, v + 1)
                        pe.wait_ge(s_rT0p, v + 1)
                        pe.wait_ge(s_rAVc, v + 1)
                    else:
                        pe.wait_ge(s_rTu, LEVELS * v + l)
                    for h in range(HH):
                        last = mm(ps[:, 4 * z, toks(h)], Nm[z][:, h, :], TTm[z][:, h, :], start=True, stop=True)
                    last.then_inc(s_rX, 1)
                elif step == "T":
                    pe.wait_ge(s_rXm, LEVELS * v + l + 1)
                    for h in range(HH):
                        if l < LEVELS - 1:
                            mm(ps[:, 4 * z + 1, toks(h)], Xm[z][:, h, :], Tm[z][:, h, :], start=True, stop=True)
                        last = mm(ps[:, 4 * z + 2, toks(h)], Tm[z][:, h, :], Xm[z][:, h, :], start=True, stop=True)
                    last.then_inc(s_rTp, 1)
                elif step == "ZU":
                    pe.wait_ge(s_rTu, LEVELS * (v + 1))
                    pe.wait_ge(s_rpl, v + 1)
                    for h in range(HH):
                        last = mm(ps[:, 4 * z + 3, toks(h)], TTm[z][:, h, :], ZA[z][:, h, :, :].rearrange("p a b -> p (a b)"), start=True, stop=True)
                    last.then_inc(s_rZU, 1)
                elif step == "QM":
                    pe.wait_ge(s_rZUc, v + 1)
                    for h in range(HH):
                        r, i = half(h % 2), h // 2
                        mm(ps[r, 4 * z, toks(i)], ZU[z][:, h, 0, :], Am[z][:, h, 1, :], start=True, stop=True)
                    for p in range(2):
                        c = half(p)
                        for h in range(HH):
                            r, i = half(h % 2), h // 2
                            hs = slice(HD * h, HD * h + HD)
                            m_, s_ = (slice(q + HD * i, q + HD * i + HD) for q in (0, P))
                            mm(ps[r, 4 * z + 1 + p, m_], ZU[z][c, h, 0, :], Bbar[z][c, hs], start=True, stop=True)
                            mm(ps[r, 4 * z + 1 + p, s_], Bbar[z][c, hs], ZU[z][c, h, 1, :], start=True, stop=False)
                            last = mm(ps[r, 4 * z + 1 + p, s_], Kbar[z][c, hs], vals[c, hs], start=False, stop=True)
                    last.then_inc(s_rQM, 1)
                elif step == "S":
                    c = l if d == 0 else 1 - l
                    if l == 0:
                        pe.wait_ge(s_rQMc, v + 1)
                        pe.wait_ge(s_S0, 2 * gr + 1 + (v % NG >= 2))
                        if v:
                            pe.wait_ge(s_rS, 2 * v)
                    else:
                        pe.wait_ge(s_rS, 2 * v + 1)
                    for h in range(HH):
                        r, i = half(h % 2), h // 2
                        last = mm(ps[r, 4 * z + 3 * (1 - h % 2), HD * i:HD * i + HD], MT[z][r, c, i, :], S[r, 5 * d + s0 + l, i, :], start=True, stop=True)
                    last.then_inc(s_rSp, 1)
                elif step == "O":
                    for h in range(HH):
                        r, i = half(h % 2), h // 2
                        b_ = 4 * z + 1 + h % 2
                        o_ = ps[:, b_, HD * i:HD * i + HD]
                        mm(o_, Am[z][:, h, 1, :], ZU[z][:, h, 1, :], start=True, stop=False)
                        for c in range(2):
                            s = c if d == 0 else 1 - c
                            mm(ps[half(c), b_, HD * i:HD * i + HD], QT[z][r, i, half(c)], S[r, 5 * d + s0 + s, i, :], start=False, stop=False)
                        last = mm(o_, Am[z][:, h, 3, :], vals[:, HD * h:HD * h + HD], start=False, stop=True)
                    last.then_inc(s_rO, 1)
                elif step == "lora":
                    pe.wait_ge(s_par, 16 * 9 * (gr + 1))
                    mm(ps[:, spare, 0:HW], lora[half(d), 0, toks(t)], par[half(d), 7, :], start=True, stop=True)
                    mm(ps[:, spare, HW:2 * HW], lora[half(d), 1, toks(t)], par[half(d), 8, :], start=True, stop=True).then_inc(s_rlora, 1)
                elif step == "cum" and l == 0:
                    pe.wait_ge(s_rsig, v + 1)
                    mm(ps[:, spare, 0:HW], masks[d][:, P:2 * P], tW[z], start=True, stop=True)
                    mm(ps[:, spare, HW:2 * HW], masks[d][:, 0:P], tW[z], start=True, stop=True).then_inc(s_rcum, 1)
                elif step == "cum":
                    pe.wait_ge(s_rexp, v + 1)
                    mm(ps[:, spare, 0:HW], masks[1 - d][:, 0:P], tW[z], start=True, stop=True)
                    mm(ps[:, spare, HW:2 * HW], consts[:, C_BONES:C_BONES + P], tW[z], start=True, stop=True).then_inc(s_rcum, 1)
                elif step == "tr":
                    pe.wait_ge(s_rtil, v + 1)
                    if v >= 2:
                        pe.wait_ge(s_rdone, v - 1)
                    for i in range(CT):
                        tr(ps[:, 4 * z, toks(2 * i)], eE[z][:, toks(i)], ident)
                        tr(ps[:, 4 * z, toks(2 * i + 1)], eP[z][:, toks(i)], ident)
                    for i in range(CT):
                        tr(ps[:, 4 * z + 3, toks(i)], btil[z][:, toks(i)], ident)
                        last = tr(ps[:, 4 * z + 3, toks(CT + i)], ktil[z][:, toks(i)], ident)
                    last.then_inc(s_rtr, 1)
                elif step == "A":
                    pe.wait_ge(s_rtc, v + 1)
                    for h in (2 * l, 2 * l + 1):
                        r, i = half(h % 2), h // 2
                        if h >= 2:
                            pe.wait_ge(s_rAm, HH * v + h - 1)
                        zr = zrT[z][r, i, :, :].rearrange("p a b -> p (a b)")
                        mm(ps[:, 4 * z + 1 + h % 2, 0:2 * P], bT[z][r, i, :], zr, start=True, stop=True)
                        mm(ps[:, 4 * z + 1 + h % 2, 2 * P:4 * P], kT[z][r, i, :], zr, start=True, stop=True).then_inc(s_rA, 1)
                elif step == "N":
                    for h in range(HH):
                        pe.wait_ge(s_rAm, HH * v + h + 1)
                        last = tr(ps[:, 4 * z + 3, toks(h)], Am[z][:, h, 0, :], ident)
                    last.then_inc(s_rN, 1)
                    for h in range(HH):
                        last = mm(ps[:, 4 * z, HD * h:HD * h + HD], Am[z][:, h, 2, :], vals[:, HD * h:HD * h + HD], start=True, stop=True)
                    last.then_inc(s_rAV, 1)
                elif step == "out":
                    pe.wait_ge(s_rexp2, min(v + 2, NU))
                    pe.wait_ge(s_rS, 2 * v)
                    for dd in range(2):
                        for i in range(CT):
                            last = mm(ps[half(dd), spare, toks(i)], S[:, 5 * dd + 2, i, :], ident, start=True, stop=True)
                    last.then_inc(s_stT, 1)
                elif step == "in":
                    pe.wait_ge(s_sraw, 32 * (gr + 1))
                    pe.wait_ge(s_stc, gr + 1)
                    for dd in range(2):
                        if dd:
                            pe.wait_ge(s_sT, 2 * gr + 1)
                        for i in range(CT):
                            last = mm(ps[:, spare, (CT * dd + i) * HD:(CT * dd + i + 1) * HD], sraw[half(dd), toks(i)],
                                      ident[half(dd), half(dd)], start=True, stop=True)
                        last.then_inc(s_sT, 1)
                elif step == "F" and l == 1:
                    pe.wait_ge(s_parf, 16 * 3 * (gr + 1))
                    pe.wait_ge(s_rexp2, min(v + 4, NU))
                    mm(ps[:, spare, 0:HW], lora[:, 2, toks(FINAL[v % NG][1])], par[:, 11, :], start=True, stop=True).then_inc(s_fg, 1)
                elif step == "F" and l == 2:
                    w_, t_, _ = FINAL[v % NG]
                    pe.wait_ge(s_fy, 3 * gr + w_ + 1)
                    for i in range(CT):
                        last = tr(ps[:, spare, toks(CT + i)], Oacc[t_][:, toks(i)], ident)
                    last.then_inc(s_fT, 1)

            for u in PERIODS:
                for step in steps(u):
                    rwkv_step(u, *step)
            pe.wait_ge(s_fc, 3 * GROUPS)

            def gate_rows(col0, ready, read):
                for n in range(8):
                    g, q = n // 4, n % 4
                    if n >= 2:
                        pe.wait_ge(read, n - 1)
                    for j in range(4):
                        col = modcol[:, col0 + 4 * q + j, g:g + 1].broadcast_to([P, P])
                        last = mm(ps[:, 6 + n % 2, toks(j)], col, ident, start=True, stop=True)
                    last.then_inc(ready, 1)

            gate_rows(2 * KT, s_gbp, s_gbc)
            for j in range(D // BLK):
                for p in range(PARTS):
                    n = P_OUT + PARTS * j + p
                    pe.wait_ge(s_lo, n + 1)
                    w_hi, w_lo = parts(n, KQ)
                    for t in range(3):
                        if j >= 2 and p == 0:
                            pe.wait_ge(s_oc, 3 * (j - 2) + t + 1)
                        for k in range(KQ):
                            q = KQ * p + k
                            last = three(ps[:, 3 * (j % 2) + t, 0:BLK], yh[:, q, toks(t)], yl[:, q, toks(t)],
                                         w_hi[:, k, :], w_lo[:, k, :], start=(q == 0), stop=(q == KT - 1))
                    last.then_inc(s_blk, 1)
            pe.wait_ge(s_oc, 3 * (D // BLK))
            for t in range(3):
                pe.wait_ge(s_xn2, t + 1)
                for g in range(4):
                    n = 4 * t + g
                    if n >= 4:
                        pe.wait_ge(s_hm2, n - 3)
                    for j in range(4):
                        last = tr(ps[:, n % 4, toks(j)], xn2[:, t, toks(4 * g + j)], ident)
                    last.then_inc(s_xt2, 1)
            pe.wait_ge(s_h2, 12)
            for i in range(DFF // BLK):
                for w in range(2):
                    if i >= 2:
                        pe.wait_ge(s_uc if w == 0 else s_uact, 2 * (i - 1))
                    for p in range(PARTS):
                        n = P_UP + PARTS * (2 * i + w) + p
                        pe.wait_ge(s_lo, n + 1)
                        w_hi, w_lo = parts(n, KQ)
                        for s in range(2):
                            for k in range(KQ):
                                q = KQ * p + k
                                last = three(ps[:, 4 * (i % 2) + 2 * w + s, 0:TOK], w_hi[:, k, toks(s)], w_lo[:, k, toks(s)],
                                             hh[:, q, :], hl[:, q, :], start=(q == 0), stop=(q == KT - 1))
                        last.then_inc(s_blk, 1)
            pe.wait_ge(s_uact, FT)
            gate_rows(5 * KT, s_gb2p, s_gb2c)
            pe.wait_ge(s_gb2c, 8)
            for q in range(2):
                for f in range(FT):
                    i = q * FT + f
                    n = P_DOWN + i
                    pe.wait_ge(s_lo, n + 1)
                    pe.wait_ge(s_al, i + 1)
                    w_hi, w_lo = parts(n, 1)
                    for t in range(3):
                        for c in range(2):
                            if q == 1 and f == 0 and 2 * t + c >= 2:
                                pe.wait_ge(s_dc, 2 * t + c - 1)
                            cs = slice(512 * c, 512 * c + 512)
                            last = three(ps[:, (6 * q + 2 * t + c) % 8, :], ah[i % 3][:, toks(t)], al[i % 3][:, toks(t)],
                                         w_hi[:, 0, cs], w_lo[:, 0, cs], start=(f == 0), stop=(f == FT - 1))
                    last.then_inc(s_kd, 1)

        @block.scalar
        def _(ac):
            AC = nc.scalar.activation
            cnt = [0]

            def link(ins):
                cnt[0] += 1
                ins.then_inc(s_a, 1)
                ac.wait_ge(s_a, cnt[0])

            roots = [0]

            def root(ap):
                roots[0] += 1
                ac.wait_ge(s_var, roots[0])
                AC(ap, ap, ACT.Sqrt).then_inc(s_root, 1)

            def hi(n):
                ac.wait_ge(s_w[n // 2 % RING], 16 * (n // 2 // RING + 1))
                if n >= SPLITS:
                    used(ac, n - SPLITS)
                AC(wh[n % SPLITS][:, 0:width(n)], arrived(n), ACT.Copy).then_inc(s_hi, 1)

            for t in range(3):
                ac.wait_ge(s_x, 48)
                AC(junk, x[:, t, :], ACT.Square, accum_out=stat[:, t:t + 1]).then_inc(s_ssq, 1)
                ac.wait_ge(s_ssq, t + 1)
            ac.wait_ge(s_vt, 1)
            AC(csig, ps[:, 0, 0:2 * KT], ACT.Sigmoid).then_inc(s_csig, 1)
            root(stat[:, 4:7])
            ac.wait_ge(s_ct, 1)
            c4v = c4_t[:, :].rearrange("p (k r g) -> p r k g", r=2, g=2)
            AC(c4v[:, 0], cT.rearrange("p (g k) -> p k g", g=2), ACT.Copy).then_inc(s_c4, 1)
            ac.wait_ge(s_xn, 3)
            for n in range(12):
                t, g = n // 4, n % 4
                ac.wait_ge(s_xt, n + 1)
                AC(xT[:, 4 * g:4 * g + 4, toks(t)], ps[:, 5 + n % 3, :].rearrange("p (j c) -> p j c", j=4), ACT.Copy).then_inc(s_xc, 1)

            def mod_row(i):
                ac.wait_ge(s_blk, MOD_END[i])
                if i >= 2:
                    ac.wait_ge(s_mcT, i - 1)
                AC(modrow[0:4, i % 2, :], ps[0:4, i % 2, 0:BLK], ACT.Copy).then_inc(s_mrow, 1)

            for n in range(P_MIX + SPLITS):
                hi(n)
                if n - SPLITS in MOD_LAST:
                    mod_row(MOD_LAST[n - SPLITS])
            for q in range(4):
                ac.wait_ge(s_hm, q + 1)
                AC(hh[:, 4 * q:4 * q + 4, :], xT[:, 4 * q:4 * q + 4, :], ACT.Copy).then_inc(s_hh, 1)

            def take_items(b):
                for m, (n, kind, what, j, s, eng) in enumerate(ITEMS):
                    if eng != "act" or n != b:
                        continue
                    ac.wait_ge(s_blk, IN_END[n])
                    if what == "q":
                        AC(qkT[:, j + s, :], ps[:, bank_of(m), 0:TOK], ACT.Copy).then_inc(s_eact, 1)
                    elif what == "v":
                        AC(v_tok[:, s, BLK * j:BLK * j + BLK], ps[:, bank_of(m), 0:BLK], ACT.Copy).then_inc(s_eact, 1)
                    elif what == "rkv":
                        AC(rkv[:, s, BLK * j:BLK * j + BLK], ps[:, bank_of(m), 0:BLK], ACT.Copy).then_inc(s_eact, 1)
                    elif what == "glu_b":
                        if j:
                            ac.wait_ge(s_edve, evacs("dve", m))
                        AC(sgt[:, s, :], ps[:, bank_of(m), 0:TOK], ACT.Sigmoid).then_inc(s_eact, 1)
                    else:
                        f = (ACT.Tanh, ACT.Copy, ACT.Sigmoid)[j + s]
                        AC(lora[:, j + s, :], ps[:, bank_of(m), 0:TOK], f).then_inc(s_eact, 1)

            for n in range(P_MIX + SPLITS, P_OUT + SPLITS):
                if n < P_OUT:
                    hi(n)
                if n - SPLITS in MOD_LAST:
                    mod_row(MOD_LAST[n - SPLITS])
                if n - SPLITS in IN_LAST:
                    take_items(IN_LAST[n - SPLITS])
            ac.wait_ge(s_ccen, 1)
            AC(csq, cbuf, ACT.Square).then_inc(s_csq, 1)
            ac.wait_ge(s_ckt, 1)
            for i in range(2):
                AC(ckT[:, 3 * i:3 * i + 3, :], ps[:, 6 + i, 0:TOK].rearrange("p (j c) -> p j c", j=3), ACT.Copy).then_inc(s_ckc, 1)
            ac.wait_ge(s_knt, 1)
            for i in range(2):
                AC(knew[:, TOK * i:TOK * i + TOK], ps[:, 4 + i, 0:TOK], ACT.Copy).then_inc(s_knc, 1)
            root(crstd)
            ac.wait_ge(s_cn, 1)
            for t in range(BT):
                AC(cbuf[:, t, :], cbuf[:, t, :], ACT.Silu,
                   scale=vcol[:, 2, 92 + t:93 + t], bias=vcol[:, 2, 96 + t:97 + t]).then_inc(s_cs, 1)
            ac.wait_ge(s_blk, P_OUT)
            for t in range(BT):
                ac.wait_ge(s_cs, t + 1)
                for (a0, b0, n) in ((0, 0, P), (P + PADC, P, 2 * P)):
                    AC(yh[:, 6 + t, b0:b0 + n], cbuf[:, t, a0:a0 + n], ACT.Copy).then_inc(s_cy, 1)

            def expo(u):
                t, h = ATT[u]
                n = P if t == 0 else TOK
                ac.wait_ge(s_sm, u + 1)
                AC(ss[:, u % 3, 0:n], ss[:, u % 3, 0:n], ACT.Exp, bias=stat[:, 8 + u % 4:9 + u % 4],
                   accum_out=stat[:, 16 + u % 4:17 + u % 4]).then_inc(s_ex, 1)

            def take(u):
                t, h = ATT[u]
                n = P if t == 0 else TOK
                ac.wait_ge(s_pt, u + 1)
                if u >= 2:
                    ac.wait_ge(s_pv, u - 1)
                AC(PT[:, u % 2, 0:n], ps[:, 2 + u % 2, 0:n], ACT.Copy).then_inc(s_ptc, 1)

            def result(u):
                t, h = ATT[u]
                ac.wait_ge(s_pv, u + 1)
                AC(yh[:, h // 2, toks(t)], ps[:, 4 + (u // 2) % 2, 0:P], ACT.Copy).then_inc(s_pvh, 1)

            for u in range(len(ATT) + 3):
                if u < len(ATT):
                    expo(u)
                if 0 <= u - 2 < len(ATT):
                    take(u - 2)
                if 0 <= u - 3 and (u - 3) % 2 == 1:
                    result(u - 3)

            def mats(b):
                return ps[:, b, :].rearrange("p (j c) -> p j c", c=P)

            def rwkv_step(u, step, l, v):
                z, gr, t, d, s0, first = unit(v)
                spare = 4 * (u % 2) + 3
                if step == "lora":
                    ac.wait_ge(s_rpre, v + 1)
                    AC(tW[z], tW[z], ACT.Sigmoid)
                    AC(tA[z], tA[z], ACT.Sigmoid).then_inc(s_rsig, 1)
                elif step == "kk":
                    root(kss)
                elif step == "cum" and l == 0:
                    if v >= 2:
                        ac.wait_ge(s_rpl, v - 1)
                    ac.wait_ge(s_rcum, 2 * v + 1)
                    AC(eE[z], ps[:, spare, HW:2 * HW], ACT.Exp, scale=-DECAY)
                    AC(eP[z], ps[:, spare, 0:HW], ACT.Exp, scale=-DECAY)
                    AC(eN[z], ps[:, spare, 0:HW], ACT.Exp, scale=DECAY).then_inc(s_rexp, 1)
                elif step == "cum":
                    ac.wait_ge(s_rcum, 2 * v + 2)
                    AC(eR[z], ps[:, spare, 0:HW], ACT.Exp, scale=-DECAY)
                    AC(eT[z], ps[:, spare, HW:2 * HW], ACT.Exp, scale=-DECAY).then_inc(s_rexp2, 1)
                elif step == "tr":
                    ac.wait_ge(s_rtr, v + 1)
                    AC(zrT[z].rearrange("p i a c -> p (i a c)"), ps[:, 4 * z, :], ACT.Copy)
                    AC(bT[z], mats(4 * z + 3)[:, 0:CT], ACT.Copy)
                    AC(kT[z], mats(4 * z + 3)[:, CT:2 * CT], ACT.Copy).then_inc(s_rtc, 1)
                elif step == "N":
                    ac.wait_ge(s_rN, v + 1)
                    AC(Nm[z], mats(4 * z + 3), ACT.Copy).then_inc(s_rNc, 1)
                    ac.wait_ge(s_rpl, v + 1)
                    ac.wait_ge(s_rAV, v + 1)
                    AC(ZA[z][:, :, 1, :], ps[:, 4 * z, 0:HW].rearrange("p (h c) -> p h c", h=HH), ACT.Copy).then_inc(s_rAVc, 1)
                elif step == "ZU":
                    ac.wait_ge(s_rZU, v + 1)
                    AC(ZU[z].rearrange("p h a c -> p (h a c)"), ps[:, 4 * z + 3, :], ACT.Copy).then_inc(s_rZUc, 1)
                elif step == "out":
                    ac.wait_ge(s_stT, gr + 1)
                    if gr:
                        ac.wait_ge(s_stout, 32 * gr)
                    AC(sout, ps[:, spare, 0:HW], ACT.Copy).then_inc(s_stc, 1)
                elif step == "F" and l == 0:
                    root(st6[:, 3, :])
                elif step == "F" and l == 2:
                    w_, t_, _ = FINAL[v % NG]
                    ac.wait_ge(s_fT, 3 * gr + w_ + 1)
                    AC(yh[:, 10 + CT * gr:10 + CT * (gr + 1), toks(t_)], mats(spare)[:, CT:2 * CT], ACT.Copy).then_inc(s_fh, 1)

            for u in PERIODS:
                for step in steps(u):
                    rwkv_step(u, *step)

            for n in range(8):
                ac.wait_ge(s_gbp, n + 1)
                AC(gb[:, n // 4, 512 * (n % 4):512 * (n % 4) + 512], ps[:, 6 + n % 2, :], ACT.Copy).then_inc(s_gbc, 1)
            for n in range(P_OUT, P_UP):
                hi(n)
            ac.wait_ge(s_oc, 3 * (D // BLK))
            for t in range(3):
                AC(xn2[:, t, :], x2[:, t, :], ACT.Square, accum_out=stat[:, 24 + t:25 + t]).then_inc(s_ssq2, 1)
            root(stat[:, 28:31])
            for n in range(12):
                ac.wait_ge(s_hm2, n + 1)
                AC(hh[:, 4 * (n % 4):4 * (n % 4) + 4, toks(n // 4)], mtmp[:, n % 2], ACT.Copy).then_inc(s_hh2, 1)
            for b in range(2 * (DFF // BLK) + 1):
                if b < 2 * (DFF // BLK):
                    for p in range(PARTS):
                        hi(P_UP + PARTS * b + p)
                if b % 2:
                    i = b // 2
                    ac.wait_ge(s_blk, P_UP + PARTS * b)
                    ac.wait_ge(s_pad, 2)
                    for s in range(2):
                        if i:
                            ac.wait_ge(s_ucv, 2 * (i - 1) + s + 1)
                        b_ = 4 * (i % 2) + s
                        AC(up2[:, s, 1:1 + P], ps[:, b_, 0:P], ACT.Copy)
                        AC(up2[:, s, 2 + P:2 + TOK], ps[:, b_, P:TOK], ACT.Copy).then_inc(s_uc, 1)
                elif b:
                    i = b // 2 - 1
                    for s in range(2):
                        ac.wait_ge(s_ucv, 2 * i + s + 1)
                        if i:
                            ac.wait_ge(s_uact, 2 * (i - 1) + s + 1)
                        AC(sg2[:, s, :], cv2[:, s, :], ACT.Silu).then_inc(s_usg, 1)
            for n in range(8):
                ac.wait_ge(s_gb2p, n + 1)
                AC(gb2[:, n // 4, 512 * (n % 4):512 * (n % 4) + 512], ps[:, 6 + n % 2, :], ACT.Copy).then_inc(s_gb2c, 1)
            ac.wait_ge(s_uact, FT)
            for i in range(2 * FT):
                hi(P_DOWN + i)
                if i >= 3:
                    ac.wait_ge(s_kd, i - 2)
                AC(ah[i % 3], act[:, i % FT, :], ACT.Copy).then_inc(s_ah, 1)
            for t in range(3):
                ac.wait_ge(s_dc, 6 + 2 * t + 2)
                AC(junk2, x3[:, t, :], ACT.Square, accum_out=stat[:, 32 + t:33 + t]).then_inc(s_fss, 1)
                ac.wait_ge(s_fss, t + 1)
                root(stat[:, 36 + t:37 + t])

        @block.vector
        def _(dv):
            V = nc.vector
            cnt = [0]

            def link(ins):
                cnt[0] += 1
                ins.then_inc(s_d, 1)
                dv.wait_ge(s_d, cnt[0])

            roots = [0]

            def ask_root(ins):
                roots[0] += 1
                ins.then_inc(s_var, 1)

            def take_root(ap):
                dv.wait_ge(s_root, roots[0])
                link(V.reciprocal(ap, ap))

            def inv_root(ins, ap):
                ask_root(ins)
                take_root(ap)

            def mark(ins):
                cnt[0] += 1
                ins.then_inc(s_d, 1)
                return cnt[0]

            def lo(n):
                dv.wait_ge(s_hi, n + 1)
                w = width(n)
                V.tensor_tensor(wl[n % SPLITS][:, 0:w], arrived(n), wh[n % SPLITS][:, 0:w].bitcast(F32),
                                ALU.subtract).then_inc(s_lo, 1)

            dv.wait_ge(s_csig, 1)
            V.tensor_tensor(cT, csig, ps[:, 0, 0:2 * KT], ALU.mult).then_inc(s_ct, 1)
            for g, rows in enumerate((128, 124, 100, 88)):
                dv.wait_ge(s_vt, g + 2)
                V.tensor_copy(vcol[:, g, 0:rows], ps[:, 1 + g, 0:rows]).then_inc(s_vc, 1)
            dv.wait_ge(s_ssq, 3)
            inv_root(V.tensor_scalar(stat[:, 4:7], stat[:, 0:3], 1.0 / D, 1e-6, ALU.mult, ALU.add), stat[:, 4:7])
            for t in range(3):
                V.tensor_scalar(xn[:, t, :], x[:, t, :], stat[:, 4 + t:5 + t], None, ALU.mult).then_inc(s_xn, 1)
            dv.wait_ge(s_c4, 1)
            c4v = c4_t[:, :].rearrange("p (k r g) -> p r k g", r=2, g=2)
            V.tensor_tensor(c4v[:, 1], cT.rearrange("p (g k) -> p k g", g=2), c4v[:, 0].bitcast(F32), ALU.subtract).then_inc(s_c4, 1)
            dv.wait_ge(s_vc, 4)

            def mod_col(i):
                dv.wait_ge(s_mcT, i + 1)
                bank, c0 = (2 + i % 2, 0) if i < N_EARLY else (i % 2, BLK)
                V.tensor_tensor(modcol[:, 2 * i:2 * i + 2, :], ps[:, bank, c0:c0 + 4].rearrange("p (t g) -> p t g", g=2),
                                vcol[:, 0, 32 + 2 * i:34 + 2 * i].unsqueeze(2).broadcast_to([P, 2, 2]), ALU.add).then_inc(s_mcol, 1)

            for n in range(P_MIX + SPLITS):
                lo(n)
                if n - SPLITS - 3 in MOD_LAST:
                    mod_col(MOD_LAST[n - SPLITS - 3])
            mod_col(N_EARLY - 1)
            dv.wait_ge(s_mcol, N_EARLY)
            n1 = vcol[:, 0, 0:KT].unsqueeze(2).broadcast_to([P, KT, 2])
            n2 = vcol[:, 0, KT:2 * KT].unsqueeze(2).broadcast_to([P, KT, 2])
            link(V.tensor_scalar(scol, modcol[:, KT:2 * KT, :], 1.0, None, ALU.add))
            link(V.tensor_tensor(scol, scol, n1, ALU.mult))
            dv.wait_ge(s_xc, 12)
            for k in range(KT):
                for g, r in ((0, slice(0, P)), (1, slice(P, TOK))):
                    last = V.tensor_scalar(xT[:, k, r], xT[:, k, r], scol[:, k, g:g + 1], modcol[:, k, g:g + 1], ALU.mult, ALU.add)
                if k % 4 == 3:
                    last.then_inc(s_hm, 1)
            for q in range(4):
                dv.wait_ge(s_hh, q + 1)
                last = V.tensor_tensor(hl[:, 4 * q:4 * q + 4, :], xT[:, 4 * q:4 * q + 4, :],
                                       hh[:, 4 * q:4 * q + 4, :].bitcast(F32), ALU.subtract)
            last.then_inc(s_h, 1)
            dv.wait_ge(s_h, 1)
            for c_, n in ((0, PADC), (PADC + P, PADC), (PADC * 2 + TOK, PADC)):
                link(V.memset(upad[:, :, c_:c_ + n], 0.0))
            def take_items(b):
                for m, (n, kind, what, j, s, eng) in enumerate(ITEMS):
                    if eng != "dve" or n != b:
                        continue
                    dv.wait_ge(s_blk, IN_END[n])
                    if what == "k":
                        V.tensor_copy(qkT[:, 6 + j + s, :], ps[:, bank_of(m), 0:TOK]).then_inc(s_edve, 1)
                    else:
                        dv.wait_ge(s_eact, evacs("act", m))
                        V.tensor_tensor(upad[:, j + s, PADC:PADC + P], ps[:, bank_of(m), 0:P], sgt[:, s, 0:P], ALU.mult)
                        V.tensor_tensor(upad[:, j + s, 2 * PADC + P:2 * PADC + TOK], ps[:, bank_of(m), P:TOK], sgt[:, s, P:TOK],
                                        ALU.mult).then_inc(s_edve, 1)

            at = [0] * BT

            def conv(n):
                j, t = n // BT, n % BT
                w = vcol[:, 1, n:n + 1]
                if j == 0:
                    at[t] = mark(V.tensor_scalar(cbuf[:, t, :], upad[:, t, 0:CW], w, vcol[:, 2, 88 + t:89 + t], ALU.mult, ALU.add))
                else:
                    dv.wait_ge(s_d, at[t])
                    at[t] = mark(V.scalar_tensor_tensor(cbuf[:, t, :], upad[:, t, j:j + CW], w, cbuf[:, t, :], ALU.mult, ALU.add))

            glu_end = IN_END[max(it[0] for it in ITEMS if it[2] == "glu_a")] + SPLITS
            taps = CONV_K * BT
            for n in range(P_MIX + SPLITS, P_OUT + SPLITS + 3):
                if n < P_OUT:
                    lo(n)
                if n - SPLITS - 3 in MOD_LAST and MOD_LAST[n - SPLITS - 3] >= N_EARLY:
                    mod_col(MOD_LAST[n - SPLITS - 3])
                if n - SPLITS in IN_LAST:
                    take_items(IN_LAST[n - SPLITS])
                if n == glu_end:
                    dv.wait_ge(s_edve, evacs("dve", len(ITEMS)))
                if glu_end <= n < P_OUT:
                    span = P_OUT - glu_end
                    for tap in range((n - glu_end) * taps // span, (n - glu_end + 1) * taps // span):
                        conv(tap)
            dv.wait_ge(s_mcol, N_MOD)
            link(V.tensor_scalar(scol, modcol[:, 4 * KT:5 * KT, :], 1.0, None, ALU.add))
            link(V.tensor_tensor(scol, scol, n2, ALU.mult))
            dv.wait_ge(s_d, cnt[0])
            dv.sem_inc(s_cbuf, 1)
            dv.wait_ge(s_cmean, 1)
            for t in range(BT):
                last = V.tensor_tensor(cbuf[:, t, :], cbuf[:, t, :], ps[:, 0, 0:CW], ALU.subtract)
            last.then_inc(s_ccen, 1)
            dv.wait_ge(s_cvar, 1)
            inv_root(V.tensor_scalar(crstd, ps[:, 1, 0:CW], 1e-5, None, ALU.add), crstd)
            for t in range(BT):
                last = V.tensor_tensor(cbuf[:, t, :], cbuf[:, t, :], crstd, ALU.mult)
            last.then_inc(s_cn, 1)

            for t in range(BT):
                for i, (a0, b0, n) in enumerate(((0, 0, P), (P + PADC, P, 2 * P))):
                    dv.wait_ge(s_cy, 2 * t + i + 1)
                    V.tensor_tensor(yl[:, 6 + t, b0:b0 + n], cbuf[:, t, a0:a0 + n], yh[:, 6 + t, b0:b0 + n].bitcast(F32),
                                    ALU.subtract).then_inc(s_cyh, 1)


            def softmax(u):
                t, h = ATT[u]
                n = P if t == 0 else TOK
                dv.wait_ge(s_sc, u + 1)
                if u >= 3:
                    dv.wait_ge(s_pt, u - 2)
                if t == 0:
                    link(V.tensor_scalar(ss[:, u % 3, 0:P], ps[:, u % 2, 0:P], SCALE, None, ALU.mult))
                else:
                    b_ = Bm[:, h, 4 - 2 * t:8 - 2 * t, :].rearrange("p r c -> p (r c)")
                    V.scalar_tensor_tensor(ss[:, u % 3, 0:2 * P], ps[:, u % 2, 0:2 * P], SCALE, b_, ALU.mult, ALU.add)
                    link(V.tensor_scalar(ss[:, u % 3, 2 * P:TOK], ps[:, u % 2, 2 * P:TOK], SCALE, None, ALU.mult))
                V.tensor_reduce(stat[:, 8 + u % 4:9 + u % 4], ss[:, u % 3, 0:n], AX.X, ALU.max, negate=True).then_inc(s_sm, 1)

            def norm(u):
                t, h = ATT[u]
                n = P if t == 0 else TOK
                dv.wait_ge(s_ex, u + 1)
                link(V.reciprocal(stat[:, 20 + u % 4:21 + u % 4], stat[:, 16 + u % 4:17 + u % 4]))
                V.tensor_scalar(ss[:, u % 3, 0:n], ss[:, u % 3, 0:n], stat[:, 20 + u % 4:21 + u % 4], None, ALU.mult).then_inc(s_nr, 1)

            def result(u):
                t, h = ATT[u]
                dv.wait_ge(s_pvh, u // 2 + 1)
                V.tensor_tensor(yl[:, h // 2, toks(t)], ps[:, 4 + (u // 2) % 2, 0:P], yh[:, h // 2, toks(t)].bitcast(F32),
                                ALU.subtract).then_inc(s_pvc, 1)

            for u in range(len(ATT) + 4):
                if u == HA:
                    dv.wait_ge(s_Bm, 16 * 2 * HA)
                    V.tensor_tensor(Bm.rearrange("p h r c -> p (h r) c"), Bm.rearrange("p h r c -> p (h r) c"),
                                    consts[:, C_COL:C_COL + GRID].unsqueeze(1).broadcast_to([P, 6 * HA, GRID]), ALU.add).then_inc(s_Bmask, 1)
                    dv.wait_ge(s_Bmask, 1)
                if u < len(ATT):
                    softmax(u)
                if 0 < u <= len(ATT):
                    norm(u - 1)
                if u >= 4 and (u - 4) % 2 == 1:
                    result(u - 4)
            dv.wait_ge(s_pvc, len(ATT) // 2)

            def heads(ap):
                return ap.rearrange("p (h c) -> p h c", h=HH)

            def mats(b):
                return ps[:, b, :].rearrange("p (j c) -> p j c", c=P)

            same2 = consts[:, C_SAME2:C_SAME2 + P].unsqueeze(1).broadcast_to([P, HH, P])
            idb = ident.unsqueeze(1).broadcast_to([P, HH, P])

            def rwkv_step(u, step, l, v):
                z, gr, t, d, s0, first = unit(v)
                spare = 4 * (u % 2) + 3

                def part(t, q):
                    return rkv[:, t, q + HW * gr:q + HW * gr + HW]

                if step == "X":
                    c0 = C_XM + (LEVELS * d + l) * P
                    dv.wait_ge(s_rX, LEVELS * v + l + 1)
                    V.tensor_tensor(Xm[z], mats(4 * z), consts[:, c0:c0 + P].unsqueeze(1).broadcast_to([P, HH, P]), ALU.mult).then_inc(s_rXm, 1)
                elif step == "T":
                    dv.wait_ge(s_rTp, LEVELS * v + l + 1)
                    last = V.tensor_tensor(TTm[z], TTm[z], mats(4 * z + 2), ALU.add)
                    if l < LEVELS - 1:
                        last = V.tensor_tensor(Tm[z], Tm[z], mats(4 * z + 1), ALU.add)
                    last.then_inc(s_rTu, 1)
                    dv.wait_ge(s_rTu, LEVELS * v + l + 1)
                elif step == "QM":
                    dv.wait_ge(s_rQM, v + 1)
                    V.tensor_tensor(QT[z], mats(4 * z)[:, 0:CT], zrT[z][:, :, 1, :], ALU.add)
                    for p in range(2):
                        V.tensor_tensor(MT[z][:, p], ps[:, 4 * z + 1 + p, 0:P].rearrange("p (i c) -> p i c", i=CT), dP[z][:, p], ALU.add)
                        last = V.tensor_copy(Sh[z][:, p], ps[:, 4 * z + 1 + p, P:2 * P].rearrange("p (i c) -> p i c", i=CT))
                    last.then_inc(s_rQMc, 1)
                    if v % NG == 0:
                        for dd in range(2):
                            last = V.memset(S[:, 5 * dd, :, :], 0.0)
                        last.then_inc(s_S0, 1)
                elif step == "S":
                    c = l if d == 0 else 1 - l
                    dv.wait_ge(s_rQMc, v + 1)
                    dv.wait_ge(s_rSp, 2 * v + l + 1)
                    for hp in range(2):
                        last = V.tensor_tensor(S[half(hp), 5 * d + s0 + l + 1], Sh[z][half(hp), c],
                                               ps[half(hp), 4 * z + 3 * (1 - hp), 0:P].rearrange("p (i c) -> p i c", i=CT), ALU.add)
                    last.then_inc(s_rS, 1)
                elif step == "O":
                    dv.wait_ge(s_rO, v + 1)
                    for hp in range(2):
                        dst = Oacc[t].rearrange("p (i a c) -> p i a c", i=CT, a=2)[:, :, hp, :]
                        src = ps[:, 4 * z + 1 + hp, 0:P].rearrange("p (i c) -> p i c", i=CT)
                        if first:
                            last = V.tensor_copy(dst, src)
                        else:
                            last = V.tensor_tensor(dst, dst, src, ALU.add)
                    last.then_inc(s_rdone, 1)
                    dv.wait_ge(s_rdone, v + 1)
                elif step == "lora":
                    dv.wait_ge(s_par, 16 * 9 * (gr + 1))
                    dv.wait_ge(s_rlora, v + 1)
                    V.tensor_tensor(tW[z], ps[:, spare, 0:HW], par[:, d, :], ALU.add)
                    V.tensor_tensor(tA[z], ps[:, spare, HW:2 * HW], par[:, 2 + d, :], ALU.add).then_inc(s_rpre, 1)
                elif step == "kk":
                    for t_ in range(3):
                        last = V.tensor_tensor(kkn[t_], part(t_, 768), par[:, 4, :], ALU.mult)
                    link(last)
                    for t_ in range(3):
                        link(V.tensor_tensor(sq[t_ % 2], kkn[t_], kkn[t_], ALU.mult))
                        last = V.tensor_reduce(kss[:, t_, :], heads(sq[t_ % 2]), AX.X, ALU.add)
                    link(last)
                    inv_root(V.tensor_scalar(kss, kss, 1e-12, None, ALU.add), kss)
                    for t_ in range(3):
                        last = V.tensor_tensor(heads(kkn[t_]), heads(kkn[t_]), kss[:, t_, :].unsqueeze(2).broadcast_to([P, HH, HD]), ALU.mult)
                    link(last)
                elif step == "cum" and l == 0:
                    dv.wait_ge(s_rsig, v + 1)
                    if v >= 2:
                        dv.wait_ge(s_rpl, v - 1)
                    V.tensor_tensor(b1[z], kkn[t], tA[z], ALU.mult)
                    link(V.scalar_tensor_tensor(kd[z], tA[z], 1.0, par[:, 5, :], ALU.subtract, ALU.mult))
                    link(V.scalar_tensor_tensor(kd[z], kd[z], 1.0, part(t, 768), ALU.add, ALU.mult))
                elif step == "cum":
                    dv.wait_ge(s_rexp, v + 1)
                    V.scalar_tensor_tensor(eE[z], kkn[t], -1.0, eE[z], ALU.mult, ALU.mult)
                    V.tensor_tensor(eP[z], part(t, 0), eP[z], ALU.mult)
                    V.tensor_tensor(btil[z], b1[z], eN[z], ALU.mult)
                    V.tensor_tensor(ktil[z], kd[z], eN[z], ALU.mult).then_inc(s_rtil, 1)
                elif step == "tr":
                    dv.wait_ge(s_rexp2, v + 1)
                    for p in range(2):
                        for hp in range(2):
                            src = eT[z][half(p), :].rearrange("p (i a c) -> p i a c", i=CT, a=2)[:, :, hp, :]
                            V.tensor_tensor(dP[z][half(hp), p, :, :], src,
                                            consts[half(p), C_ID + 64 * p:C_ID + 64 * p + 64].unsqueeze(1).broadcast_to([HD, CT, HD]), ALU.mult)
                    link(V.tensor_tensor(sq[0], part(t, 0), kd[z], ALU.mult))
                    link(V.tensor_tensor(sq[0], sq[0], par[:, 6, :], ALU.mult))
                    V.tensor_reduce(bonus[:, v % (2 * NG), :], heads(sq[0]), AX.X, ALU.add).then_inc(s_rbon, 1)
                    dv.wait_ge(s_rbon, v + 1)
                elif step == "A":
                    for h in (2 * l, 2 * l + 1):
                        dv.wait_ge(s_rA, HH * v + h + 1)
                        V.tensor_tensor(Am[z][:, h, :, :].rearrange("p a b -> p (a b)"), ps[:, 4 * z + 1 + h % 2, :],
                                        consts[:, C_M4 + 512 * d:C_M4 + 512 * d + 512], ALU.mult).then_inc(s_rAm, 1)
                elif step == "N":
                    dv.wait_ge(s_rNc, v + 1)
                    link(V.tensor_tensor(Tm[z], Nm[z], same2, ALU.mult))
                    V.tensor_tensor(Tm[z], Tm[z], idb, ALU.add).then_inc(s_rT0, 1)
                    dv.wait_ge(s_rT0, v + 1)
                elif step == "in":
                    dv.wait_ge(s_sT, 2 * gr + 2)
                    for dd in range(2):
                        last = V.tensor_copy(S[:, 5 * dd, :, :], ps[:, spare, P * dd:P * dd + P].rearrange("p (i c) -> p i c", i=CT))
                    last.then_inc(s_S0, 1)
                elif step == "F":
                    w_, t_, pair = FINAL[v % NG]
                    O = Oacc[t_]
                    if l == 0:
                        link(V.tensor_reduce(st6[:, 2, :], heads(O), AX.X, ALU.add))
                        link(V.scalar_tensor_tensor(heads(O), st6[:, 2, :].unsqueeze(2).broadcast_to([P, HH, HD]), -1.0 / HD, heads(O), ALU.mult, ALU.add))
                        link(V.tensor_tensor(sq[1], O, O, ALU.mult))
                        link(V.tensor_reduce(st6[:, 3, :], heads(sq[1]), AX.X, ALU.add))
                        ask_root(V.tensor_scalar(st6[:, 3, :], st6[:, 3, :], 1.0 / HD, 64e-5, ALU.mult, ALU.add))
                        b_ = [bonus[:, (NG * gr + k) % (2 * NG), :] for k in pair]
                        link(V.tensor_tensor(st6[:, 0, :], b_[0], b_[1], ALU.add))
                    elif l == 1:
                        V.tensor_tensor(heads(sq[1]), heads(part(t_, 1536)), st6[:, 0, :].unsqueeze(2).broadcast_to([P, HH, HD]), ALU.mult)
                        take_root(st6[:, 3, :])
                        link(V.tensor_tensor(heads(O), heads(O), st6[:, 3, :].unsqueeze(2).broadcast_to([P, HH, HD]), ALU.mult))
                        dv.wait_ge(s_parf, 16 * 3 * (gr + 1))
                        link(V.tensor_tensor(O, O, par[:, 9, :], ALU.mult))
                        link(V.tensor_tensor(O, O, par[:, 10, :], ALU.add))
                        link(V.tensor_tensor(O, O, sq[1], ALU.add))
                        dv.wait_ge(s_fg, 3 * gr + w_ + 1)
                        V.tensor_tensor(O, O, ps[:, spare, 0:HW], ALU.mult).then_inc(s_fy, 1)
                    else:
                        dv.wait_ge(s_fh, 3 * gr + w_ + 1)
                        ydst = slice(10 + CT * gr, 10 + CT * (gr + 1))
                        V.tensor_tensor(yl[:, ydst, toks(t_)], mats(spare)[:, CT:2 * CT], yh[:, ydst, toks(t_)].bitcast(F32), ALU.subtract).then_inc(s_fc, 1)

            for u in PERIODS:
                for step in steps(u):
                    rwkv_step(u, *step)

            dv.wait_ge(s_fc, 3 * GROUPS)

            def residual(j):
                used(dv, P_OUT + PARTS * (j + 1) - 1)
                for t in range(3):
                    n = 3 * j + t
                    cs = slice(BLK * j, BLK * j + BLK)
                    link(V.tensor_tensor(ytmp[:, t % 2], ps[:, 3 * (j % 2) + t, 0:BLK], gb[:, min(t, 1), cs], ALU.mult))
                    V.tensor_tensor(x2[:, t, cs], x2[:, t, cs], ytmp[:, t % 2], ALU.add).then_inc(s_oc, 1)
                    dv.wait_ge(s_oc, n + 1)

            for j in range(D // BLK):
                for p in range(PARTS):
                    lo(P_OUT + PARTS * j + p)
                if j == 0:
                    dv.wait_ge(s_x2, 48)
                    dv.wait_ge(s_gbc, 8)
                else:
                    residual(j - 1)
            residual(D // BLK - 1)
            dv.wait_ge(s_ssq2, 3)
            inv_root(V.tensor_scalar(stat[:, 28:31], stat[:, 24:27], 1.0 / D, 1e-6, ALU.mult, ALU.add), stat[:, 28:31])
            for t in range(3):
                V.tensor_scalar(xn2[:, t, :], x2[:, t, :], stat[:, 28 + t:29 + t], None, ALU.mult).then_inc(s_xn2, 1)

            def h2_lo(n):
                dv.wait_ge(s_hh2, n + 1)
                at_ = (slice(4 * (n % 4), 4 * (n % 4) + 4), toks(n // 4))
                V.tensor_tensor(hl[:, at_[0], at_[1]], mtmp[:, n % 2], hh[:, at_[0], at_[1]].bitcast(F32), ALU.subtract).then_inc(s_h2, 1)

            for n in range(12):
                t, q = n // 4, n % 4
                g = min(t, 1)
                if n >= 2:
                    h2_lo(n - 2)
                    dv.wait_ge(s_h2, n - 1)
                dv.wait_ge(s_xt2, n + 1)
                for j in range(4):
                    k = 4 * q + j
                    last = V.tensor_scalar(mtmp[:, n % 2, j], ps[:, n % 4, toks(j)], scol[:, k, g:g + 1],
                                           modcol[:, 3 * KT + k, g:g + 1], ALU.mult, ALU.add)
                last.then_inc(s_hm2, 1)
            h2_lo(10)
            h2_lo(11)
            dv.wait_ge(s_h2, 12)
            for c_ in (0, 1 + P, 2 + TOK):
                last = V.memset(up2[:, :, c_:c_ + 1], 0.0)
            last.then_inc(s_pad, 2)
            dv.wait_ge(s_xs, 16)
            W3 = TOK + 1
            for b in range(2 * (DFF // BLK) + 1):
                if b < 2 * (DFF // BLK):
                    for p in range(PARTS):
                        lo(P_UP + PARTS * b + p)
                if b % 2:
                    for s in range(2):
                        f = b - 1 + s
                        dv.wait_ge(s_uc, f + 1)
                        if f >= 2:
                            dv.wait_ge(s_usg, f - 1)
                        link(V.tensor_scalar(cv2[:, s, :], up2[:, s, 0:W3], vcol[:, 2, f:f + 1], vcol[:, 3, 44 + f:45 + f], ALU.mult, ALU.add))
                        link(V.scalar_tensor_tensor(cv2[:, s, :], up2[:, s, 1:1 + W3], vcol[:, 2, 44 + f:45 + f], cv2[:, s, :], ALU.mult, ALU.add))
                        V.scalar_tensor_tensor(cv2[:, s, :], up2[:, s, 2:2 + W3], vcol[:, 3, f:f + 1], cv2[:, s, :], ALU.mult, ALU.add).then_inc(s_ucv, 1)
                elif b:
                    i = b // 2 - 1
                    dv.wait_ge(s_blk, P_UP + PARTS * b)
                    for s in range(2):
                        f = 2 * i + s
                        dv.wait_ge(s_usg, f + 1)
                        b_ = 4 * (i % 2) + 2 + s
                        V.tensor_tensor(act[:, f, 0:P], ps[:, b_, 0:P], sg2[:, s, 0:P], ALU.mult)
                        V.tensor_tensor(act[:, f, P:TOK], ps[:, b_, P:TOK], sg2[:, s, P + 1:TOK + 1], ALU.mult).then_inc(s_uact, 1)

            def residual2(q):
                dv.wait_ge(s_kd, FT * (q + 1))
                tmp2 = ytmp1 if q == 0 else ytmp2
                w = 256 if q == 0 else 512
                for t in range(3):
                    for c in range(2):
                        n = 6 * q + 2 * t + c
                        for e in range(512 // w):
                            cs = slice(DOWN_W * q + 512 * c + w * e, DOWN_W * q + 512 * c + w * (e + 1))
                            link(V.tensor_tensor(tmp2[:, e % 2 if q == 0 else c], ps[:, n % 8, w * e:w * (e + 1)], gb2[:, min(t, 1), cs], ALU.mult))
                            last = V.tensor_tensor(x3[:, t, cs], x3[:, t, cs], tmp2[:, e % 2 if q == 0 else c], ALU.add)
                            if e < 512 // w - 1:
                                link(last)
                        last.then_inc(s_dc, 1)
                        dv.wait_ge(s_dc, n + 1)

            for i in range(2 * FT):
                lo(P_DOWN + i)
                dv.wait_ge(s_ah, i + 1)
                V.tensor_tensor(al[i % 3], act[:, i % FT, :], ah[i % 3].bitcast(F32), ALU.subtract).then_inc(s_al, 1)
                if i == FT + 2:
                    dv.wait_ge(s_x3, 16)
                    dv.wait_ge(s_gb2c, 8)
                    residual2(0)
            residual2(1)
            dv.wait_ge(s_fgl, 16)
            for t in range(3):
                dv.wait_ge(s_fss, t + 1)
                inv_root(V.tensor_scalar(stat[:, 36 + t:37 + t], stat[:, 32 + t:33 + t], 1.0 / D, 1e-6, ALU.mult, ALU.add),
                         stat[:, 36 + t:37 + t])
                V.scalar_tensor_tensor(x3[:, t, :], x3[:, t, :], stat[:, 36 + t:37 + t], fg, ALU.mult, ALU.mult).then_inc(s_yf, 1)


_INS = ['x_prompt', 'x_sample', 'cache_k', 'cache_v', 'state_fwd', 'state_bwd', 'c', 'c_ctx', 'norm1_g', 'norm2_g',
        'w_mod', 'b_mod', 'w_in', 'w_out', 'rpb', 'conv_w', 'conv_b', 'conv_ln_g', 'conv_ln_b', 'rwkv_w0',
        'rwkv_w_lora', 'rwkv_a0', 'rwkv_a_lora', 'rwkv_g_lora', 'rwkv_k_k', 'rwkv_k_a', 'rwkv_r_k', 'rwkv_ln_g',
        'rwkv_ln_b', 'w_up', 'ffn_conv_w', 'ffn_conv_b', 'w_down', 'final_g']
_OUTS = [("y_prompt", (1, 128, 2048)), ("y_sample", (1, 256, 2048)), ("new_cache_k", (1, 1, 128, 12, 64)),
         ("new_cache_v", (1, 1, 128, 12, 64)), ("new_state_fwd", (1, 1, 12, 64, 64)), ("new_state_bwd", (1, 1, 12, 64, 64))]


def _constants():
    import numpy as np
    j, t = np.meshgrid(np.arange(P), np.arange(P), indexing="ij")
    same = (j // CHUNK) == (t // CHUNK)
    cols = [np.eye(P)]
    for before in ((j < t), (j > t)):
        strict = same & before
        incl = same & (before | (j == t))
        cols += [strict, incl, strict, incl]
    cols.append(same)
    for d in range(2):
        for l in range(LEVELS):
            n = 2 << l
            pair = (j // (2 * n)) == (t // (2 * n))
            a, b = (j // n) % 2, (t // n) % 2
            cols.append(pair & ((a == 0) & (b == 1) if d == 0 else (a == 1) & (b == 0)))
    cols.append((j // 2) == (t // 2))
    q = np.arange(P) % GRID
    start = np.clip(q - 8, 0, GRID - 16)
    kc = np.arange(GRID)
    cols.append(np.where((kc >= start[:, None]) & (kc < start[:, None] + 16), 0.0, -1e30))
    cols.append(np.zeros((P, P)))
    cols.append(np.full((P, P), 1.0 / (BT * P)))
    cols.append((np.arange(P)[:, None] % 2 == np.arange(4)) & (np.arange(P)[:, None] < 4))
    return np.concatenate([np.asarray(c, np.float32) for c in cols], axis=1)


def kernel(**inputs):
    import numpy as _np
    import concourse.bacc as _bacc
    from concourse import mybir as _mybir
    from concourse.bass_utils import run_bass_kernel_spmd as _run

    nc = _bacc.Bacc("TRN2", target_bir_lowering=False, num_devices=1)
    arrays, args, outs = {}, {}, {}
    for name in _INS + ["consts"]:
        a = _constants() if name == "consts" else _np.ascontiguousarray(inputs[name])
        arrays[f"in_{name}_dram"] = a
        args[name] = nc.dram_tensor(f"in_{name}_dram", a.shape, _mybir.dt.from_np(a.dtype), kind="ExternalInput").ap()
    for name, shape in _OUTS:
        outs[name] = nc.dram_tensor(f"out_{name}_dram", shape, F32, kind="ExternalOutput").ap()
    build(nc, args, outs)
    r = _run(nc, [arrays], core_ids=[0])
    return tuple(r.results[0][f"out_{name}_dram"] for name, _ in _OUTS)
```
